# Optimizing a Trainium2 kernel written in Bass

```python
import jax, jax.numpy as jnp
from jax import lax
import numpy as np

D_MODEL = 1024
BATCH = 1
SEQ = 512
DEPTH = 2

CHUNK = 64
HEAD_DIM = 64
ATT_HEADS = 6
ATT_WIDTH = ATT_HEADS * HEAD_DIM
ATT_LEFT_CHUNKS = 8
ATT_BAND = (ATT_LEFT_CHUNKS + 1) * CHUNK
REL_CLIP = 128
CONV_WIDTH = D_MODEL // 4
CONV_KERNEL = 31
RET_HEADS = 6
RET_WIDTH = RET_HEADS * HEAD_DIM
D_MIX = ATT_WIDTH + CONV_WIDTH + RET_WIDTH
D_IN = 3 * ATT_WIDTH + 2 * CONV_WIDTH + 4 * RET_WIDTH
SPLITS = (ATT_WIDTH, 2 * ATT_WIDTH, 3 * ATT_WIDTH,
          3 * ATT_WIDTH + 2 * CONV_WIDTH,
          3 * ATT_WIDTH + 2 * CONV_WIDTH + RET_WIDTH,
          3 * ATT_WIDTH + 2 * CONV_WIDTH + 2 * RET_WIDTH,
          3 * ATT_WIDTH + 2 * CONV_WIDTH + 3 * RET_WIDTH)
D_FF = 4 * D_MODEL
ROPE_BASE = 10000.0
EPS = 1e-6
NEG_INF = -1e30


def rms_norm(x, g):
    xf = x.astype(jnp.float32)
    y = xf * lax.rsqrt(jnp.mean(xf * xf, axis=-1, keepdims=True) + EPS)
    return (y * g.astype(jnp.float32)).astype(x.dtype)

def layer_norm(x):
    xf = x.astype(jnp.float32)
    mu = jnp.mean(xf, axis=-1, keepdims=True)
    var = jnp.mean(jnp.square(xf - mu), axis=-1, keepdims=True)
    return (xf - mu) * lax.rsqrt(var + EPS)

def chunk_attention(q, k, v, rel_bias):
    b, s, _ = q.shape
    nc = s // CHUNK
    shp = (b, nc, CHUNK, ATT_HEADS, HEAD_DIM)
    q = q.reshape(shp) * (HEAD_DIM ** -0.5)
    k = k.reshape(shp)
    v = v.reshape(shp)
    pad = ((0, 0), (ATT_LEFT_CHUNKS, 0), (0, 0), (0, 0), (0, 0))
    kp, vp = jnp.pad(k, pad), jnp.pad(v, pad)
    band_idx = jnp.arange(nc)[:, None] + jnp.arange(ATT_LEFT_CHUNKS + 1)[None, :]
    kb = kp[:, band_idx].reshape(b, nc, ATT_BAND, ATT_HEADS, HEAD_DIM)
    vb = vp[:, band_idx].reshape(b, nc, ATT_BAND, ATT_HEADS, HEAD_DIM)
    scores = jnp.einsum('bnqhd,bnkhd->bnhqk', q, kb).astype(jnp.float32)
    qpos = jnp.arange(CHUNK)
    kpos = jnp.arange(ATT_BAND)
    rel = qpos[:, None] + ATT_LEFT_CHUNKS * CHUNK - kpos[None, :]
    rel_idx = jnp.clip(rel, -REL_CLIP, REL_CLIP) + REL_CLIP
    bias = rel_bias[:, rel_idx].astype(jnp.float32)
    key_chunk = jnp.arange(nc)[:, None] + (kpos // CHUNK)[None, :] - ATT_LEFT_CHUNKS
    valid = key_chunk >= 0
    scores = jnp.where(valid[None, :, None, None, :], scores + bias[None, None], NEG_INF)
    p = jax.nn.softmax(scores, axis=-1).astype(v.dtype)
    o = jnp.einsum('bnhqk,bnkhd->bnqhd', p, vb)
    return o.reshape(b, s, ATT_WIDTH)

def conv_module(u, conv_w, conv_b, ln_g, ln_b):
    a, gate = jnp.split(u, 2, axis=-1)
    y = a * jax.nn.sigmoid(gate)
    y = jnp.pad(y, ((0, 0), (CONV_KERNEL - 1, 0), (0, 0)))
    y = lax.conv_general_dilated(y, conv_w[:, None, :], (1,), 'VALID',
                                 dimension_numbers=('NWC', 'WIO', 'NWC'),
                                 feature_group_count=CONV_WIDTH) + conv_b
    y = layer_norm(y) * ln_g.astype(jnp.float32) + ln_b.astype(jnp.float32)
    return jax.nn.silu(y).astype(u.dtype)

def rotary(x, pos):
    half = HEAD_DIM // 2
    inv = 1.0 / (ROPE_BASE ** jnp.linspace(0.0, 1.0, half, dtype=jnp.float32))
    ang = pos[:, None] * inv[None, :]
    cos = jnp.cos(ang)[None, :, None, :]
    sin = jnp.sin(ang)[None, :, None, :]
    x1 = x[..., :half].astype(jnp.float32)
    x2 = x[..., half:].astype(jnp.float32)
    out = jnp.concatenate([x1 * cos - x2 * sin, x2 * cos + x1 * sin], axis=-1)
    return out.astype(x.dtype)

def retention(q, k, v, g):
    b, s, _ = q.shape
    nc = s // CHUNK
    dt = q.dtype
    pos = jnp.arange(s, dtype=jnp.float32)
    q = rotary(q.reshape(b, s, RET_HEADS, HEAD_DIM), pos)
    k = rotary(k.reshape(b, s, RET_HEADS, HEAD_DIM), pos) * (HEAD_DIM ** -0.5)
    shp = (b, nc, CHUNK, RET_HEADS, HEAD_DIM)
    qc, kc, vc = q.reshape(shp), k.reshape(shp), v.reshape(shp)
    log_g = jnp.log1p(-(2.0 ** (-5.0 - jnp.arange(RET_HEADS, dtype=jnp.float32))))
    idx = jnp.arange(CHUNK, dtype=jnp.float32)
    diff = idx[:, None] - idx[None, :]
    intra = jnp.where(diff >= 0, jnp.exp(jnp.maximum(diff, 0.0) * log_g[:, None, None]), 0.0)
    xi = jnp.exp((idx + 1.0)[None, :] * log_g[:, None]).astype(dt)
    zeta = jnp.exp((CHUNK - 1.0 - idx)[None, :] * log_g[:, None]).astype(dt)
    gamma_c = jnp.exp(CHUNK * log_g).astype(dt)
    sc = jnp.einsum('bnihd,bnjhd->bnhij', qc, kc) * intra.astype(dt)
    y_intra = jnp.einsum('bnhij,bnjhe->bnihe', sc, vc)
    kv = jnp.einsum('bnjhd,hj,bnjhe->nbhde', kc, zeta, vc)

    def step(state, kv_n):
        return state * gamma_c[None, :, None, None] + kv_n, state

    _, state_prev = lax.scan(step, jnp.zeros_like(kv[0]), kv)
    y_cross = jnp.einsum('bnihd,hi,nbhde->bnihe', qc, xi, state_prev)
    y = (y_intra + y_cross).reshape(b, s, RET_HEADS, HEAD_DIM)
    y = layer_norm(y).reshape(b, s, RET_WIDTH)
    return (jax.nn.silu(g.astype(jnp.float32)) * y).astype(dt)

def hybrid_layer(x, g_mix_pre, g_mix_post, g_mlp_pre, g_mlp_post, w_in, rel_bias,
                 conv_w, conv_b, conv_ln_g, conv_ln_b, w_out, w_up, w_down):
    h = rms_norm(x, g_mix_pre)
    u = h @ w_in
    aq, ak, av, cu, rq, rk, rv, rg = jnp.split(u, SPLITS, axis=-1)
    y_att = chunk_attention(aq, ak, av, rel_bias)
    y_conv = conv_module(cu, conv_w, conv_b, conv_ln_g, conv_ln_b)
    y_ret = retention(rq, rk, rv, rg)
    mix = jnp.concatenate([y_att, y_conv, y_ret], axis=-1) @ w_out
    x = x + rms_norm(mix, g_mix_post)
    h = rms_norm(x, g_mlp_pre)
    f = jnp.square(jax.nn.relu(h @ w_up)) @ w_down
    return x + rms_norm(f, g_mlp_post)

def first_inputs(seed: int = 0) -> dict:
    key = jax.random.key(seed)
    ks = jax.random.split(key, 16)
    f32 = jnp.float32

    def nrm(k, shape, scale):
        return jax.random.normal(k, shape, f32) * scale

    def gain(k, shape):
        return 1.0 + nrm(k, shape, 0.02)

    return {
        "x": nrm(ks[0], (BATCH, SEQ, D_MODEL), 1.0),
        "norm_mix_pre": gain(ks[1], (DEPTH, D_MODEL)),
        "norm_mix_post": gain(ks[2], (DEPTH, D_MODEL)),
        "norm_mlp_pre": gain(ks[3], (DEPTH, D_MODEL)),
        "norm_mlp_post": gain(ks[4], (DEPTH, D_MODEL)),
        "w_in": nrm(ks[5], (DEPTH, D_MODEL, D_IN), D_MODEL ** -0.5),
        "attn_rel_bias": nrm(ks[6], (DEPTH, ATT_HEADS, 2 * REL_CLIP + 1), 0.5),
        "conv_w": nrm(ks[7], (DEPTH, CONV_KERNEL, CONV_WIDTH), CONV_KERNEL ** -0.5),
        "conv_b": nrm(ks[8], (DEPTH, CONV_WIDTH), 0.02),
        "conv_ln_g": gain(ks[9], (DEPTH, CONV_WIDTH)),
        "conv_ln_b": nrm(ks[10], (DEPTH, CONV_WIDTH), 0.02),
        "w_out": nrm(ks[11], (DEPTH, D_MIX, D_MODEL), D_MIX ** -0.5),
        "w_up": nrm(ks[12], (DEPTH, D_MODEL, D_FF), D_MODEL ** -0.5),
        "w_down": nrm(ks[13], (DEPTH, D_FF, D_MODEL), D_FF ** -0.5),
    }

def first_block(x, norm_mix_pre, norm_mix_post, norm_mlp_pre, norm_mlp_post, w_in,
              attn_rel_bias, conv_w, conv_b, conv_ln_g, conv_ln_b, w_out, w_up, w_down):
    for l in range(DEPTH):
        x = hybrid_layer(x, norm_mix_pre[l], norm_mix_post[l], norm_mlp_pre[l], norm_mlp_post[l],
                         w_in[l], attn_rel_bias[l], conv_w[l], conv_b[l], conv_ln_g[l],
                         conv_ln_b[l], w_out[l], w_up[l], w_down[l])
    return x


DEPTH_2 = 1

ATTN_PATTERNS = ((128, 1), (512, 4), (2048, 16))
N_PATTERNS = 3
HEADS_PER_PATTERN = 4
N_ATTN_HEADS = N_PATTERNS * HEADS_PER_PATTERN
ATTN_WIDTH = N_ATTN_HEADS * HEAD_DIM
ATTN_OUT_WIDTH = HEADS_PER_PATTERN * HEAD_DIM
N_KEYS = ATTN_PATTERNS[0][0] // ATTN_PATTERNS[0][1] + 1
Q_BLOCK = 128
REL_BUCKETS = 32
REL_MAX_DIST = 2048
SSM_GROUP = 16
SSM_STATE = 64
SSM_WIDTH = 512
SSM_GROUPS = SSM_WIDTH // SSM_GROUP
DT_MIN = 1e-3
DT_MAX = 1e-1
MEM_LEN = 256
XATTN_HEADS = 4
XATTN_HEAD_DIM = 128
XATTN_WIDTH = XATTN_HEADS * XATTN_HEAD_DIM
N_BRANCHES = 3
IN_WIDTH = SSM_WIDTH + 3 * ATTN_WIDTH + XATTN_WIDTH + N_BRANCHES * D_MODEL
D_FF_2 = 2816


def rmsnorm(x, g):
    xf = x.astype(jnp.float32)
    y = xf * lax.rsqrt(jnp.mean(xf * xf, axis=-1, keepdims=True) + EPS)
    return (y * g.astype(jnp.float32)).astype(x.dtype)

def swiglu_ffn(x, w_in, w_down):
    a, b = jnp.split(x @ w_in, 2, axis=-1)
    return (jax.nn.silu(a) * b) @ w_down

def t5_causal_buckets(dist):
    dist = np.asarray(dist, np.int32)
    max_exact = REL_BUCKETS // 2
    safe = np.maximum(dist, 1).astype(np.float32)
    large = max_exact + (np.log(safe / max_exact) / np.log(REL_MAX_DIST / max_exact)
                         * (REL_BUCKETS - max_exact)).astype(np.int32)
    large = np.minimum(large, REL_BUCKETS - 1)
    return np.where(dist < max_exact, dist, large).astype(np.int32)

def pattern_offsets():
    return np.stack([np.arange(N_KEYS, dtype=np.int32) * d for (_, d) in ATTN_PATTERNS])

def s5_scan(u, a_re, a_im, log_dt, b_re, b_im, c_re, c_im, d_skip):
    bsz, seqlen, _ = u.shape
    f32 = jnp.float32
    uf = u.astype(f32).reshape(bsz, seqlen, SSM_GROUPS, SSM_GROUP)
    a_re = a_re.astype(f32); a_im = a_im.astype(f32)
    dt = jnp.exp(log_dt.astype(f32))[:, None]
    mag = jnp.exp(a_re * dt)
    ang = a_im * dt
    abar_re = mag * jnp.cos(ang)
    abar_im = mag * jnp.sin(ang)
    nr = abar_re - 1.0
    ni = abar_im
    den = a_re * a_re + a_im * a_im
    coef_re = (nr * a_re + ni * a_im) / den
    coef_im = (ni * a_re - nr * a_im) / den
    b_re = b_re.astype(f32); b_im = b_im.astype(f32)
    bbar_re = coef_re[..., None] * b_re - coef_im[..., None] * b_im
    bbar_im = coef_re[..., None] * b_im + coef_im[..., None] * b_re
    bu_re = jnp.einsum('blgh,gph->blgp', uf, bbar_re)
    bu_im = jnp.einsum('blgh,gph->blgp', uf, bbar_im)
    a_seq_re = jnp.broadcast_to(abar_re[None, None], (1, seqlen, SSM_GROUPS, SSM_STATE))
    a_seq_im = jnp.broadcast_to(abar_im[None, None], (1, seqlen, SSM_GROUPS, SSM_STATE))

    def combine(e1, e2):
        a1r, a1i, b1r, b1i = e1
        a2r, a2i, b2r, b2i = e2
        return (a2r * a1r - a2i * a1i,
                a2r * a1i + a2i * a1r,
                a2r * b1r - a2i * b1i + b2r,
                a2r * b1i + a2i * b1r + b2i)

    _, _, x_re, x_im = lax.associative_scan(combine, (a_seq_re, a_seq_im, bu_re, bu_im), axis=1)
    y = (jnp.einsum('blgp,ghp->blgh', x_re, c_re.astype(f32))
         - jnp.einsum('blgp,ghp->blgh', x_im, c_im.astype(f32))
         + uf * d_skip.astype(f32))
    return y.reshape(bsz, seqlen, SSM_WIDTH).astype(u.dtype)

def dilated_mixture_attention(q, k, v, rel_table):
    bsz, seqlen = q.shape[0], q.shape[1]
    f32 = jnp.float32
    offsets = pattern_offsets()
    buckets = t5_causal_buckets(offsets)
    table = rel_table.astype(f32).reshape(REL_BUCKETS, N_PATTERNS, HEADS_PER_PATTERN)
    grp = np.arange(N_PATTERNS)[:, None]
    bias = jnp.transpose(table[buckets, grp], (0, 2, 1))
    grp3 = np.arange(N_PATTERNS)[:, None, None]
    scale = HEAD_DIM ** -0.5

    def block(start):
        qb = lax.dynamic_slice_in_dim(q, start, Q_BLOCK, axis=1).astype(f32)
        pos = start + jnp.arange(Q_BLOCK, dtype=jnp.int32)
        idx = pos[None, :, None] - offsets[:, None, :]
        valid = idx >= 0
        idx = jnp.maximum(idx, 0)
        kb = k[:, idx, grp3].astype(f32)
        vb = v[:, idx, grp3].astype(f32)
        logits = jnp.einsum('bqghd,bgqkhd->bghqk', qb, kb) * scale + bias[None, :, :, None, :]
        logits = jnp.where(valid[None, :, None], logits, -jnp.inf)
        lse = jax.nn.logsumexp(logits, axis=-1)
        probs = jnp.exp(logits - lse[..., None])
        out = jnp.einsum('bghqk,bgqkhd->bqghd', probs, vb)
        mix = jax.nn.softmax(lse, axis=1)
        return jnp.einsum('bghq,bqghd->bqhd', mix, out).astype(q.dtype)

    starts = jnp.arange(seqlen // Q_BLOCK, dtype=jnp.int32) * Q_BLOCK
    out = lax.map(block, starts)
    return out.transpose(1, 0, 2, 3, 4).reshape(bsz, seqlen, ATTN_OUT_WIDTH)

def memory_cross_attention(xq, mem_n, w_kv):
    bsz, seqlen, _ = xq.shape
    f32 = jnp.float32
    mk, mv = jnp.split(mem_n @ w_kv, 2, axis=-1)
    mk = mk.reshape(bsz, -1, XATTN_HEADS, XATTN_HEAD_DIM).astype(f32)
    mv = mv.reshape(bsz, -1, XATTN_HEADS, XATTN_HEAD_DIM).astype(f32)
    qh = xq.reshape(bsz, seqlen, XATTN_HEADS, XATTN_HEAD_DIM).astype(f32)
    logits = jnp.einsum('bqhd,bkhd->bhqk', qh, mk) * (XATTN_HEAD_DIM ** -0.5)
    probs = jax.nn.softmax(logits, axis=-1)
    out = jnp.einsum('bhqk,bkhd->bqhd', probs, mv)
    return out.reshape(bsz, seqlen, XATTN_WIDTH).astype(xq.dtype)

def hybrid_layer_2(x, mem, rel_table, ffn1_norm, ffn1_w_in, ffn1_w_down, mix_norm, w_in,
                 ssm_a_re, ssm_a_im, ssm_log_dt, ssm_b_re, ssm_b_im, ssm_c_re, ssm_c_im, ssm_d, ssm_w_glu,
                 attn_w_up, mem_norm, xattn_w_kv, xattn_w_up, w_out, ffn2_norm, ffn2_w_in, ffn2_w_down):
    bsz, seqlen, _ = x.shape
    x = x + 0.5 * swiglu_ffn(rmsnorm(x, ffn1_norm), ffn1_w_in, ffn1_w_down)
    u = rmsnorm(x, mix_norm)
    proj = u @ w_in
    cuts = np.cumsum([SSM_WIDTH, ATTN_WIDTH, ATTN_WIDTH, ATTN_WIDTH, XATTN_WIDTH, D_MODEL, D_MODEL]).tolist()
    u_ssm, q, k, v, xq, g_ssm, g_attn, g_mem = jnp.split(proj, cuts, axis=-1)
    y_ssm = jax.nn.gelu(s5_scan(u_ssm, ssm_a_re, ssm_a_im, ssm_log_dt, ssm_b_re, ssm_b_im,
                                ssm_c_re, ssm_c_im, ssm_d))
    glu_a, glu_b = jnp.split(y_ssm @ ssm_w_glu, 2, axis=-1)
    br_ssm = glu_a * jax.nn.sigmoid(glu_b)
    hshape = (bsz, seqlen, N_PATTERNS, HEADS_PER_PATTERN, HEAD_DIM)
    br_attn = dilated_mixture_attention(q.reshape(hshape), k.reshape(hshape), v.reshape(hshape),
                                        rel_table) @ attn_w_up
    br_mem = memory_cross_attention(xq, rmsnorm(mem, mem_norm), xattn_w_kv) @ xattn_w_up
    merged = (jax.nn.sigmoid(g_ssm) * br_ssm + jax.nn.sigmoid(g_attn) * br_attn
              + jax.nn.sigmoid(g_mem) * br_mem)
    x = x + merged @ w_out
    x = x + 0.5 * swiglu_ffn(rmsnorm(x, ffn2_norm), ffn2_w_in, ffn2_w_down)
    return x

def second_inputs(seed: int = 0) -> dict:
    key = jax.random.key(seed)
    ks = jax.random.split(key, 32)
    f32 = jnp.float32

    def nrm(k, shape, fan_in):
        return jax.random.normal(k, shape, f32) * (fan_in ** -0.5)

    def gain(k, shape):
        return 1.0 + 0.02 * jax.random.normal(k, shape, f32)

    L = DEPTH_2
    a_im_init = jnp.pi * jnp.arange(SSM_STATE, dtype=f32)
    return {
        "x": jax.random.normal(ks[0], (BATCH, SEQ, D_MODEL), f32),
        "mem": jax.random.normal(ks[1], (BATCH, MEM_LEN, D_MODEL), f32),
        "ffn1_norm": gain(ks[2], (L, D_MODEL)),
        "ffn1_w_in": nrm(ks[3], (L, D_MODEL, 2 * D_FF_2), D_MODEL),
        "ffn1_w_down": nrm(ks[4], (L, D_FF_2, D_MODEL), D_FF_2),
        "mix_norm": gain(ks[5], (L, D_MODEL)),
        "w_in": nrm(ks[6], (L, D_MODEL, IN_WIDTH), D_MODEL),
        "ssm_a_re": -0.5 + 0.01 * jax.random.normal(ks[7], (L, SSM_GROUPS, SSM_STATE), f32),
        "ssm_a_im": a_im_init + 0.01 * jax.random.normal(ks[8], (L, SSM_GROUPS, SSM_STATE), f32),
        "ssm_log_dt": jax.random.uniform(ks[9], (L, SSM_GROUPS), f32,
                                         float(np.log(DT_MIN)), float(np.log(DT_MAX))),
        "ssm_b_re": nrm(ks[10], (L, SSM_GROUPS, SSM_STATE, SSM_GROUP), 2 * SSM_GROUP),
        "ssm_b_im": nrm(ks[11], (L, SSM_GROUPS, SSM_STATE, SSM_GROUP), 2 * SSM_GROUP),
        "ssm_c_re": nrm(ks[12], (L, SSM_GROUPS, SSM_GROUP, SSM_STATE), SSM_STATE),
        "ssm_c_im": nrm(ks[13], (L, SSM_GROUPS, SSM_GROUP, SSM_STATE), SSM_STATE),
        "ssm_d": jax.random.normal(ks[14], (L, SSM_GROUPS, SSM_GROUP), f32),
        "ssm_w_glu": nrm(ks[15], (L, SSM_WIDTH, 2 * D_MODEL), SSM_WIDTH),
        "rel_table": 0.5 * jax.random.normal(ks[16], (REL_BUCKETS, N_ATTN_HEADS), f32),
        "attn_w_up": nrm(ks[17], (L, ATTN_OUT_WIDTH, D_MODEL), ATTN_OUT_WIDTH),
        "mem_norm": gain(ks[18], (L, D_MODEL)),
        "xattn_w_kv": nrm(ks[19], (L, D_MODEL, 2 * XATTN_WIDTH), D_MODEL),
        "xattn_w_up": nrm(ks[20], (L, XATTN_WIDTH, D_MODEL), XATTN_WIDTH),
        "w_out": nrm(ks[21], (L, D_MODEL, D_MODEL), D_MODEL),
        "ffn2_norm": gain(ks[22], (L, D_MODEL)),
        "ffn2_w_in": nrm(ks[23], (L, D_MODEL, 2 * D_FF_2), D_MODEL),
        "ffn2_w_down": nrm(ks[24], (L, D_FF_2, D_MODEL), D_FF_2),
        "final_norm": gain(ks[25], (D_MODEL,)),
    }

def second_block(x, mem, ffn1_norm, ffn1_w_in, ffn1_w_down, mix_norm, w_in,
              ssm_a_re, ssm_a_im, ssm_log_dt, ssm_b_re, ssm_b_im, ssm_c_re, ssm_c_im, ssm_d, ssm_w_glu,
              rel_table, attn_w_up, mem_norm, xattn_w_kv, xattn_w_up, w_out,
              ffn2_norm, ffn2_w_in, ffn2_w_down, final_norm):
    h = x
    for l in range(DEPTH_2):
        h = hybrid_layer_2(h, mem, rel_table, ffn1_norm[l], ffn1_w_in[l], ffn1_w_down[l], mix_norm[l], w_in[l],
                         ssm_a_re[l], ssm_a_im[l], ssm_log_dt[l], ssm_b_re[l], ssm_b_im[l],
                         ssm_c_re[l], ssm_c_im[l], ssm_d[l], ssm_w_glu[l],
                         attn_w_up[l], mem_norm[l], xattn_w_kv[l], xattn_w_up[l], w_out[l],
                         ffn2_norm[l], ffn2_w_in[l], ffn2_w_down[l])
    return rmsnorm(h, final_norm)


def setup_inputs(seed=0):
    out = dict(first_inputs(seed))
    for name, value in second_inputs(seed + 1).items():
        if name != "x":
            out[name + "_2"] = value
    return out


def reference(
    x, norm_mix_pre, norm_mix_post, norm_mlp_pre, norm_mlp_post, w_in, attn_rel_bias, conv_w,
    conv_b, conv_ln_g, conv_ln_b, w_out, w_up, w_down, mem_2, ffn1_norm_2, ffn1_w_in_2,
    ffn1_w_down_2, mix_norm_2, w_in_2, ssm_a_re_2, ssm_a_im_2, ssm_log_dt_2, ssm_b_re_2,
    ssm_b_im_2, ssm_c_re_2, ssm_c_im_2, ssm_d_2, ssm_w_glu_2, rel_table_2, attn_w_up_2,
    mem_norm_2, xattn_w_kv_2, xattn_w_up_2, w_out_2, ffn2_norm_2, ffn2_w_in_2, ffn2_w_down_2,
    final_norm_2,
):
    x = first_block(
        x, norm_mix_pre, norm_mix_post, norm_mlp_pre, norm_mlp_post, w_in, attn_rel_bias,
        conv_w, conv_b, conv_ln_g, conv_ln_b, w_out, w_up, w_down,
    )
    return second_block(
        x, mem_2, ffn1_norm_2, ffn1_w_in_2, ffn1_w_down_2, mix_norm_2, w_in_2, ssm_a_re_2,
        ssm_a_im_2, ssm_log_dt_2, ssm_b_re_2, ssm_b_im_2, ssm_c_re_2, ssm_c_im_2, ssm_d_2,
        ssm_w_glu_2, rel_table_2, attn_w_up_2, mem_norm_2, xattn_w_kv_2, xattn_w_up_2, w_out_2,
        ffn2_norm_2, ffn2_w_in_2, ffn2_w_down_2, final_norm_2,
    )


_drawn_inputs = setup_inputs


def setup_inputs(seed=0):
    import zlib

    import numpy as np

    out = dict(_drawn_inputs(seed))
    spreads = {}
    factors = {'norm_mlp_pre': 3.026,
     'norm_mlp_post': 3.213,
     'conv_ln_g': 3.414,
     'conv_ln_b': 3.704,
     'ffn1_norm_2': 8.0,
     'mix_norm_2': 8.0,
     'ssm_a_re_2': 64.0,
     'ssm_a_im_2': 58.008,
     'ssm_log_dt_2': 64.0,
     'ssm_b_re_2': 64.0,
     'ssm_b_im_2': 64.0,
     'ssm_c_re_2': 64.0,
     'ssm_c_im_2': 64.0,
     'rel_table_2': 2.776,
     'mem_norm_2': 8.0,
     'ffn2_norm_2': 24.754,
     'final_norm_2': 8.006}
    for name, (base, spread) in spreads.items():
        noise = np.random.default_rng([zlib.crc32(name.encode()), seed]).standard_normal(out[name].shape)
        drawn = base * np.exp(spread * noise) if base else spread * noise
        out[name] = __import__('jax').numpy.asarray(drawn.astype(out[name].dtype))
    for name, factor in factors.items():
        out[name] = (out[name] * factor).astype(out[name].dtype)
    return out
```

```python
from contextlib import ExitStack

import concourse.bass as bass
import numpy as np
from concourse import mybir

F32 = mybir.dt.float32
F32R = mybir.dt.float32r
I32 = mybir.dt.int32
ALU = mybir.AluOpType
ACT = mybir.ActivationFunctionType
AX_X = mybir.AxisListType.X

P = 128
SEQ = 512
TOKT = SEQ // P
DM = 1024
KD = DM // P
DEPTH = 2
HD = 64
ATT_HEADS = 6
ATT_W = ATT_HEADS * HD
RET_HEADS = 6
RET_W = RET_HEADS * HD
CONV_W = DM // 4
TAPS = 31
PAD = TAPS - 1
CHUNK = 64
REL_CLIP = 128
D_FF = 4096
EPS = 1e-6
MASKED = -1e30
F2 = 2816
F2T = F2 // P
PATTERNS = 3
SLOTS = 4
A2 = PATTERNS * SLOTS * HD
BUCKETS = 32
MAX_DIST = 2048
ROW = 384
SSM_W = 512
SSM_G = 16
SSM_N = 64
STILES = SSM_W // SSM_G * SSM_N // P
XH = 4
MEM = 256
MEMT = MEM // P
TWO_PI = 2 * np.pi
PI2_A = 6.28125
PI2_B = float(np.float32(np.round((TWO_PI - PI2_A) * 2 ** 20) / 2 ** 20))
PI2_C = float(np.float32(TWO_PI - PI2_A - PI2_B))
BELOW_2PI = 6.283185
BELOW_PI = 3.1415925
MAGIC = 12582912.0
WCOLS = 256
WSIZE = KD * WCOLS
BIAS_ROW = SEQ + P - 1
KB = 1024
BASE = 16640


class Piece:

    def __init__(self, rows, cols, w, kt, kind, src="", group=None):
        self.rows, self.cols, self.w, self.kt, self.kind, self.src = rows, cols, w, kt, kind, src
        self.group = group


def number(pieces, tok_tiles=None):
    units = 0
    groups = []
    for n, b in enumerate(pieces):
        b.n, b.slot = n, n % 2
        b.tiles = b.w // P if b.kind == "feat" else (tok_tiles[n] if tok_tiles else TOKT)
        b.u0 = units
        units += b.tiles
        b.u1 = units
        if b.group is None or n == 0 or pieces[n - 1].group != b.group:
            b.first, b.k0 = True, 0
            groups.append(b.tiles)
        else:
            b.first, b.k0 = False, pieces[n - 1].k0 + pieces[n - 1].kt
        b.last = b.group is None or n + 1 == len(pieces) or pieces[n + 1].group != b.group
        b.g = len(groups) - 1
    for b in pieces:
        b.t0 = sum(groups[:b.g])
        b.free = sum(groups[:b.g - 1]) if b.g >= 2 else 0
        b.bank = 2 * (b.g % 2)
    return pieces


class Turn:

    def __init__(self, i=0, dn=0, du=0, dt=0):
        self.i, self.dn, self.du, self.dt = i, dn, du, dt

    def n(self, v):
        return v + self.i * self.dn

    def loads(self, n):
        return (n // 2 + 1) * 16 + self.i * (self.dn * 8)

    def u(self, v):
        return v + self.i * self.du

    def t(self, v):
        return v + self.i * self.dt


ONCE = Turn()


def layer_pieces():
    out = []
    a = ATT_W

    def feat(c0, c1):
        for c in range(c0, c1, WCOLS):
            out.append(Piece(0, c, min(WCOLS, c1 - c), KD, "feat", "w_in"))

    def tok(c0, c1):
        for c in range(c0, c1, WCOLS):
            out.append(Piece(0, c, min(WCOLS, c1 - c), KD, "tok", "w_in"))

    feat(0, 2 * a)
    tok(2 * a, 3 * a)
    feat(3 * a, 3 * a + 2 * CONV_W)
    r = 3 * a + 2 * CONV_W
    feat(r, r + 2 * RET_W)
    tok(r + 2 * RET_W, r + 3 * RET_W)
    feat(r + 3 * RET_W, r + 4 * RET_W)
    for c in range(0, DM, WCOLS):
        out.append(Piece(0, c, WCOLS, KD, "feat", "w_out"))
    for half in range(2):
        for j in range(8):
            out.append(Piece(0, half * 2048 + j * WCOLS, WCOLS, KD, "feat", "w_up"))
        for j in range(4):
            for kb in range(2):
                out.append(Piece(half * 2048 + kb * KB, j * WCOLS, WCOLS, KD, "feat", "w_down",
                                 group=("down", half, j)))
    return number(out)


FFN_PARTS = (6, 6, 5, 5)
GATES = ("glu_b", "glu_a", "gate0", "attn_up", "gate1", "xattn_up", "gate2")


def third_pieces():
    out, start = [], {}

    def ffn(name):
        start[name + "_up"] = len(out)
        for j in range(F2 // WCOLS):
            for c in (0, F2):
                out.append(Piece(0, c + j * WCOLS, WCOLS, KD, "feat", name + "_in"))
        start[name + "_down"] = len(out)
        for j in range(DM // WCOLS):
            k0 = 0
            for kt in FFN_PARTS:
                out.append(Piece(k0 * P, j * WCOLS, WCOLS, kt, "feat", name + "_down", group=(name, j)))
                k0 += kt

    ffn("ffn1")
    start["mk"] = len(out)
    for c in range(0, 512, WCOLS):
        out.append(Piece(0, c, WCOLS, KD, "feat", "w_kv"))
    start["mv"] = len(out)
    for c in range(512, 1024, WCOLS):
        out.append(Piece(0, c, WCOLS, KD, "tok", "w_kv"))
    col = 0
    for name, width, kind in (("u", SSM_W, "feat"), ("q", A2, "feat"), ("k", A2, "feat"), ("v", A2, "tok"),
                              ("xq", 512, "feat")):
        start[name] = len(out)
        for c in range(col, col + width, WCOLS):
            out.append(Piece(0, c, WCOLS, KD, kind, "w_in2"))
        col += width
    start["gates"] = len(out)
    for p in range(DM // WCOLS):
        c = p * WCOLS
        for name in GATES:
            if name == "glu_a":
                out.append(Piece(0, c, WCOLS, 4, "feat", "w_glu"))
            elif name == "glu_b":
                out.append(Piece(0, DM + c, WCOLS, 4, "feat", "w_glu"))
            elif name == "attn_up":
                out.append(Piece(0, c, WCOLS, 2, "feat", "w_attn_up"))
            elif name == "xattn_up":
                out.append(Piece(0, c, WCOLS, 4, "feat", "w_xattn_up"))
            else:
                out.append(Piece(0, col + int(name[-1]) * DM + c, WCOLS, KD, "feat", "w_in2"))
    start["w_out2"] = len(out)
    for c in range(0, DM, WCOLS):
        out.append(Piece(0, c, WCOLS, KD, "feat", "w_out2"))
    ffn("ffn2")
    tok_tiles = [MEMT if b.kind == "tok" and b.src == "w_kv" else TOKT for b in out]
    return number(out, tok_tiles), start


def build(nc, ins, outs):
    A = ins
    plan1 = layer_pieces()
    plan2, AT2 = third_pieces()
    with ExitStack() as ctx:
        def at(name, shape, dt, kb):
            return nc.alloc_sbuf_tensor_at(name, shape, dt, offset=BASE + int(kb * 1024))

        def sem(name):
            s = ctx.enter_context(nc.semaphore(name))
            return s

        w_raw = at("w_raw", [P, 2, WSIZE], F32, 0)
        w_hi = at("w_hi", [P, 2, WSIZE], F32R, 16)
        w_lo = at("w_lo", [P, 2, WSIZE], F32R, 32)
        x_sb = at("x_sb", [P, KD, SEQ], F32, 48)
        h_hi = at("h_hi", [P, KD, SEQ], F32R, 64)
        h_lo = at("h_lo", [P, KD, SEQ], F32R, 80)
        FZ = 96
        OZ = FZ + 88
        out_sb = at("out_sb", [P, KD, SEQ], F32, OZ)
        CZ = OZ + 16
        ident = at("ident_sb", [P, P], F32, CZ)
        ones = at("ones_sb", [P, P], F32, CZ + 0.5)
        head_ones = at("head_ones_sb", [P, P], F32, CZ + 1)
        swap = at("swap_sb", [P, P], F32, CZ + 1.5)
        rs = at("rs", [P, SEQ], F32, CZ + 2)
        par = at("par_sb", [P, 128], F32, CZ + 4)
        tiny = at("tiny", [P, 64], F32, CZ + 4.5)
        eps_c = at("eps_c", [P, 1], F32, CZ + 4.75)
        quarter = at("quarter", [P, 1], F32, CZ + 4.8125)
        par2 = at("par2_sb", [P, 96], F32, CZ + 5)

        qk = at("qk", [P, 6, SEQ], F32, FZ)
        av = at("av", [P, TOKT, ATT_W], F32, FZ + 12)
        rv = at("rv", [P, TOKT, RET_W], F32, FZ + 18)
        rg = at("rg", [P, 3, SEQ], F32, FZ + 24)
        rqk = at("rqk", [P, 6, SEQ], F32, FZ + 30)
        ca = at("ca", [P, 2, SEQ + PAD], F32, FZ + 42)
        cg = at("cg", [P, 2, SEQ], F32, FZ + 46.25)
        bias_t = at("bias_t", [P, ATT_HEADS, SEQ], F32, FZ + 50.5)
        decay_t = at("decay_t", [P, RET_HEADS, SEQ], F32, FZ + 62.5)
        cos_t = at("cos_t", [P, SEQ], F32, FZ + 74.5)
        sin_t = at("sin_t", [P, SEQ], F32, FZ + 76.5)
        probs = at("probs", [P, 4, SEQ], F32, FZ + 78.5)
        sc_off = [0, 512, 896, 1152]
        ret_sc = at("ret_sc", [P, 2, 1280], F32, 64)
        ln_sq = at("ln_sq", [P, 5, SEQ], F32, 74)
        rot_a = at("rot_a", [P, 2, SEQ], F32, 84)
        probs_t = at("probs_t", [P, 2, SEQ], F32, 84)
        ln_rs = at("ln_rs", [P, 4, SEQ], F32, 88)
        f_hi = at("f_hi", [P, 16, SEQ], F32R, FZ)
        f_lo = at("f_lo", [P, 16, SEQ], F32R, FZ + 32)
        sq_f = at("sq_f", [P, KD, SEQ], F32, FZ + 64)
        tt = at("tt", [P, 4, SEQ], F32, FZ + 80)
        part = at("part", [P, KD, SEQ], F32, 64)

        bank = [ctx.enter_context(nc.psum_tensor(f"gemm{i}", [P, SEQ], F32)) for i in range(4)]
        s_ps = [ctx.enter_context(nc.psum_tensor(f"score{i}", [P, SEQ], F32)) for i in range(2)]
        t_ps = ctx.enter_context(nc.psum_tensor("turned", [P, SEQ], F32))
        o_ps = ctx.enter_context(nc.psum_tensor("mixed", [P, SEQ], F32))

        score_bank = [s_ps[0], s_ps[1], bank[0], bank[1]]
        turn_bank = [t_ps, bank[2]]

        bias_rep = nc.dram_tensor("bias_rep", [DEPTH, ATT_HEADS, P, BIAS_ROW], F32, kind="Internal").ap()

        def skewed(rep, width, cols):
            flat = rep.rearrange("h p n -> h (p n)")[:, P - 1:P - 1 + P * (width - 1)]
            return flat.rearrange("h (p n) -> p h n", n=width - 1)[:, :, 0:cols]

        consts_in = sem("consts_in")

        eps_set, picked, picked_out = sem("eps_set"), sem("picked"), sem("picked_out")
        t5_rep = nc.dram_tensor("t5_rep", [PATTERNS, SLOTS, P, ROW], F32, kind="Internal").ap()
        table = at("table_sb", [BUCKETS + 1, PATTERNS * SLOTS], F32, FZ)
        one_hot = at("one_hot_sb", [BUCKETS + 1, PATTERNS, ROW], F32, FZ + 1)
        row_sb = at("row_sb", [SLOTS, PATTERNS, ROW], F32, FZ + 6)
        with nc.Block() as block:
            @block.gpsimd
            def _(pool):
                pool.memset(table[:], MASKED).then_inc(eps_set, 1)

            @block.tensor
            def _(pe):
                pe.wait_ge(consts_in, 16 * (7 + DEPTH))
                for g in range(PATTERNS):
                    pe.matmul(bank[g][0:SLOTS, 0:ROW], table[:, SLOTS * g:SLOTS * g + SLOTS], one_hot[:, g, :],
                              start=True, stop=True).then_inc(picked, 1)

            @block.sync
            def _(sp):
                for dst, src in ((ident, "c_ident"), (ones, "c_ones"), (head_ones, "c_head_ones"), (swap, "c_swap")):
                    sp.dma_start(dst[:], A[src]).then_inc(consts_in, 16)
                sp.dma_start(x_sb[:], A["x"].rearrange("(k p) t -> p k t", p=P)).then_inc(consts_in, 16)
                for l in range(DEPTH):
                    sp.dma_start(bias_rep[l], A["att_bias_rows"][l].unsqueeze(1).broadcast_to(
                        [ATT_HEADS, P, BIAS_ROW])).then_inc(consts_in, 16)
                sp.dma_start(one_hot[:], A["c_one_hot"]).then_inc(consts_in, 16)
                sp.wait_ge(eps_set, 1)
                sp.dma_start(table[0:BUCKETS, :], A["rel_table"]).then_inc(consts_in, 16)
                sp.wait_ge(consts_in, 16 * (7 + DEPTH))
                sp.wait_ge(picked_out, PATTERNS)
                for g in range(PATTERNS):
                    sp.dma_start(t5_rep[g], row_sb[:, g, :].unsqueeze(1).broadcast_to(
                        [SLOTS, P, ROW])).then_inc(consts_in, 16)
                sp.wait_ge(consts_in, 16 * (7 + PATTERNS + DEPTH))

            @block.vector
            def _(dve):
                dve.memset(eps_c[:], EPS)
                dve.memset(quarter[:], np.pi / 2)
                for g in range(PATTERNS):
                    dve.wait_ge(picked, g + 1)
                    dve.tensor_copy(row_sb[:, g, :], bank[g][0:SLOTS, 0:ROW]).then_inc(picked_out, 1)

        names = ["w_in0", "w_in1", "w_rounded", "w_rest", "units", "g_free", "par_in", "tab_in", "squares",
                 "norm_sum", "norm_root", "norm_inv", "normed", "norm_hi", "h_ready", "x_done", "dve_own",
                 "centred", "maxed", "glu", "taps", "ln_mean", "ln_sq_s", "ln_var", "ln_root", "ln_done", "rot_ps", "rot_done",
                 "score_ps", "biased", "exped", "inverted", "scaled", "turned_ps", "turned", "mixed_ps", "att_out",
                 "ret_ps", "ret_sc_s", "ret_mix", "ret_out", "y_hi", "f_sq", "f_hi_s", "f_ready", "part_done", "act_own"]
        S = {n: sem(n) for n in names}
        w_in_s = [S["w_in0"], S["w_in1"]]

        def view(buf, b):
            return buf[:, b.slot, 0:b.kt * b.w].rearrange("p (k c) -> p k c", k=b.kt)

        def load_block(sp, src, b, t=ONCE):
            if b.n >= 2:
                sp.wait_ge(S["w_rounded"], t.n(b.n - 1))
                sp.wait_ge(S["w_rest"], t.n(b.n - 1))
            size = b.kt * b.w
            sp.dma_start(w_raw[:, b.slot, 0:size], src[t.n(b.n), :, 0:size]).then_inc(w_in_s[b.slot], 16)

        def round_block(act, plan, n, t=ONCE, whole=False):
            if isinstance(t.n(n), int) and t.n(n) >= len(plan):
                return
            b = plan[n]
            act.wait_ge(w_in_s[b.slot], t.loads(n))
            if n >= 2:
                act.wait_ge(S["units"], t.u(plan[n - 2].u1))
            size = WSIZE if whole else b.kt * b.w
            act.activation(w_hi[:, b.slot, 0:size], w_raw[:, b.slot, 0:size], ACT.Copy).then_inc(S["w_rounded"], 1)

        def rest_block(dve, plan, n, t=ONCE, whole=False):
            if isinstance(t.n(n), int) and t.n(n) >= len(plan):
                return
            b = plan[n]
            dve.wait_ge(S["w_rounded"], t.n(n + 1))
            size = WSIZE if whole else b.kt * b.w
            dve.tensor_tensor(w_lo[:, b.slot, 0:size], w_raw[:, b.slot, 0:size],
                              w_hi[:, b.slot, 0:size].bitcast(F32), ALU.subtract).then_inc(S["w_rest"], 1)

        def product(pe, b, hi, lo, t=ONCE, ready=None, k0=None, width=SEQ, tokens=None, between=None):
            tokens = tokens or (lambda m: lambda a: a[:, m * P:(m + 1) * P])
            pe.wait_ge(S["w_rest"], t.n(b.n + 1))
            k0 = b.k0 if k0 is None else k0
            wh, wl = view(w_hi, b), view(w_lo, b)
            for m in range(b.tiles):
                if b.first and b.free:
                    pe.wait_ge(S["g_free"], t.t(b.free))
                for k in range(b.kt):
                    if ready is not None and m == 0:
                        pe.wait_ge(S["h_ready"], ready + k + 1)
                    if b.kind == "feat":
                        c = slice(m * P, (m + 1) * P)
                        dst = bank[b.bank + m][:, 0:width]
                        trio = ((wh[:, k, c], hi[:, k0 + k, :]), (wh[:, k, c], lo[:, k0 + k, :]),
                                (wl[:, k, c], hi[:, k0 + k, :]))
                    else:
                        pick = tokens(m)
                        dst = bank[b.bank + m // 2][:, (m % 2) * 256:(m % 2) * 256 + b.w]
                        h, r = pick(hi[:, k, :]), pick(lo[:, k, :])
                        trio = ((h, wh[:, k, :]), (h, wl[:, k, :]), (r, wh[:, k, :]))
                    for j, (lhs, rhs) in enumerate(trio):
                        mm = pe.matmul(dst, lhs, rhs, start=b.first and k == 0 and j == 0,
                                       stop=b.last and k == b.kt - 1 and j == 2)
                mm.then_inc(S["units"], 1)
                if between:
                    between(m)

        def tile_of(b, m, width=SEQ):
            if b.kind == "feat":
                return bank[b.bank + m][:, 0:width]
            return bank[b.bank + m // 2][:, (m % 2) * 256:(m % 2) * 256 + b.w]

        def norm_squares(act, i, src, sq, wait=None, count=KD, own=None, act_src=False):
            for k in range(KD):
                if wait is not None:
                    act.wait_ge(wait[0], wait[1] + k + 1)
                act.activation(sq[:, k, :], src[:, k, :], ACT.Square).then_inc(S["squares"], 1)

        def norm_total(pe, i, sq, n=SEQ):
            for k in range(KD):
                pe.wait_ge(S["squares"], KD * i + k + 1)
                if k == 0 and i:
                    pe.wait_ge(S["norm_root"], i)
                mm = pe.matmul(o_ps[:, 0:n], ones[:], sq[:, k, :], start=k == 0, stop=k == KD - 1)
            mm.then_inc(S["norm_sum"], 1)

        def norm_rooted(act, i, n=SEQ):
            act.wait_ge(S["norm_sum"], i + 1)
            if i:
                act.wait_ge(S["normed"], KD * i)
            act.activation(rs[:, 0:n], o_ps[:, 0:n], ACT.Sqrt, scale=1.0 / DM, bias=eps_c[:, 0:1]).then_inc(S["norm_root"], 1)

        def norm_inverse(dve, i, n=SEQ):
            dve.wait_ge(S["norm_root"], i + 1)
            dve.reciprocal(rs[:, 0:n], rs[:, 0:n]).then_inc(S["norm_inv"], 1)
            dve.wait_ge(S["norm_inv"], i + 1)

        def norm_scale(dve, i, k, src, dst, gain, n=SEQ):
            dve.scalar_tensor_tensor(out=dst[:, k, :], in0=src[:, k, :], scalar=gain[:, k:k + 1], in1=rs[:, 0:n],
                                     op0=ALU.mult, op1=ALU.mult).then_inc(S["normed"], 1)

        def split_hi(act, i, j, src, wait_sem, wait_base, hi=h_hi):
            for k in range(KD):
                act.wait_ge(wait_sem, wait_base + k + 1)
                act.activation(hi[:, k, :], src[:, k, :], ACT.Copy).then_inc(S["norm_hi"], 1)

        def pre_norm_dve(dve, i, j, gain, n=SEQ, src=x_sb, tmp=out_sb, hi=h_hi, lo=h_lo):
            norm_inverse(dve, i, n)
            for k in range(KD + 1):
                if k < KD:
                    norm_scale(dve, i, k, src, tmp, gain, n)
                if k:
                    dve.wait_ge(S["norm_hi"], KD * j + k)
                    dve.tensor_tensor(lo[:, k - 1, :], tmp[:, k - 1, :], hi[:, k - 1, :].bitcast(F32),
                                      ALU.subtract).then_inc(S["h_ready"], 1)

        def post_norm_dve(dve, i, gain, base):
            norm_inverse(dve, i)
            for k in range(KD + 1):
                if k < KD:
                    norm_scale(dve, i, k, out_sb, out_sb, gain)
                if k:
                    dve.wait_ge(S["normed"], KD * i + k)
                    dve.tensor_tensor(x_sb[:, k - 1, :], x_sb[:, k - 1, :], out_sb[:, k - 1, :],
                                      ALU.add).then_inc(S["x_done"], 1)

        gains = {n: par[:, 8 * i:8 * i + 8] for i, n in enumerate(("mix_pre", "mix_post", "mlp_pre", "mlp_post"))}
        conv_w = par[:, 32:94].rearrange("p (j t) -> p j t", j=2)
        conv_b, ln_g, ln_b = par[:, 94:96], par[:, 96:98], par[:, 98:100]
        N_IN = 14
        W_OUT = 14
        UP = [18, 34]
        DOWN = [26, 42]
        PAIRS = RET_HEADS // 2
        LN = [(ones, (3, 4), CONV_W)] + [(head_ones, (5 + p,), HD) for p in range(PAIRS)]
        TAP_OPS = 2 * TAPS
        TAP_SLOTS = 7

        with nc.Fori(0, DEPTH) as layer:
            with nc.Block() as block:
                @block.sync
                def _(sp):
                    sp.dma_start(par[:, 0:100], A["par1"][layer]).then_inc(S["par_in"], 16)
                    src = A["w1"][layer]
                    for b in plan1[:2]:
                        load_block(sp, src, b)
                    for dst, s in ((cos_t[:], A["c_cos"]), (sin_t[:], A["c_sin"]),
                                   (decay_t[:], A["c_decay"]), (bias_t[:], skewed(bias_rep[layer], BIAS_ROW, SEQ))):
                        sp.dma_start(dst, s).then_inc(S["tab_in"], 16)
                    for b in plan1[2:N_IN]:
                        load_block(sp, src, b)
                    with sp.Fori(0, (len(plan1) - N_IN) // 2) as i:
                        for b in plan1[N_IN:N_IN + 2]:
                            load_block(sp, src, b, Turn(i, dn=2))

                @block.tensor
                def _(pe):
                    norm_total(pe, 0, out_sb)
                    for b in plan1[:N_IN]:
                        product(pe, b, h_hi, h_lo, ready=0 if b.n == 0 else None)

                    for j in range(6):
                        if j >= 2:
                            pe.wait_ge(S["rot_done"], j - 1)
                        if j == 0:
                            pe.wait_ge(S["g_free"], plan1[9].t0 + 2)
                        pe.matmul(s_ps[j % 2][:], swap[:], rqk[:, j, :], start=True, stop=True).then_inc(S["rot_ps"], 1)

                    def layer_norm_mean(j):
                        mat, tiles, _ = LN[j]
                        for q, m in enumerate(tiles):
                            mm = pe.matmul(t_ps[:], mat[:], out_sb[:, m, :], start=q == 0, stop=q == len(tiles) - 1)
                        mm.then_inc(S["ln_mean"], 1)

                    def layer_norm_var(j):
                        mat, tiles, _ = LN[j]
                        pe.wait_ge(S["ln_sq_s"], sum(len(LN[q][1]) for q in range(j + 1)))
                        for q, m in enumerate(tiles):
                            mm = pe.matmul(t_ps[:], mat[:], ln_sq[:, m - 3, :], start=q == 0, stop=q == len(tiles) - 1)
                        mm.then_inc(S["ln_var"], 1)

                    pe.wait_ge(S["taps"], TAP_OPS)
                    layer_norm_mean(0)
                    layer_norm_var(0)

                    pe.wait_ge(S["rot_done"], 6)
                    pe.wait_ge(S["ln_root"], 1)
                    steps = [(h, q) for h in range(ATT_HEADS) for q in range(TOKT)]

                    def scores(s):
                        h, q = steps[s]
                        r = slice(HD * (h % 2), HD * (h % 2) + HD)
                        if s >= 4:
                            pe.wait_ge(S["biased"], s - 3)
                        pe.matmul(score_bank[s % 4][:, 0:P * (q + 1)], qk[r, h // 2, P * q:P * q + P],
                                  qk[r, 3 + h // 2, 0:P * (q + 1)], start=True, stop=True).then_inc(S["score_ps"], 1)

                    def turn(s):
                        h, q = steps[s]
                        pe.wait_ge(S["scaled"], s + 1)
                        if s >= 2:
                            pe.wait_ge(S["turned"], s - 1)
                        for j in range(q + 1):
                            mm = pe.transpose(turn_bank[s % 2][:, P * j:P * j + P], probs[:, s % 4, P * j:P * j + P],
                                              ident[:])
                        mm.then_inc(S["turned_ps"], 1)

                    def mix(s):
                        h, q = steps[s]
                        pe.wait_ge(S["turned"], s + 1)
                        if q == 0 and h % 2 == 0 and h:
                            pe.wait_ge(S["att_out"], h // 2)
                        r = slice(HD * (h % 2), HD * (h % 2) + HD)
                        for j in range(q + 1):
                            mm = pe.matmul(o_ps[r, P * q:P * q + P], av[:, j, HD * h:HD * h + HD],
                                           probs_t[:, s % 2, P * j:P * j + P], start=j == 0, stop=j == q)
                        mm.then_inc(S["mixed_ps"], 1)

                    n = len(steps)
                    pe.wait_ge(S["g_free"], plan1[N_IN].t0)
                    for s in range(n + 3):
                        if s < n:
                            scores(s)
                        if 2 <= s <= n + 1:
                            turn(s - 2)
                        if s >= 3:
                            mix(s - 3)

                    rsteps = [(h, j) for h in range(RET_HEADS) for j in range(TOKT)]

                    def ret_scores(s):
                        h, j = rsteps[s]
                        r = slice(HD * (h % 2), HD * (h % 2) + HD)
                        if s < 2:
                            pe.wait_ge(S["biased"], n - 3 + s)
                        else:
                            pe.wait_ge(S["ret_sc_s"], s - 1)
                        pe.matmul(s_ps[s % 2][:, 0:SEQ - P * j], rqk[r, 3 + h // 2, P * j:P * j + P],
                                  rqk[r, h // 2, P * j:SEQ], start=True, stop=True).then_inc(S["ret_ps"], 1)

                    def ret_mixed(s):
                        h, j = rsteps[s]
                        pe.wait_ge(S["ret_sc_s"], s + 1)
                        if j == 0 and h % 2 == 0:
                            if h:
                                pe.wait_ge(S["ret_out"], h // 2)
                            else:
                                pe.wait_ge(S["att_out"], ATT_HEADS // 2)
                        r = slice(HD * (h % 2), HD * (h % 2) + HD)
                        pe.matmul(o_ps[r, P * j:SEQ], rv[:, j, HD * h:HD * h + HD],
                                  ret_sc[:, h % 2, sc_off[j]:sc_off[j] + SEQ - P * j],
                                  start=j == 0, stop=j == TOKT - 1).then_inc(S["ret_mix"], 1)

                    for s in range(len(rsteps) + 1):
                        if s < len(rsteps):
                            ret_scores(s)
                        if s:
                            ret_mixed(s - 1)
                    for p in range(PAIRS):
                        pe.wait_ge(S["ret_out"], p + 1)
                        pe.wait_ge(S["ln_root"], p + 1)
                        layer_norm_mean(1 + p)
                        layer_norm_var(1 + p)

                    for b in plan1[W_OUT:W_OUT + 4]:
                        product(pe, b, h_hi, h_lo, ready=KD if b.n == W_OUT else None)
                    norm_total(pe, 1, sq_f)
                    norm_total(pe, 2, out_sb)
                    for half in range(2):
                        first = plan1[UP[half]]
                        if half == 0:
                            pe.wait_ge(S["h_ready"], 3 * KD)
                        with pe.Fori(0, 4) as i:
                            for b in plan1[first.n:first.n + 2]:
                                product(pe, b, h_hi, h_lo, Turn(i, dn=2, du=4, dt=4))
                        pe.wait_ge(S["f_ready"], 16 * (half + 1))
                        with pe.Fori(0, 2) as i:
                            for b in plan1[DOWN[half]:DOWN[half] + 4]:
                                product(pe, b, f_hi, f_lo, Turn(i, dn=4, du=8, dt=4))
                    norm_total(pe, 3, sq_f)

                @block.scalar
                def _(act):
                    norm_squares(act, 0, x_sb, out_sb)
                    round_block(act, plan1, 0)
                    round_block(act, plan1, 1)
                    norm_rooted(act, 0)
                    split_hi(act, 0, 0, out_sb, S["normed"], 0)

                    def evacuate(b, dst, func=ACT.Copy):
                        for m in range(b.tiles):
                            act.wait_ge(S["units"], b.u0 + (m + 1 if b.kind == "feat" else m // 2 * 2 + 2))
                            act.activation(dst(m), tile_of(b, m), func).then_inc(S["g_free"], 1)

                    for b in plan1[:N_IN]:
                        if b.n < 3:
                            evacuate(b, lambda m: qk[:, 2 * b.n + m, :])
                        elif b.n < 5:
                            evacuate(b, lambda m: av[:, m, 256 * (b.n - 3):256 * (b.n - 3) + b.w])
                        elif b.n == 5:
                            evacuate(b, lambda m: ca[:, m, PAD:PAD + SEQ])
                        elif b.n == 6:
                            evacuate(b, lambda m: cg[:, m, :], ACT.Sigmoid)
                        elif b.n < 10:
                            evacuate(b, lambda m: rqk[:, 2 * (b.n - 7) + m, :])
                        elif b.n < 12:
                            evacuate(b, lambda m: rv[:, m, 256 * (b.n - 10):256 * (b.n - 10) + b.w])
                        else:
                            evacuate(b, lambda m: rg[:, 2 * (b.n - 12) + m, :], ACT.Silu)
                        round_block(act, plan1, b.n + 2)

                    def layer_norm(j):
                        _, tiles, width = LN[j]
                        before = sum(len(LN[q][1]) for q in range(j))
                        for q, m in enumerate(tiles):
                            act.wait_ge(S["centred"], before + q + 1)
                            act.activation(ln_sq[:, m - 3, :], out_sb[:, m, :], ACT.Square).then_inc(S["ln_sq_s"], 1)
                        act.wait_ge(S["ln_var"], j + 1)
                        act.activation(ln_rs[:, j, :], t_ps[:], ACT.Sqrt, scale=1.0 / width,
                                       bias=eps_c[:, 0:1]).then_inc(S["ln_root"], 1)

                    layer_norm(0)
                    for q in range(2):
                        act.wait_ge(S["ln_done"], q + 1)
                        act.activation(out_sb[:, 3 + q, :], out_sb[:, 3 + q, :], ACT.Silu).then_inc(S["act_own"], 1)

                    steps = [(h, q) for h in range(ATT_HEADS) for q in range(TOKT)]
                    n = len(steps)
                    for s in range(n + 3):
                        if s < n:
                            q = steps[s][1]
                            act.wait_ge(S["maxed"], s + 1)
                            act.activation(probs[:, s % 4, 0:P * (q + 1)], probs[:, s % 4, 0:P * (q + 1)], ACT.Exp,
                                           bias=tiny[:, s % 4:s % 4 + 1],
                                           accum_out=tiny[:, 4 + s % 4:5 + s % 4]).then_inc(S["exped"], 1)
                        if 2 <= s <= n + 1:
                            p = s - 2
                            q = steps[p][1]
                            act.wait_ge(S["turned_ps"], p + 1)
                            if p >= 2:
                                act.wait_ge(S["mixed_ps"], p - 1)
                            act.activation(probs_t[:, p % 2, 0:P * (q + 1)], turn_bank[p % 2][:, 0:P * (q + 1)],
                                           ACT.Copy).then_inc(S["turned"], 1)
                        if s >= 3 and (s - 2) % (2 * TOKT) == 0:
                            pair = (s - 2) // (2 * TOKT)
                            act.wait_ge(S["mixed_ps"], 2 * TOKT * pair)
                            act.activation(out_sb[:, pair - 1, :], o_ps[:], ACT.Copy).then_inc(S["att_out"], 1)
                    for p in range(PAIRS):
                        act.wait_ge(S["ret_mix"], 2 * TOKT * (p + 1))
                        act.activation(out_sb[:, 5 + p, :], o_ps[:], ACT.Copy).then_inc(S["ret_out"], 1)
                    for p in range(PAIRS):
                        layer_norm(1 + p)
                    act.wait_ge(S["ln_done"], 5)
                    act.wait_ge(S["act_own"], 2)
                    act.wait_ge(S["att_out"], 3)
                    for k in range(KD):
                        act.activation(h_hi[:, k, :], out_sb[:, k, :], ACT.Copy).then_inc(S["norm_hi"], 1)
                    for b in plan1[W_OUT:W_OUT + 4]:
                        evacuate(b, lambda m: out_sb[:, 2 * (b.n - W_OUT) + m, :])
                        round_block(act, plan1, b.n + 2)
                    norm_squares(act, 1, out_sb, sq_f, wait=(S["g_free"], plan1[W_OUT].t0))
                    norm_rooted(act, 1)
                    norm_squares(act, 2, x_sb, out_sb, wait=(S["x_done"], 0))
                    norm_rooted(act, 2)
                    split_hi(act, 2, 2, out_sb, S["normed"], 2 * KD)
                    for half in range(2):
                        first = plan1[UP[half]]
                        with act.Fori(0, 4) as i:
                            t = Turn(i, dn=2, du=4, dt=4)
                            for b in plan1[first.n:first.n + 2]:
                                j = b.n - first.n
                                for m in range(2):
                                    act.wait_ge(S["units"], t.u(b.u0 + m + 1))
                                    act.activation(tt[:, 2 * j + m, :], tile_of(b, m), ACT.Relu).then_inc(S["g_free"], 1)
                                for m in range(2):
                                    act.wait_ge(S["f_sq"], 16 * half + i * 4 + (2 * j + m + 1))
                                    act.activation(f_hi[:, i * 4 + (2 * j + m), :], tt[:, 2 * j + m, :],
                                                   ACT.Copy).then_inc(S["f_hi_s"], 1)
                                round_block(act, plan1, b.n + 2, t)

                        def down(t, dst):
                            for b in plan1[DOWN[half]:DOWN[half] + 4]:
                                if b.last:
                                    for m in range(2):
                                        act.wait_ge(S["units"], t.u(b.u0 + m + 1))
                                        act.activation(dst[:, t.i * 4 + (b.n - DOWN[half]) // 2 * 2 + m, :],
                                                       tile_of(b, m), ACT.Copy).then_inc(S["g_free"], 1)
                                round_block(act, plan1, b.n + 2, t)

                        if half == 0:
                            with act.Fori(0, 2) as i:
                                down(Turn(i, dn=4, du=8, dt=4), out_sb)
                        else:
                            for i in range(2):
                                down(Turn(i, dn=4, du=8, dt=4), part)
                    norm_squares(act, 3, out_sb, sq_f, wait=(S["part_done"], 0))
                    norm_rooted(act, 3)

                @block.vector
                def _(dve):
                    own = [0]

                    def step(instruction):
                        own[0] += 1
                        instruction.then_inc(S["dve_own"], 1)
                        dve.wait_ge(S["dve_own"], own[0])

                    for j in range(2):
                        step(dve.memset(ca[:, j, 0:PAD], 0.0))
                    rest_block(dve, plan1, 0)
                    rest_block(dve, plan1, 1)
                    dve.wait_ge(S["par_in"], 16)
                    pre_norm_dve(dve, 0, 0, gains["mix_pre"])

                    def tap(t):
                        q, j = t % 2, t // 2
                        acc = out_sb[:, 3 + q, :]
                        if j == 0:
                            ins = dve.tensor_scalar(acc, ca[:, q, 0:SEQ], conv_w[:, q, 0:1], conv_b[:, q:q + 1],
                                                    ALU.mult, ALU.add)
                        else:
                            dve.wait_ge(S["taps"], t - 1)
                            ins = dve.scalar_tensor_tensor(out=acc, in0=ca[:, q, j:j + SEQ],
                                                           scalar=conv_w[:, q, j:j + 1], in1=acc,
                                                           op0=ALU.mult, op1=ALU.add)
                        ins.then_inc(S["taps"], 1)

                    per = -(-TAP_OPS // TAP_SLOTS)
                    for b in plan1[:N_IN]:
                        rest_block(dve, plan1, b.n + 2)
                        at_slot = b.n - (N_IN - TAP_SLOTS)
                        if at_slot == 0:
                            dve.wait_ge(S["g_free"], plan1[6].t0 + 2)
                            for q in range(2):
                                step(dve.tensor_tensor(ca[:, q, PAD:PAD + SEQ], ca[:, q, PAD:PAD + SEQ], cg[:, q, :],
                                                       ALU.mult))
                        if at_slot >= 0:
                            for t in range(at_slot * per, min(TAP_OPS, (at_slot + 1) * per)):
                                tap(t)

                    dve.wait_ge(S["tab_in"], 64)
                    for j in range(6):
                        dve.wait_ge(S["rot_ps"], j + 1)
                        if j:
                            dve.wait_ge(S["rot_done"], j)
                        dve.tensor_tensor(rot_a[:, 0, :], rqk[:, j, :], cos_t[:], ALU.mult)
                        step(dve.tensor_tensor(rot_a[:, 1, :], s_ps[j % 2][:], sin_t[:], ALU.mult))
                        dve.tensor_tensor(rqk[:, j, :], rot_a[:, 0, :], rot_a[:, 1, :],
                                          ALU.add).then_inc(S["rot_done"], 1)

                    def layer_norm(j):
                        _, tiles, width = LN[j]
                        dve.wait_ge(S["ln_mean"], j + 1)
                        for m in tiles:
                            dve.scalar_tensor_tensor(out=out_sb[:, m, :], in0=t_ps[:], scalar=-1.0 / width,
                                                     in1=out_sb[:, m, :], op0=ALU.mult,
                                                     op1=ALU.add).then_inc(S["centred"], 1)
                        dve.wait_ge(S["ln_root"], j + 1)
                        step(dve.reciprocal(ln_rs[:, j, :], ln_rs[:, j, :]))
                        for q, m in enumerate(tiles):
                            step(dve.tensor_tensor(out_sb[:, m, :], out_sb[:, m, :], ln_rs[:, j, :], ALU.mult))
                            if j == 0:
                                ins = dve.tensor_scalar(out_sb[:, m, :], out_sb[:, m, :], ln_g[:, q:q + 1],
                                                        ln_b[:, q:q + 1], ALU.mult, ALU.add)
                            else:
                                ins = dve.tensor_tensor(out_sb[:, m, :], out_sb[:, m, :], rg[:, j - 1, :], ALU.mult)
                            ins.then_inc(S["ln_done"], 1)

                    layer_norm(0)

                    step(dve.memset(bias_t[0:CHUNK, :, SEQ - CHUNK:SEQ], MASKED))
                    steps = [(h, q) for h in range(ATT_HEADS) for q in range(TOKT)]
                    n = len(steps)
                    for s in range(n + 1):
                        p = s - 1
                        if s < n:
                            h, q = steps[s]
                            size = P * (q + 1)
                            row = probs[:, s % 4, 0:size]
                            dve.wait_ge(S["score_ps"], s + 1)
                            if s >= 4:
                                dve.wait_ge(S["turned_ps"], s - 3)
                            dve.scalar_tensor_tensor(out=row, in0=score_bank[s % 4][:, 0:size], scalar=HD ** -0.5,
                                                     in1=bias_t[:, h, SEQ - size:SEQ], op0=ALU.mult,
                                                     op1=ALU.add).then_inc(S["biased"], 1)
                        if s:
                            dve.wait_ge(S["exped"], s)
                            dve.reciprocal(tiny[:, 8 + p % 4:9 + p % 4], tiny[:, 4 + p % 4:5 + p % 4]).then_inc(
                                S["inverted"], 1)
                        if s < n:
                            dve.wait_ge(S["biased"], s + 1)
                            dve.tensor_reduce(tiny[:, s % 4:s % 4 + 1], row, AX_X, ALU.max,
                                              negate=True).then_inc(S["maxed"], 1)
                        if s:
                            size = P * (steps[p][1] + 1)
                            dve.wait_ge(S["inverted"], s)
                            dve.tensor_scalar(probs[:, p % 4, 0:size], probs[:, p % 4, 0:size],
                                              tiny[:, 8 + p % 4:9 + p % 4], None, ALU.mult).then_inc(S["scaled"], 1)

                    for h in range(RET_HEADS):
                        if h >= 2:
                            dve.wait_ge(S["ret_mix"], TOKT * (h - 1))
                        for j in range(TOKT):
                            size = SEQ - P * j
                            dve.wait_ge(S["ret_ps"], TOKT * h + j + 1)
                            dve.scalar_tensor_tensor(out=ret_sc[:, h % 2, sc_off[j]:sc_off[j] + size],
                                                     in0=s_ps[j % 2][:, 0:size], scalar=HD ** -0.5,
                                                     in1=decay_t[:, h, 0:size], op0=ALU.mult,
                                                     op1=ALU.mult).then_inc(S["ret_sc_s"], 1)
                    for p in range(PAIRS):
                        layer_norm(1 + p)
                    for k in range(KD):
                        dve.wait_ge(S["norm_hi"], KD + k + 1)
                        dve.tensor_tensor(h_lo[:, k, :], out_sb[:, k, :], h_hi[:, k, :].bitcast(F32),
                                          ALU.subtract).then_inc(S["h_ready"], 1)
                    for b in plan1[W_OUT:W_OUT + 4]:
                        rest_block(dve, plan1, b.n + 2)
                    post_norm_dve(dve, 1, gains["mix_post"], 0)
                    pre_norm_dve(dve, 2, 2, gains["mlp_pre"])
                    for half in range(2):
                        first = plan1[UP[half]]
                        with dve.Fori(0, 4) as i:
                            t = Turn(i, dn=2, du=4, dt=4)
                            for b in plan1[first.n:first.n + 2]:
                                j = b.n - first.n
                                for m in range(2):
                                    dve.wait_ge(S["g_free"], t.t(b.t0 + m + 1))
                                    dve.tensor_tensor(tt[:, 2 * j + m, :], tt[:, 2 * j + m, :], tt[:, 2 * j + m, :],
                                                      ALU.mult).then_inc(S["f_sq"], 1)
                                for m in range(2):
                                    at_tile = i * 4 + (2 * j + m)
                                    dve.wait_ge(S["f_hi_s"], 16 * half + i * 4 + (2 * j + m + 1))
                                    dve.tensor_tensor(f_lo[:, at_tile, :], tt[:, 2 * j + m, :],
                                                      f_hi[:, at_tile, :].bitcast(F32),
                                                      ALU.subtract).then_inc(S["f_ready"], 1)
                                rest_block(dve, plan1, b.n + 2, t)

                        if half == 0:
                            with dve.Fori(0, 2) as i:
                                for b in plan1[DOWN[0]:DOWN[0] + 4]:
                                    rest_block(dve, plan1, b.n + 2, Turn(i, dn=4, du=8, dt=4))
                        else:
                            for i in range(2):
                                t = Turn(i, dn=4, du=8, dt=4)
                                for b in plan1[DOWN[1]:DOWN[1] + 4]:
                                    rest_block(dve, plan1, b.n + 2, t)
                                    if b.last:
                                        for m in range(2):
                                            k = i * 4 + (b.n - DOWN[1]) // 2 * 2 + m
                                            dve.wait_ge(S["g_free"], t.t(b.t0 + m + 1))
                                            dve.tensor_tensor(out_sb[:, k, :], out_sb[:, k, :], part[:, k, :],
                                                              ALU.add).then_inc(S["part_done"], 1)
                    post_norm_dve(dve, 3, gains["mlp_post"], KD)

            for s in S.values():
                nc.gpsimd.sem_clear(s)
            nc.all_engine_barrier()

        g_hi = at("g_hi", [P, F2T, SEQ], F32R, FZ)
        g_lo = at("g_lo", [P, F2T, SEQ], F32R, FZ + 44)
        swi = at("swi", [P, 8, SEQ], F32, OZ)
        mk = at("mk", [P, XH, MEM], F32, FZ)
        mv = at("mv", [P, MEMT, SSM_W], F32, FZ + 4)
        u_sb = at("u_sb", [P, 4, SEQ], F32, FZ + 8)
        xq = at("xq", [P, XH, SEQ], F32, FZ + 16)
        q2 = at("q2", [P, 6, SEQ], F32, FZ + 24)
        k2 = at("k2", [P, 6, SEQ], F32, FZ + 36)
        v2 = at("v2", [P, TOKT, A2], F32, FZ + 48)
        mem_sb = at("mem_sb", [P, KD, MEM], F32, FZ + 60)
        mem_t = at("mem_t", [P, KD, MEM], F32, FZ + 68)
        m_hi = at("m_hi", [P, KD, MEM], F32R, 64)
        m_lo = at("m_lo", [P, KD, MEM], F32R, 80)
        bc = at("bc", [P, 4, STILES * SSM_G], F32, FZ + 60)
        bbar = at("bbar", [P, 4, STILES * SSM_G], F32, FZ + 64)
        b_mat = at("b_mat", [P, 4, 2, P], F32, FZ + 68)
        c_mat = at("c_mat", [P, 4, 2, P], F32, FZ + 72)
        b_turned = at("b_turned", [P, 2, 2 * P], F32, FZ + 76)
        time_t = at("time_t", [P, SEQ], F32, FZ + 78)
        trig = at("trig", [P, 2, 2, SEQ], F32, FZ + 80)
        phase = at("phase", [P, 2, SEQ], F32, FZ + 88)
        z_sc = at("z_sc", [P, 2, 2, SEQ], F32, FZ + 92)
        tmp2 = at("tmp2", [P, 2, SEQ], F32, FZ + 100)
        x_kept = nc.dram_tensor("x_kept", [P, KD, SEQ], F32, kind="Internal").ap()
        state = at("state", [P, 2, 2, SEQ], F32, 48)
        z_sin = at("z_sin", [P, 2, 2, SEQ], F32, 56)
        sp_ = at("state_par", [P, 24, STILES], F32, CZ + 5.5)
        t5a = at("t5a", [P, SLOTS, MEM], F32, FZ + 60)
        t5b = at("t5b", [P, 2, SLOTS, P], F32, FZ + 64)
        row2 = at("row2", [P, 2, MEM], F32, FZ + 69)
        row2_t = at("row2_t", [P, 2, MEM], F32, FZ + 71)
        peak = at("peak", [P, 80], F32, FZ + 73)
        pv = at("pv", [P, PATTERNS, SEQ], F32, FZ + 74)
        mb = at("mb", [P, PATTERNS, SEQ], F32, FZ + 80)
        low = at("low", [P, SEQ], F32, FZ + 86)
        rden = at("rden", [P, SEQ], F32, FZ + 88)
        ya = at("ya", [P, 2, SEQ], F32, FZ + 90)
        yx = at("yx", [P, XH, SEQ], F32, FZ + 94)
        ys_hi = at("ys_hi", [P, 4, SEQ], F32R, FZ + 24)
        ys_lo = at("ys_lo", [P, 4, SEQ], F32R, FZ + 32)
        yx_hi = at("yx_hi", [P, 4, SEQ], F32R, FZ + 40)
        yx_lo = at("yx_lo", [P, 4, SEQ], F32R, FZ + 48)
        ya_hi = at("ya_hi", [P, 2, SEQ], F32R, FZ + 56)
        ya_lo = at("ya_lo", [P, 2, SEQ], F32R, FZ + 60)
        mg_hi = at("mg_hi", [P, KD, SEQ], F32R, FZ + 64)
        mg_lo = at("mg_lo", [P, KD, SEQ], F32R, FZ + 80)
        gate_a = at("gate_a", [P, 12, SEQ], F32, FZ)
        gate_b = at("gate_b", [P, 2, SEQ], F32, FZ + 96)

        def gate_tile(j, m):
            return gate_a[:, 2 * j + m, :] if j < 6 else gate_b[:, m, :]

        gains2 = {n: par2[:, 8 * i:8 * i + 8] for i, n in enumerate(("ffn1", "mem", "mix", "ffn2", "final"))}
        a_re, a_im, log_dt = (par2[:, 40 + 16 * i:56 + 16 * i] for i in range(3))
        ssm_d = par2[:, 88:92]
        names2 = ["par2_in", "mem_in", "bc_in", "time_in", "mat_zero", "mats", "turns_a", "turns_s", "fract", "fract_low", "phased",
                  "trig_s", "rotated", "summed", "scanned", "z_sin_s", "z_cos_s", "real_s", "x_kept_s", "x_back", "coef_a",
                  "coef_t", "bbar_s", "turned_b", "bt_s", "bu_ps", "bu_read", "state_s", "y_ps", "y_read", "y_s", "gelu_s",
                  "t5_in", "s2_ps", "s2_bias", "s2_max", "s2_exp", "s2_prob", "s2_turn_ps", "s2_turn", "s2_mix", "s2_out",
                  "mb_ps", "low_s", "weigh", "ya_s", "yx_s", "split2", "rest2", "prod2", "merged", "mg_hi_s", "mg_s",
                  "x2_done", "g2", "g2_hi", "g2_s", "final_s", "stored"]
        S.update({n: sem(n) for n in names2})
        n_up, n_down = F2T, F2T - 2

        first_q = AT2["q"]
        n_proj = AT2["gates"] - first_q
        slot_at = {}
        for s in range(STILES):
            slot_at[divmod(s * 2 * n_proj // STILES, 2)] = s

        def slot_of(b, m):
            half, left = divmod(m + 1, b.tiles // 2)
            return slot_at.get((b.n - first_q, half - 1)) if left == 0 else None

        def residues(g, i):
            if g == 0:
                return lambda a: a[:, i * P:(i + 1) * P]
            return lambda a: a.rearrange("p (m r) -> p r m", r=4)[:, i, :]

        steps2 = [(h, g, i) for h in range(SLOTS) for g in range(PATTERNS) for i in range(TOKT)]
        N2 = len(steps2)
        xsteps = [(h, i) for h in range(XH) for i in range(TOKT)]
        NX = len(xsteps)

        def keys_of(s):
            h, g, i = steps2[s]
            return (P * (i - 1), 2 * P) if g == 0 and i else (P * i, P)

        def bias_of(s):
            h, g, i = steps2[s]
            if g == 0:
                return t5a[:, h, :] if i else t5a[:, h, P:2 * P]
            return t5b[:, g - 1, h, :]

        with nc.Block() as block:
            @block.sync
            def _(sp):
                src = A["w2"]
                sp.dma_start(par2[:, 0:92], A["par2"]).then_inc(S["par2_in"], 16)

                def load_loop(start, turns, body):
                    with sp.Fori(0, turns) as i:
                        for b in plan2[start:start + body]:
                            load_block(sp, src, b, Turn(i, dn=body))

                load_block(sp, src, plan2[0])
                load_block(sp, src, plan2[1])
                load_loop(2, 10, 2)
                load_loop(AT2["ffn1_down"], 4, 4)
                load_block(sp, src, plan2[AT2["mk"]])
                load_block(sp, src, plan2[AT2["mk"] + 1])
                sp.wait_ge(S["units"], plan2[AT2["mk"] - 1].u1)
                sp.dma_start(mem_sb[:], A["mem"].rearrange("(k p) t -> p k t", p=P)).then_inc(S["mem_in"], 16)
                for b in plan2[AT2["mv"]:AT2["u"]]:
                    load_block(sp, src, b)
                sp.wait_ge(S["h_ready"], 2 * KD)
                sp.dma_start(bc[:], A["ssm_bc"]).then_inc(S["bc_in"], 16)
                sp.dma_start(time_t[:], A["c_time"]).then_inc(S["time_in"], 16)
                for b in plan2[AT2["u"]:AT2["u"] + 2]:
                    load_block(sp, src, b)
                sp.wait_ge(S["x2_done"], KD)
                sp.dma_start(x_kept, x_sb[:]).then_inc(S["x_kept_s"], 16)
                for b in plan2[AT2["q"]:AT2["gates"]]:
                    load_block(sp, src, b)
                load_block(sp, src, plan2[AT2["gates"]])
                load_block(sp, src, plan2[AT2["gates"] + 1])
                sp.wait_ge(S["y_s"], 4)
                sp.dma_start(t5a[:], skewed(t5_rep[0], ROW, MEM)).then_inc(S["t5_in"], 16)
                for g in (1, 2):
                    sp.dma_start(t5b[:, g - 1], skewed(t5_rep[g], ROW, P)).then_inc(S["t5_in"], 16)
                sp.wait_ge(S["x_kept_s"], 16)
                sp.dma_start(x_sb[:], x_kept).then_inc(S["x_back"], 16)
                load_loop_start = AT2["gates"] + 2
                for b in plan2[load_loop_start:AT2["ffn2_up"]]:
                    load_block(sp, src, b)
                load_loop(AT2["ffn2_up"], 11, 2)
                load_loop(AT2["ffn2_down"], 4, 4)
                sp.wait_ge(S["final_s"], KD)
                sp.dma_start(outs[0].rearrange("(k p) t -> p k t", p=P), out_sb[:]).then_inc(S["stored"], 16)
                sp.wait_ge(S["stored"], 16)

            @block.gpsimd
            def _(pool):
                pool.wait_ge(S["h_ready"], 2 * KD)
                pool.memset(b_mat[:], 0.0).then_inc(S["mat_zero"], 1)
                pool.memset(c_mat[:], 0.0).then_inc(S["mat_zero"], 1)
                pool.wait_ge(S["mat_zero"], 2)
                pool.wait_ge(S["bbar_s"], 3)
                def mats(s):
                    b = s % 4
                    if s >= 4:
                        pool.wait_ge(S["turned_b"], s - 3)
                        pool.wait_ge(S["y_ps"], s - 3)
                    for q in range(2):
                        r = slice(SSM_N * q, SSM_N * q + SSM_N)
                        c = slice(32 * b + 16 * q, 32 * b + 16 * q + 16)
                        f = slice(SSM_G * s, SSM_G * s + SSM_G)
                        for j in range(2):
                            pool.tensor_copy(b_mat[r, b, j, c], bbar[r, j, f]).then_inc(S["mats"], 1)
                            pool.tensor_copy(c_mat[r, b, j, c], (bc[r, 2, f], bbar[r, 3, f])[j]).then_inc(S["mats"], 1)

                def whole_turns(s):
                    if s >= 2:
                        pool.wait_ge(S["fract"], s - 1)
                    to = phase[:, s % 2, :]
                    pool.tensor_scalar(to, time_t[:], sp_[:, 9, s:s + 1], MAGIC, ALU.mult,
                                       ALU.add).then_inc(S["turns_a"], 1)
                    pool.wait_ge(S["turns_a"], s + 1)
                    pool.tensor_scalar(to, to, MAGIC, None, ALU.subtract).then_inc(S["turns_s"], 1)

                def sines(s):
                    pool.wait_ge(S["scanned"], 2 * s + 2)
                    if s >= 2:
                        pool.wait_ge(S["state_s"], s - 1)
                    for w in range(2):
                        pool.tensor_tensor(z_sin[:, s % 2, w, :], z_sc[:, s % 2, 1 - w, :], trig[:, s % 2, 1, :],
                                           ALU.mult).then_inc(S["z_sin_s"], 1)

                pool.wait_ge(S["time_in"], 16)
                for s in range(2):
                    whole_turns(s)
                    pool.wait_ge(S["turns_s"], s + 1)
                    mats(s)
                    pool.wait_ge(S["mats"], 8 * (s + 1))
                pool.wait_ge(S["x_kept_s"], 16)
                pool.wait_ge(S["normed"], 3 * KD)
                for s in range(STILES):
                    if s + 2 < STILES:
                        mats(s + 2)
                        pool.wait_ge(S["mats"], 8 * (s + 3))
                    sines(s)
                    if s + 2 < STILES:
                        whole_turns(s + 2)
                        pool.wait_ge(S["z_sin_s"], 2 * s + 2)
                        pool.wait_ge(S["turns_s"], s + 3)

            @block.tensor
            def _(pe):
                def ffn(name, g_base, ready):
                    pe.wait_ge(S["h_ready"], ready)
                    up, down = AT2[name + "_up"], AT2[name + "_down"]
                    if up == 0:
                        for b in plan2[0:2]:
                            product(pe, b, h_hi, h_lo)
                        with pe.Fori(0, 10) as i:
                            for b in plan2[2:4]:
                                product(pe, b, h_hi, h_lo, Turn(i, dn=2, du=4, dt=4))
                    else:
                        with pe.Fori(0, 11) as i:
                            for b in plan2[up:up + 2]:
                                product(pe, b, h_hi, h_lo, Turn(i, dn=2, du=4, dt=4))
                    pe.wait_ge(S["g2_s"], g_base + F2T + 2)
                    with pe.Fori(0, 2) as i:
                        for b in plan2[down:down + 8]:
                            product(pe, b, g_hi, g_lo, Turn(i, dn=8, du=16, dt=4))

                norm_total(pe, 0, out_sb)
                ffn("ffn1", 0, KD)
                norm_total(pe, 1, mem_t, MEM)
                for b in plan2[AT2["mk"]:AT2["u"]]:
                    product(pe, b, m_hi, m_lo, ready=KD if b.n == AT2["mk"] else None, width=MEM)
                norm_total(pe, 2, out_sb)
                for b in plan2[AT2["u"]:AT2["q"]]:
                    product(pe, b, h_hi, h_lo, ready=2 * KD if b.n == AT2["u"] else None)

                def turn_b(s):
                    pe.wait_ge(S["mats"], 8 * (s + 1))
                    if s:
                        pe.wait_ge(S["bt_s"], s)
                    for j in range(2):
                        mm = pe.transpose(t_ps[:, P * j:P * j + P], b_mat[:, s % 4, j, :], ident[:])
                    mm.then_inc(S["turned_b"], 1)

                def scan_in(s):
                    pe.wait_ge(S["bt_s"], s + 1)
                    if s:
                        pe.wait_ge(S["bu_read"], s)
                    for j in range(2):
                        mm = pe.matmul(s_ps[j][:], b_turned[:, s % 2, P * j:P * j + P], u_sb[:, s // 4, :],
                                       start=True, stop=True)
                    mm.then_inc(S["bu_ps"], 1)

                def scan_out(s):
                    pe.wait_ge(S["real_s"], s + 1)
                    pe.wait_ge(S["state_s"], s + 1)
                    if s % 4 == 0:
                        pe.wait_ge(S["y_read"], s // 4) if s else pe.wait_ge(S["norm_root"], 3)
                    for j in range(2):
                        mm = pe.matmul(o_ps[:], c_mat[:, s % 4, j, :], state[:, s % 2, j, :],
                                       start=s % 4 == 0 and j == 0, stop=s % 4 == 3 and j == 1)
                    mm.then_inc(S["y_ps"], 1)

                turn_b(0)
                pe.wait_ge(S["g_free"], plan2[AT2["q"]].t0)
                for b in plan2[AT2["q"]:AT2["gates"]]:
                    def between(m):
                        s = slot_of(b, m)
                        if s is not None:
                            scan_in(s)
                            if s >= 2:
                                scan_out(s - 2)
                            if s + 1 < STILES:
                                turn_b(s + 1)

                    g = b.n - AT2["v"]
                    product(pe, b, h_hi, h_lo, tokens=(lambda m: residues(g, m)) if b.kind == "tok" else None,
                            between=between)
                for s in (STILES - 2, STILES - 1):
                    scan_out(s)

                pe.wait_ge(S["g_free"], plan2[AT2["gates"]].t0)
                pe.wait_ge(S["bu_read"], STILES)

                def scores2(s):
                    h, g, i = steps2[s]
                    t, r = 2 * g + h // 2, slice(HD * (h % 2), HD * (h % 2) + HD)
                    k0, size = keys_of(s)
                    if s >= 2:
                        pe.wait_ge(S["s2_bias"], s - 1)
                    pe.matmul(s_ps[s % 2][:, 0:size], q2[r, t, P * i:P * i + P], k2[r, t, k0:k0 + size],
                              start=True, stop=True).then_inc(S["s2_ps"], 1)

                def turn2(s):
                    size = keys_of(s)[1]
                    pe.wait_ge(S["s2_exp"], s + 1)
                    if s:
                        pe.wait_ge(S["s2_turn"], s)
                    for j in range(size // P):
                        mm = pe.transpose(t_ps[:, P * j:P * j + P], row2[:, s % 2, P * j:P * j + P], ident[:])
                    mm.then_inc(S["s2_turn_ps"], 1)

                def mix2(s):
                    h, g, i = steps2[s]
                    k0, size = keys_of(s)
                    hg = s // TOKT
                    pe.wait_ge(S["s2_turn"], s + 1)
                    if i == 0 and hg >= 2:
                        pe.wait_ge(S["s2_out"], 2 * (hg - 1))
                    c = slice(P * i, P * i + P)
                    v_cols = slice(2 * P * g + HD * h, 2 * P * g + HD * h + HD)
                    for j in range(size // P):
                        last = j == size // P - 1
                        kt = k0 // P + j
                        pe.matmul(bank[hg % 2][0:HD, c], v2[:, kt, v_cols], row2_t[:, s % 2, P * j:P * j + P],
                                  start=j == 0, stop=last)
                        pe.matmul(bank[hg % 2][HD:P, c], ones[:, 0:HD], row2_t[:, s % 2, P * j:P * j + P],
                                  start=j == 0, stop=last)
                    pe.matmul(bank[2 + hg % 2][:, c], peak[:, s:s + 1].broadcast_to([P, P]), ident[:],
                              start=True, stop=True).then_inc(S["s2_mix"], 1)

                for s in range(N2 + 2):
                    if s < N2:
                        scores2(s)
                    if 1 <= s <= N2:
                        turn2(s - 1)
                    if s >= 2:
                        mix2(s - 2)

                def scores_x(s):
                    h, i = xsteps[s]
                    n = N2 + s
                    pe.wait_ge(S["s2_bias"], n - 1)
                    pe.matmul(s_ps[n % 2][:, 0:MEM], xq[:, h, P * i:P * i + P], mk[:, h, :],
                              start=True, stop=True).then_inc(S["s2_ps"], 1)

                def turn_x(s):
                    n = N2 + s
                    pe.wait_ge(S["s2_prob"], s + 1)
                    pe.wait_ge(S["s2_turn"], n)
                    for j in range(MEMT):
                        mm = pe.transpose(t_ps[:, P * j:P * j + P], row2[:, n % 2, P * j:P * j + P], ident[:])
                    mm.then_inc(S["s2_turn_ps"], 1)

                def mix_x(s):
                    h, i = xsteps[s]
                    n = N2 + s
                    pe.wait_ge(S["s2_turn"], n + 1)
                    if i == 0 and h:
                        pe.wait_ge(S["yx_s"], h)
                    for j in range(MEMT):
                        mm = pe.matmul(o_ps[:, P * i:P * i + P], mv[:, j, P * h:P * h + P],
                                       row2_t[:, n % 2, P * j:P * j + P], start=j == 0, stop=j == MEMT - 1)
                    mm.then_inc(S["s2_mix"], 1)

                pe.wait_ge(S["y_read"], 4)
                for s in range(NX + 2):
                    if s < NX:
                        scores_x(s)
                    if 1 <= s <= NX:
                        turn_x(s - 1)
                    if s >= 2:
                        mix_x(s - 2)

                pe.wait_ge(S["s2_out"], 2 * SLOTS * PATTERNS)
                pe.wait_ge(S["rest2"], 10)
                sources = {"glu_b": (ys_hi, ys_lo), "glu_a": (ys_hi, ys_lo), "attn_up": (ya_hi, ya_lo),
                           "xattn_up": (yx_hi, yx_lo)}
                for b in plan2[AT2["gates"]:AT2["w_out2"]]:
                    hi, lo = sources.get(GATES[(b.n - AT2["gates"]) % 7], (h_hi, h_lo))
                    product(pe, b, hi, lo)
                pe.wait_ge(S["mg_s"], KD)
                for b in plan2[AT2["w_out2"]:AT2["ffn2_up"]]:
                    product(pe, b, mg_hi, mg_lo)
                norm_total(pe, 3, out_sb)
                ffn("ffn2", F2T + 2, 4 * KD)
                norm_total(pe, 4, out_sb)

            @block.scalar
            def _(act):
                def evacuate(b, dst, func=ACT.Copy, scale=1.0, width=SEQ, m0=0):
                    for m in range(b.tiles):
                        act.wait_ge(S["units"], b.u0 + (m + 1 if b.kind == "feat" else m // 2 * 2 + 2))
                        act.activation(dst(m), tile_of(b, m, width), func, scale=scale).then_inc(S["g_free"], 1)

                def ffn(name, g_base):
                    up, down = AT2[name + "_up"], AT2[name + "_down"]
                    s_base = 0 if name == "ffn1" else F2T + 2
                    with act.Fori(0, 11) as i:
                        t = Turn(i, dn=2, du=4, dt=4)
                        for b in plan2[up:up + 2]:
                            j = b.n - up
                            if j == 0:
                                act.wait_ge(S["g2_s"], s_base + 2 + i * 2)
                            for m in range(2):
                                act.wait_ge(S["units"], t.u(b.u0 + m + 1))
                                act.activation(swi[:, 2 * j + m, :], tile_of(b, m),
                                               (ACT.Silu, ACT.Copy)[j]).then_inc(S["g_free"], 1)
                            if j:
                                for m in range(2):
                                    act.wait_ge(S["g2"], g_base + i * 2 + (m + 1))
                                    act.activation(g_hi[:, i * 2 + m, :], swi[:, m, :],
                                                   ACT.Copy).then_inc(S["g2_hi"], 1)
                            round_block(act, plan2, b.n + 2, t)

                    def down_pair(i):
                        for q in range(2):
                            for b in plan2[down + 4 * q:down + 4 * q + 4]:
                                t = Turn(i, dn=8, du=16, dt=4)
                                if b.last:
                                    for m in range(2):
                                        act.wait_ge(S["units"], t.u(b.u0 + m + 1))
                                        act.activation(part[:, i * 4 + (2 * q + m), :], tile_of(b, m), ACT.Copy,
                                                       scale=0.5).then_inc(S["g_free"], 1)
                                round_block(act, plan2, b.n + 2, t, whole=b.n + 2 >= down + 8)

                    if name == "ffn1":
                        with act.Fori(0, 2) as i:
                            down_pair(i)
                    else:
                        for i in range(2):
                            down_pair(i)

                norm_squares(act, 0, x_sb, out_sb)
                round_block(act, plan2, 0)
                round_block(act, plan2, 1)
                norm_rooted(act, 0)
                split_hi(act, 0, 0, out_sb, S["normed"], 0)
                ffn("ffn1", 0)
                act.wait_ge(S["mem_in"], 16)
                norm_squares(act, 1, mem_sb, mem_t)
                norm_rooted(act, 1, MEM)
                split_hi(act, 1, 1, mem_t, S["normed"], KD, hi=m_hi)
                for b in plan2[AT2["mk"]:AT2["u"]]:
                    if b.kind == "feat":
                        evacuate(b, lambda m: mk[:, 2 * (b.n - AT2["mk"]) + m, :], width=MEM)
                    else:
                        evacuate(b, lambda m: mv[:, m, 256 * (b.n - AT2["mv"]):256 * (b.n - AT2["mv"]) + 256])
                    round_block(act, plan2, b.n + 2)
                norm_squares(act, 2, x_sb, out_sb, wait=(S["x2_done"], 0))
                norm_rooted(act, 2)
                act.wait_ge(S["units"], plan2[AT2["u"] - 1].u1)
                split_hi(act, 2, 2, out_sb, S["normed"], 2 * KD)

                act.wait_ge(S["par2_in"], 16)
                act.activation(sp_[:, 0, :], log_dt, ACT.Exp).then_inc(S["coef_a"], 1)
                act.wait_ge(S["coef_t"], 1)
                act.activation(sp_[:, 2, :], sp_[:, 1, :], ACT.Exp).then_inc(S["coef_a"], 1)
                act.wait_ge(S["coef_t"], 2)
                act.activation(sp_[:, 5, :], sp_[:, 4, :], ACT.Abs).then_inc(S["coef_a"], 1)
                act.wait_ge(S["coef_a"], 3)
                act.activation(sp_[:, 6, :], sp_[:, 4, :], ACT.Sin).then_inc(S["coef_a"], 1)
                act.activation(sp_[:, 7, :], sp_[:, 5, :], ACT.Sin, scale=-1.0,
                               bias=quarter[:, 0:1]).then_inc(S["coef_a"], 1)
                for b in plan2[AT2["u"]:AT2["q"]]:
                    evacuate(b, lambda m: u_sb[:, 2 * (b.n - AT2["u"]) + m, :])
                    round_block(act, plan2, b.n + 2)

                def waves(s):
                    act.wait_ge(S["phased"], s + 1)
                    if s >= 2:
                        act.wait_ge(S["z_cos_s"], 2 * s - 2)
                    cos, sin = trig[:, s % 2, 0, :], trig[:, s % 2, 1, :]
                    act.activation(cos, sin, ACT.Abs).then_inc(S["trig_s"], 1)
                    act.wait_ge(S["trig_s"], 3 * s + 1)
                    act.activation(sin, sin, ACT.Sin, scale=BELOW_2PI).then_inc(S["trig_s"], 1)
                    act.activation(cos, cos, ACT.Sin, scale=-BELOW_2PI, bias=quarter[:, 0:1]).then_inc(S["trig_s"], 1)

                def copy_b(s):
                    act.wait_ge(S["turned_b"], s + 1)
                    if s >= 2:
                        act.wait_ge(S["bu_ps"], s - 1)
                    act.activation(b_turned[:, s % 2, :], t_ps[:, 0:2 * P], ACT.Copy).then_inc(S["bt_s"], 1)

                copy_b(0)
                waves(0)
                due = None
                for b in plan2[AT2["q"]:AT2["gates"]]:
                    for m in range(b.tiles):
                        if due is not None and (m + 1) % (b.tiles // 2) == 0:
                            waves(due)
                            due = None
                        act.wait_ge(S["units"], b.u0 + (m + 1 if b.kind == "feat" else m // 2 * 2 + 2))
                        src = tile_of(b, m)
                        if b.n < AT2["v"]:
                            to, t = (q2, 2 * (b.n - AT2["q"]) + m) if b.n < AT2["k"] else (k2, 2 * (b.n - AT2["k"]) + m)
                            r = (1, 4, 4)[t // 2]
                            dst = to[:, t, :].rearrange("p (r m) -> p m r", r=r) if r > 1 else to[:, t, :]
                            src = src.rearrange("p (m r) -> p m r", r=r) if r > 1 else src
                        elif b.n < AT2["xq"]:
                            dst = v2[:, m, 256 * (b.n - AT2["v"]):256 * (b.n - AT2["v"]) + 256]
                        else:
                            dst = xq[:, 2 * (b.n - AT2["xq"]) + m, :]
                        act.activation(dst, src, ACT.Copy).then_inc(S["g_free"], 1)
                        s = slot_of(b, m)
                        if s is not None and s + 1 < STILES:
                            copy_b(s + 1)
                            due = s + 1
                    round_block(act, plan2, b.n + 2)
                for a in range(4):
                    act.wait_ge(S["y_s"], a + 1)
                    act.activation(u_sb[:, a, :], u_sb[:, a, :], ACT.Gelu_apprx_tanh).then_inc(S["gelu_s"], 1)

                def copy_turned(n, size):
                    act.wait_ge(S["s2_turn_ps"], n + 1)
                    if n >= 2:
                        act.wait_ge(S["s2_mix"], n - 1)
                    act.activation(row2_t[:, n % 2, 0:size], t_ps[:, 0:size], ACT.Copy).then_inc(S["s2_turn"], 1)

                def copy_mixed(hg):
                    g = hg % PATTERNS
                    act.wait_ge(S["s2_mix"], TOKT * (hg + 1))
                    if hg >= PATTERNS:
                        act.wait_ge(S["ya_s"], hg // PATTERNS)
                    r = (1, 4, 4)[g]
                    for dst, src in ((pv, bank[hg % 2]), (mb, bank[2 + hg % 2])):
                        d, s_ = dst[:, g, :], src[:]
                        if r > 1:
                            d, s_ = d.rearrange("p (m r) -> p m r", r=r), s_.rearrange("p (r m) -> p m r", r=r)
                        act.activation(d, s_, ACT.Copy).then_inc(S["s2_out"], 1)

                def weights_of(h):
                    for g in range(PATTERNS):
                        act.wait_ge(S["low_s"], PATTERNS * h + g + 1)
                        act.activation(mb[:, g, :], mb[:, g, :], ACT.Exp).then_inc(S["weigh"], 1)

                for s in range(N2 + 2):
                    if s < N2:
                        size = keys_of(s)[1]
                        act.wait_ge(S["s2_max"], s + 1)
                        act.activation(row2[:, s % 2, 0:size], row2[:, s % 2, 0:size], ACT.Exp,
                                       bias=peak[:, s:s + 1]).then_inc(S["s2_exp"], 1)
                    if 1 <= s <= N2:
                        copy_turned(s - 1, keys_of(s - 1)[1])
                    if s >= 2 and (s - 1) % TOKT == 0:
                        hg = (s - 1) // TOKT - 1
                        copy_mixed(hg)
                        if hg % PATTERNS == PATTERNS - 1:
                            weights_of(hg // PATTERNS)
                for s in range(NX + 2):
                    if s < NX:
                        n = N2 + s
                        act.wait_ge(S["s2_max"], n + 1)
                        act.activation(row2[:, n % 2, :], s_ps[n % 2][:, 0:MEM], ACT.Exp, scale=P ** -0.5,
                                       bias=peak[:, N2 + s:N2 + s + 1],
                                       accum_out=peak[:, 64 + s % 2:65 + s % 2]).then_inc(S["s2_exp"], 1)
                    if 1 <= s <= NX:
                        copy_turned(N2 + s - 1, MEM)
                    if s >= 2 and (s - 1) % TOKT == 0:
                        h = (s - 1) // TOKT - 1
                        act.wait_ge(S["s2_mix"], N2 + TOKT * (h + 1))
                        act.activation(yx[:, h, :], o_ps[:], ACT.Copy).then_inc(S["yx_s"], 1)

                act.wait_ge(S["ya_s"], SLOTS)
                act.wait_ge(S["yx_s"], XH)
                act.wait_ge(S["gelu_s"], 4)
                for src, dst, tiles in ((u_sb, ys_hi, 4), (yx, yx_hi, 4), (ya, ya_hi, 2)):
                    for k in range(tiles):
                        act.activation(dst[:, k, :], src[:, k, :], ACT.Copy).then_inc(S["split2"], 1)
                act.wait_ge(S["rest2"], 10)
                for b in plan2[AT2["gates"]:AT2["w_out2"]]:
                    p, j = divmod(b.n - AT2["gates"], 7)
                    func = ACT.Sigmoid if GATES[j] in ("glu_b", "gate0", "gate1", "gate2") else ACT.Copy
                    evacuate(b, lambda m: gate_tile(j, m), func)
                    if j == 6:
                        for m in range(2):
                            act.wait_ge(S["merged"], 2 * p + m + 1)
                            act.activation(mg_hi[:, 2 * p + m, :], gate_tile(1, m), ACT.Copy).then_inc(S["mg_hi_s"], 1)
                    round_block(act, plan2, b.n + 2)
                for b in plan2[AT2["w_out2"]:AT2["ffn2_up"]]:
                    evacuate(b, lambda m: part[:, 2 * (b.n - AT2["w_out2"]) + m, :])
                    round_block(act, plan2, b.n + 2)
                norm_squares(act, 3, x_sb, out_sb, wait=(S["x2_done"], KD))
                norm_rooted(act, 3)
                split_hi(act, 3, 3, out_sb, S["normed"], 3 * KD)
                ffn("ffn2", F2T)
                norm_squares(act, 4, x_sb, out_sb, wait=(S["x2_done"], 2 * KD))
                norm_rooted(act, 4)

            @block.vector
            def _(dve):
                own = [0]

                def step(instruction):
                    own[0] += 1
                    instruction.then_inc(S["dve_own"], 1)
                    dve.wait_ge(S["dve_own"], own[0])

                def add_part(k):
                    dve.tensor_tensor(x_sb[:, k, :], x_sb[:, k, :], part[:, k, :], ALU.add).then_inc(S["x2_done"], 1)

                def ffn(name, g_base):
                    up, down = AT2[name + "_up"], AT2[name + "_down"]
                    dve.sem_inc(S["g2_s"], 2)
                    with dve.Fori(0, 11) as i:
                        t = Turn(i, dn=2, du=4, dt=4)
                        for b in plan2[up:up + 2]:
                            if b.n > up:
                                for m in range(2):
                                    dve.wait_ge(S["g_free"], t.t(b.t0 + m + 1))
                                    dve.tensor_tensor(swi[:, m, :], swi[:, m, :], swi[:, 2 + m, :],
                                                      ALU.mult).then_inc(S["g2"], 1)
                                for m in range(2):
                                    dve.wait_ge(S["g2_hi"], g_base + i * 2 + (m + 1))
                                    dve.tensor_tensor(g_lo[:, i * 2 + m, :], swi[:, m, :],
                                                      g_hi[:, i * 2 + m, :].bitcast(F32),
                                                      ALU.subtract).then_inc(S["g2_s"], 1)
                            rest_block(dve, plan2, b.n + 2, t)

                    def down_pair(i):
                        for q in range(2):
                            for b in plan2[down + 4 * q:down + 4 * q + 4]:
                                t = Turn(i, dn=8, du=16, dt=4)
                                rest_block(dve, plan2, b.n + 2, t, whole=b.n + 2 >= down + 8)
                                if b.last:
                                    for m in range(2):
                                        k = i * 4 + (2 * q + m)
                                        dve.wait_ge(S["g_free"], t.t(b.t0 + m + 1))
                                        add_part(k)

                    if name == "ffn1":
                        with dve.Fori(0, 2) as i:
                            down_pair(i)
                    else:
                        for i in range(2):
                            down_pair(i)

                rest_block(dve, plan2, 0)
                rest_block(dve, plan2, 1)
                dve.wait_ge(S["par2_in"], 16)
                pre_norm_dve(dve, 0, 0, gains2["ffn1"])
                ffn("ffn1", 0)
                pre_norm_dve(dve, 1, 1, gains2["mem"], MEM, mem_sb, mem_t, m_hi, m_lo)
                for b in plan2[AT2["mk"]:AT2["u"]]:
                    rest_block(dve, plan2, b.n + 2)
                pre_norm_dve(dve, 2, 2, gains2["mix"])

                row = lambda i: sp_[:, i, :]
                dve.wait_ge(S["coef_a"], 1)
                step(dve.tensor_tensor(row(3), a_im, row(0), ALU.mult))
                dve.tensor_tensor(row(1), a_re, row(0), ALU.mult).then_inc(S["coef_t"], 1)
                step(dve.tensor_scalar(row(8), row(3), 1.0 / TWO_PI, MAGIC, ALU.mult, ALU.add))
                step(dve.tensor_scalar(row(8), row(8), MAGIC, None, ALU.subtract))
                for c in (PI2_A, PI2_B, PI2_C):
                    step(dve.scalar_tensor_tensor(out=row(3), in0=row(8), scalar=-c, in1=row(3), op0=ALU.mult,
                                                  op1=ALU.add))
                dve.tensor_scalar(row(4), row(3), BELOW_PI, -BELOW_PI, ALU.min, ALU.max).then_inc(S["coef_t"], 1)
                step(dve.tensor_scalar(row(9), row(3), 1.0 / TWO_PI, None, ALU.mult))
                step(dve.tensor_scalar(row(10), row(9), MAGIC / 2 ** 14, None, ALU.add))
                step(dve.tensor_scalar(row(10), row(10), MAGIC / 2 ** 14, None, ALU.subtract))
                step(dve.tensor_tensor(row(11), row(9), row(10), ALU.subtract))
                dve.wait_ge(S["coef_a"], 5)
                step(dve.tensor_tensor(row(12), row(2), row(7), ALU.mult))
                step(dve.tensor_scalar(row(12), row(12), 1.0, None, ALU.subtract))
                step(dve.tensor_tensor(row(13), row(2), row(6), ALU.mult))
                step(dve.tensor_tensor(row(14), a_re, a_re, ALU.mult))
                step(dve.tensor_tensor(row(15), a_im, a_im, ALU.mult))
                step(dve.tensor_tensor(row(14), row(14), row(15), ALU.add))
                step(dve.reciprocal(row(14), row(14)))
                step(dve.tensor_tensor(row(16), row(12), a_re, ALU.mult))
                step(dve.tensor_tensor(row(17), row(13), a_im, ALU.mult))
                step(dve.tensor_tensor(row(16), row(16), row(17), ALU.add))
                step(dve.tensor_tensor(row(18), row(13), a_re, ALU.mult))
                step(dve.tensor_tensor(row(19), row(12), a_im, ALU.mult))
                step(dve.tensor_tensor(row(18), row(18), row(19), ALU.subtract))
                step(dve.tensor_tensor(row(16), row(16), row(14), ALU.mult))
                step(dve.tensor_tensor(row(18), row(18), row(14), ALU.mult))
                dve.wait_ge(S["bc_in"], 16)
                by_state = lambda a: a.rearrange("p (s h) -> p s h", h=SSM_G)
                wide = lambda i: sp_[:, i, :].unsqueeze(2).broadcast_to([P, STILES, SSM_G])
                b_re, b_im = by_state(bc[:, 0, :]), by_state(bc[:, 1, :])
                for out_i, x1, x2, op in ((0, b_re, b_im, ALU.subtract), (1, b_im, b_re, ALU.add)):
                    step(dve.tensor_tensor(by_state(bbar[:, out_i, :]), wide(16), x1, ALU.mult))
                    step(dve.tensor_tensor(by_state(bbar[:, 2, :]), wide(18), x2, ALU.mult))
                    dve.tensor_tensor(bbar[:, out_i, :], bbar[:, out_i, :], bbar[:, 2, :], op).then_inc(S["bbar_s"], 1)
                    dve.wait_ge(S["bbar_s"], out_i + 1)
                dve.tensor_scalar(bbar[:, 3, :], bc[:, 3, :], -1.0, None, ALU.mult).then_inc(S["bbar_s"], 1)
                for b in plan2[AT2["u"]:AT2["q"]]:
                    rest_block(dve, plan2, b.n + 2)

                def phase_step(s, part):
                    if s == STILES:
                        return
                    to = trig[:, s % 2, 1, :]
                    if part == 0:
                        dve.wait_ge(S["turns_s"], s + 1)
                        if s >= 2:
                            dve.wait_ge(S["z_sin_s"], 2 * s - 2)
                        dve.scalar_tensor_tensor(out=to, in0=time_t[:], scalar=sp_[:, 10, s:s + 1],
                                                 in1=phase[:, s % 2, :], op0=ALU.mult,
                                                 op1=ALU.subtract).then_inc(S["fract"], 1)
                    elif part == 1:
                        dve.wait_ge(S["fract"], s + 1)
                        dve.scalar_tensor_tensor(out=to, in0=time_t[:], scalar=sp_[:, 11, s:s + 1], in1=to,
                                                 op0=ALU.mult, op1=ALU.add).then_inc(S["fract_low"], 1)
                    else:
                        dve.wait_ge(S["fract_low"], s + 1)
                        dve.tensor_scalar(to, to, 0.5, -0.5, ALU.min, ALU.max).then_inc(S["phased"], 1)

                def state_sum(s):
                    for w, op, signal in ((0, ALU.subtract, "real_s"), (1, ALU.add, "state_s")):
                        dve.wait_ge(S["z_sin_s"], 2 * s + w + 1)
                        dve.wait_ge(S["z_cos_s"], 2 * s + w + 1)
                        dve.tensor_tensor(state[:, s % 2, w, :], state[:, s % 2, w, :], z_sin[:, s % 2, w, :],
                                          op).then_inc(S[signal], 1)

                def scan(s, rest=None):
                    if s >= 6 and s % 4 == 2:
                        skip(s // 4 - 1)
                    dve.wait_ge(S["trig_s"], 3 * s + 3)
                    dve.wait_ge(S["bu_ps"], s + 1)
                    if s >= 2:
                        dve.wait_ge(S["z_sin_s"], 2 * s - 2)
                        dve.wait_ge(S["z_cos_s"], 2 * s - 2)
                    if s:
                        dve.wait_ge(S["summed"], 2 * s)
                    cos, sin = trig[:, s % 2, 0, :], trig[:, s % 2, 1, :]
                    br, bi = s_ps[0][:], s_ps[1][:]
                    z = [z_sc[:, s % 2, w, :] for w in range(2)]
                    dve.tensor_tensor(z[0], br, cos, ALU.mult).then_inc(S["rotated"], 1)
                    dve.tensor_tensor(z[1], bi, cos, ALU.mult).then_inc(S["rotated"], 1)
                    dve.tensor_tensor(tmp2[:, 0, :], bi, sin, ALU.mult).then_inc(S["rotated"], 1)
                    dve.tensor_tensor(tmp2[:, 1, :], br, sin, ALU.mult).then_inc(S["bu_read"], 1)
                    if s:
                        state_sum(s - 1)
                    phase_step(s + 1, 0)
                    dve.wait_ge(S["rotated"], 3 * s + 3)
                    dve.wait_ge(S["bu_read"], s + 1)
                    dve.tensor_tensor(z[0], z[0], tmp2[:, 0, :], ALU.add).then_inc(S["summed"], 1)
                    dve.tensor_tensor(z[1], z[1], tmp2[:, 1, :], ALU.subtract).then_inc(S["summed"], 1)
                    phase_step(s + 1, 1)
                    decay = sp_[:, 2, s:s + 1].broadcast_to([P, SEQ])
                    for w in range(2):
                        dve.wait_ge(S["summed"], 2 * s + w + 1)
                        dve.tensor_tensor_scan(z[w], decay, z[w], 0.0, ALU.mult, ALU.add).then_inc(S["scanned"], 1)
                        if w == 0:
                            phase_step(s + 1, 2)
                    if rest is not None:
                        rest_block(dve, plan2, rest)
                    if s == 0:
                        dve.wait_ge(S["x_kept_s"], 16)
                    if s >= 2:
                        dve.wait_ge(S["y_ps"], s - 1)
                    for w in range(2):
                        dve.wait_ge(S["scanned"], 2 * s + w + 1)
                        dve.tensor_tensor(state[:, s % 2, w, :], z[w], cos, ALU.mult).then_inc(S["z_cos_s"], 1)

                def skip(a):
                    dve.wait_ge(S["y_ps"], 4 * a + 4)
                    dve.scalar_tensor_tensor(out=u_sb[:, a, :], in0=u_sb[:, a, :], scalar=ssm_d[:, a:a + 1], in1=o_ps[:],
                                             op0=ALU.mult, op1=ALU.add).then_inc(S["y_read"], 1)
                    dve.wait_ge(S["y_read"], a + 1)
                    dve.sem_inc(S["y_s"], 1)

                dve.wait_ge(S["time_in"], 16)
                for part_ in range(3):
                    phase_step(0, part_)
                for b in plan2[AT2["q"]:AT2["gates"]]:
                    for m in range(b.tiles):
                        s, last_tile = slot_of(b, m), m == b.tiles - 1
                        if s is not None:
                            scan(s, rest=b.n + 2 if last_tile else None)
                        elif last_tile:
                            rest_block(dve, plan2, b.n + 2)
                state_sum(STILES - 1)
                skip(3)

                dve.wait_ge(S["t5_in"], 48)

                def combine(h):
                    dve.wait_ge(S["s2_out"], 2 * PATTERNS * (h + 1))
                    step(dve.tensor_tensor(low[:], mb[:, 0, :], mb[:, 1, :], ALU.min))
                    step(dve.tensor_tensor(low[:], low[:], mb[:, 2, :], ALU.min))
                    for g in range(PATTERNS):
                        dve.tensor_tensor(mb[:, g, :], low[:], mb[:, g, :], ALU.subtract).then_inc(S["low_s"], 1)
                    for g in range(PATTERNS):
                        dve.wait_ge(S["weigh"], PATTERNS * h + g + 1)
                        step(dve.tensor_tensor(pv[:, g, :], pv[:, g, :], mb[:, g, :], ALU.mult))
                        if g:
                            step(dve.tensor_tensor(pv[:, 0, :], pv[:, 0, :], pv[:, g, :], ALU.add))
                    step(dve.reciprocal(rden[0:HD, :], pv[HD:P, 0, :]))
                    r = slice(HD * (h % 2), HD * (h % 2) + HD)
                    dve.tensor_tensor(ya[r, h // 2, :], pv[0:HD, 0, :], rden[0:HD, :], ALU.mult).then_inc(S["ya_s"], 1)
                    dve.wait_ge(S["ya_s"], h + 1)

                for s in range(N2 + 1):
                    if s < N2:
                        size = keys_of(s)[1]
                        row_ = row2[:, s % 2, 0:size]
                        dve.wait_ge(S["s2_ps"], s + 1)
                        if s >= 2:
                            dve.wait_ge(S["s2_turn_ps"], s - 1)
                        dve.scalar_tensor_tensor(out=row_, in0=s_ps[s % 2][:, 0:size], scalar=HD ** -0.5,
                                                 in1=bias_of(s), op0=ALU.mult, op1=ALU.add).then_inc(S["s2_bias"], 1)
                        dve.wait_ge(S["s2_bias"], s + 1)
                        dve.tensor_reduce(peak[:, s:s + 1], row_, AX_X, ALU.max, negate=True).then_inc(S["s2_max"], 1)
                    if s >= 3 and (s - 3) % (TOKT * PATTERNS) == TOKT * PATTERNS - 1 and s > 3:
                        combine((s - 3) // (TOKT * PATTERNS))
                combine(SLOTS - 1)

                def x_scaled(s):
                    n = N2 + s
                    dve.wait_ge(S["s2_exp"], n + 1)
                    step(dve.reciprocal(peak[:, 66 + s % 2:67 + s % 2], peak[:, 64 + s % 2:65 + s % 2]))
                    dve.tensor_scalar(row2[:, n % 2, :], row2[:, n % 2, :], peak[:, 66 + s % 2:67 + s % 2], None,
                                      ALU.mult).then_inc(S["s2_prob"], 1)

                for s in range(NX + 1):
                    n = N2 + s
                    if s < NX:
                        dve.wait_ge(S["s2_ps"], n + 1)
                        dve.wait_ge(S["s2_turn_ps"], n - 1)
                        step(dve.tensor_reduce(peak[:, n:n + 1], s_ps[n % 2][:, 0:MEM], AX_X, ALU.max, negate=True))
                        dve.tensor_scalar(peak[:, n:n + 1], peak[:, n:n + 1], P ** -0.5, None,
                                          ALU.mult).then_inc(S["s2_max"], 1)
                    if s:
                        x_scaled(s - 1)
                        dve.sem_inc(S["s2_bias"], 1)

                k = 0
                for src, hi, lo, tiles in ((u_sb, ys_hi, ys_lo, 4), (yx, yx_hi, yx_lo, 4), (ya, ya_hi, ya_lo, 2)):
                    for t in range(tiles):
                        k += 1
                        dve.wait_ge(S["split2"], k)
                        dve.tensor_tensor(lo[:, t, :], src[:, t, :], hi[:, t, :].bitcast(F32),
                                          ALU.subtract).then_inc(S["rest2"], 1)
                for b in plan2[AT2["gates"]:AT2["w_out2"]]:
                    p, j = divmod(b.n - AT2["gates"], 7)
                    dve.wait_ge(S["g_free"], b.t0 + 2)
                    for m in range(2):
                        total = gate_tile(1, m)
                        if j in (1, 2):
                            step(dve.tensor_tensor(total, total, gate_tile(0 if j == 1 else 2, m), ALU.mult))
                        elif j in (4, 6):
                            step(dve.tensor_tensor(gate_tile(j, m), gate_tile(j, m), gate_tile(j - 1, m), ALU.mult))
                            ins = dve.tensor_tensor(total, total, gate_tile(j, m), ALU.add)
                            if j == 6:
                                ins.then_inc(S["merged"], 1)
                            else:
                                step(ins)
                    if j == 6:
                        for m in range(2):
                            k = 2 * p + m
                            dve.wait_ge(S["mg_hi_s"], k + 1)
                            dve.tensor_tensor(mg_lo[:, k, :], gate_tile(1, m), mg_hi[:, k, :].bitcast(F32),
                                              ALU.subtract).then_inc(S["mg_s"], 1)
                    rest_block(dve, plan2, b.n + 2)
                dve.wait_ge(S["x_back"], 16)
                for b in plan2[AT2["w_out2"]:AT2["ffn2_up"]]:
                    rest_block(dve, plan2, b.n + 2)
                    for m in range(2):
                        dve.wait_ge(S["g_free"], b.t0 + m + 1)
                        add_part(2 * (b.n - AT2["w_out2"]) + m)
                pre_norm_dve(dve, 3, 3, gains2["ffn2"])
                ffn("ffn2", F2T)
                norm_inverse(dve, 4)
                for k in range(KD):
                    dve.scalar_tensor_tensor(out=out_sb[:, k, :], in0=x_sb[:, k, :], scalar=gains2["final"][:, k:k + 1],
                                             in1=rs[:], op0=ALU.mult, op1=ALU.mult).then_inc(S["final_s"], 1)


def packed(plan, *mats):
    mats = dict(mats)
    out = np.zeros((len(plan), P, WSIZE), np.float32)
    for b in plan:
        a = mats[b.src][b.rows:b.rows + b.kt * P, b.cols:b.cols + b.w]
        out[b.n, :, 0:b.kt * b.w] = a.reshape(b.kt, P, b.w).transpose(1, 0, 2).reshape(P, b.kt * b.w)
    return out


def columns(v):
    return v.reshape(-1, P).T


def t5_bucket(dist):
    exact = BUCKETS // 2
    safe = np.maximum(np.asarray(dist, np.int32), 1).astype(np.float32)
    large = exact + (np.log(safe / exact) / np.log(MAX_DIST / exact) * (BUCKETS - exact)).astype(np.int32)
    return np.where(dist < exact, dist, np.minimum(large, BUCKETS - 1))


def states(v):
    v = v.reshape(STILES, P, *v.shape[2:])
    return np.moveaxis(v, 0, 1)


def constants():
    half = HD // 2
    inv = (1.0 / (10000.0 ** np.linspace(0.0, 1.0, half, dtype=np.float32))).astype(np.float32)
    ang = (inv[:, None] * np.arange(SEQ, dtype=np.float32)[None, :]).astype(np.float32)
    cos = np.tile(np.cos(ang), (4, 1)).astype(np.float32)
    sin = np.tile(np.sin(ang), (4, 1)).astype(np.float32)
    p = np.arange(P)
    swap = np.zeros((P, P), np.float32)
    for m in range(P):
        if m % HD < half:
            swap[m + half, m] = -1.0
        else:
            swap[m - half, m] = 1.0
    log_g = np.log1p(-(2.0 ** (-5.0 - np.arange(RET_HEADS))))
    d = np.arange(SEQ)[None, :] - p[:, None]
    decay = np.where(d >= 0, np.exp(np.maximum(d, 0)[None] * log_g[:, None, None]), 0.0)
    one_hot = np.zeros((BUCKETS + 1, PATTERNS, ROW), np.float32)
    for g in range(PATTERNS):
        zero = 255 if g == 0 else 127
        every = (1, 1, 4)[g]
        for n in range(ROW):
            steps = zero - n
            b = BUCKETS
            if 0 <= steps <= P and steps % every == 0:
                b = int(t5_bucket(steps * (1, 4, 4)[g]))
            one_hot[b, g, n] = 1.0
    return {
        "c_one_hot": one_hot,
        "c_time": np.tile(np.arange(SEQ, dtype=np.float32), (P, 1)),
        "c_ident": np.eye(P, dtype=np.float32),
        "c_ones": np.ones((P, P), np.float32),
        "c_head_ones": (p[:, None] // HD == p[None, :] // HD).astype(np.float32),
        "c_swap": swap,
        "c_cos": cos,
        "c_sin": sin,
        "c_decay": np.ascontiguousarray(decay.transpose(1, 0, 2)).astype(np.float32),
    }


def laid_out(a):
    plan = layer_pieces()
    out = constants()
    out["x"] = np.ascontiguousarray(a["x"][0].T)
    out["w1"] = np.stack([packed(plan, ("w_in", a["w_in"][l]), ("w_out", a["w_out"][l]), ("w_up", a["w_up"][l]),
                                 ("w_down", a["w_down"][l])) for l in range(DEPTH)])
    par = []
    for l in range(DEPTH):
        cw = a["conv_w"][l].T.reshape(2, P, TAPS).transpose(1, 0, 2).reshape(P, 2 * TAPS)
        par.append(np.concatenate(
            [columns(a[n][l]) for n in ("norm_mix_pre", "norm_mix_post", "norm_mlp_pre", "norm_mlp_post")]
            + [cw] + [columns(a[n][l]) for n in ("conv_b", "conv_ln_g", "conv_ln_b")], axis=1))
    out["par1"] = np.stack(par)
    at = np.clip(SEQ - 1 - np.arange(SEQ + P - 1), -REL_CLIP, REL_CLIP) + REL_CLIP
    out["att_bias_rows"] = a["attn_rel_bias"][:, :, at]
    out["rel_table"] = a["rel_table_2"]
    plan2, _ = third_pieces()
    out["w2"] = packed(plan2, ("ffn1_in", a["ffn1_w_in_2"][0]), ("ffn1_down", a["ffn1_w_down_2"][0]),
                       ("w_kv", a["xattn_w_kv_2"][0]), ("w_in2", a["w_in_2"][0]), ("w_glu", a["ssm_w_glu_2"][0]),
                       ("w_attn_up", a["attn_w_up_2"][0]), ("w_xattn_up", a["xattn_w_up_2"][0]),
                       ("w_out2", a["w_out_2"][0]), ("ffn2_in", a["ffn2_w_in_2"][0]),
                       ("ffn2_down", a["ffn2_w_down_2"][0]))
    log_dt = np.broadcast_to(a["ssm_log_dt_2"][0][:, None], (SSM_W // SSM_G, SSM_N))
    out["par2"] = np.concatenate(
        [columns(v) for v in (a["ffn1_norm_2"][0], a["mem_norm_2"][0], a["mix_norm_2"][0], a["ffn2_norm_2"][0],
                              a["final_norm_2"])]
        + [states(a["ssm_a_re_2"][0]), states(a["ssm_a_im_2"][0]), states(log_dt),
           columns(a["ssm_d_2"][0].reshape(-1))], axis=1)
    out["ssm_bc"] = np.stack([states(a["ssm_b_re_2"][0]), states(a["ssm_b_im_2"][0]),
                              states(a["ssm_c_re_2"][0].transpose(0, 2, 1)),
                              states(a["ssm_c_im_2"][0].transpose(0, 2, 1))], axis=1)
    out["mem"] = a["mem_2"][0].T
    return out


def kernel(**inputs):
    import concourse.bacc as _bacc
    from concourse.bass_utils import run_bass_kernel_spmd as _run

    arrays = {n: np.ascontiguousarray(v) for n, v in laid_out({n: np.asarray(v) for n, v in inputs.items()}).items()}
    nc = _bacc.Bacc("TRN2", target_bir_lowering=False, num_devices=1)
    ins = {n: nc.dram_tensor(f"in_{n}", v.shape, F32, kind="ExternalInput").ap() for n, v in arrays.items()}
    out = nc.dram_tensor("out_t", [DM, SEQ], F32, kind="ExternalOutput").ap()
    build(nc, ins, [out])
    r = _run(nc, [{f"in_{n}": v for n, v in arrays.items()}], core_ids=[0])
    return np.ascontiguousarray(r.results[0]["out_t"].T)[None]
```

```python
from contextlib import ExitStack

import concourse.bass as bass
import numpy as np
from concourse import mybir

F32 = mybir.dt.float32
F32R = mybir.dt.float32r
I32 = mybir.dt.int32
ALU = mybir.AluOpType
ACT = mybir.ActivationFunctionType
AX_X = mybir.AxisListType.X

P = 128
SEQ = 512
TOKT = SEQ // P
DM = 1024
KD = DM // P
DEPTH = 2
HD = 64
ATT_HEADS = 6
ATT_W = ATT_HEADS * HD
RET_HEADS = 6
RET_W = RET_HEADS * HD
CONV_W = DM // 4
TAPS = 31
PAD = TAPS - 1
CHUNK = 64
REL_CLIP = 128
D_FF = 4096
EPS = 1e-6
MASKED = -1e30
F2 = 2816
F2T = F2 // P
PATTERNS = 3
SLOTS = 4
A2 = PATTERNS * SLOTS * HD
BUCKETS = 32
MAX_DIST = 2048
ROW = 384
SSM_W = 512
SSM_G = 16
SSM_N = 64
STILES = SSM_W // SSM_G * SSM_N // P
XH = 4
MEM = 256
MEMT = MEM // P
TWO_PI = 2 * np.pi
PI2_A = 6.28125
PI2_B = float(np.float32(np.round((TWO_PI - PI2_A) * 2 ** 20) / 2 ** 20))
PI2_C = float(np.float32(TWO_PI - PI2_A - PI2_B))
BELOW_2PI = 6.283185
BELOW_PI = 3.1415925
MAGIC = 12582912.0
WCOLS = 256
WSIZE = KD * WCOLS
BIAS_ROW = SEQ + P - 1
KB = 1024
BASE = 16640


class Piece:

    def __init__(self, rows, cols, w, kt, kind, src="", group=None):
        self.rows, self.cols, self.w, self.kt, self.kind, self.src = rows, cols, w, kt, kind, src
        self.group = group


def number(pieces, tok_tiles=None):
    units = 0
    groups = []
    for n, b in enumerate(pieces):
        b.n, b.slot = n, n % 2
        b.tiles = b.w // P if b.kind == "feat" else (tok_tiles[n] if tok_tiles else TOKT)
        b.u0 = units
        units += b.tiles
        b.u1 = units
        if b.group is None or n == 0 or pieces[n - 1].group != b.group:
            b.first, b.k0 = True, 0
            groups.append(b.tiles)
        else:
            b.first, b.k0 = False, pieces[n - 1].k0 + pieces[n - 1].kt
        b.last = b.group is None or n + 1 == len(pieces) or pieces[n + 1].group != b.group
        b.g = len(groups) - 1
    for b in pieces:
        b.t0 = sum(groups[:b.g])
        b.free = sum(groups[:b.g - 1]) if b.g >= 2 else 0
        b.bank = 2 * (b.g % 2)
    return pieces


class Turn:

    def __init__(self, i=0, dn=0, du=0, dt=0):
        self.i, self.dn, self.du, self.dt = i, dn, du, dt

    def n(self, v):
        return v + self.i * self.dn

    def loads(self, n):
        return (n // 2 + 1) * 16 + self.i * (self.dn * 8)

    def u(self, v):
        return v + self.i * self.du

    def t(self, v):
        return v + self.i * self.dt


ONCE = Turn()


def layer_pieces():
    out = []
    a = ATT_W

    def feat(c0, c1):
        for c in range(c0, c1, WCOLS):
            out.append(Piece(0, c, min(WCOLS, c1 - c), KD, "feat", "w_in"))

    def tok(c0, c1):
        for c in range(c0, c1, WCOLS):
            out.append(Piece(0, c, min(WCOLS, c1 - c), KD, "tok", "w_in"))

    feat(3 * a, 3 * a + 2 * CONV_W)
    feat(0, 2 * a)
    tok(2 * a, 3 * a)
    r = 3 * a + 2 * CONV_W
    feat(r, r + 2 * RET_W)
    tok(r + 2 * RET_W, r + 3 * RET_W)
    feat(r + 3 * RET_W, r + 4 * RET_W)
    for c in range(0, DM, WCOLS):
        out.append(Piece(0, c, WCOLS, KD, "feat", "w_out"))
    for half in range(2):
        for j in range(8):
            out.append(Piece(0, half * 2048 + j * WCOLS, WCOLS, KD, "feat", "w_up"))
        for j in range(4):
            for kb in range(2):
                out.append(Piece(half * 2048 + kb * KB, j * WCOLS, WCOLS, KD, "feat", "w_down",
                                 group=("down", half, j)))
    return number(out)


FFN_PARTS = (6, 6, 5, 5)
GATES = ("glu_b", "glu_a", "gate0", "attn_up", "gate1", "xattn_up", "gate2")


def third_pieces():
    out, start = [], {}

    def ffn(name):
        start[name + "_up"] = len(out)
        for j in range(F2 // WCOLS):
            for c in (0, F2):
                out.append(Piece(0, c + j * WCOLS, WCOLS, KD, "feat", name + "_in"))
        start[name + "_down"] = len(out)
        for j in range(DM // WCOLS):
            k0 = 0
            for kt in FFN_PARTS:
                out.append(Piece(k0 * P, j * WCOLS, WCOLS, kt, "feat", name + "_down", group=(name, j)))
                k0 += kt

    ffn("ffn1")
    start["mk"] = len(out)
    for c in range(0, 512, WCOLS):
        out.append(Piece(0, c, WCOLS, KD, "feat", "w_kv"))
    start["mv"] = len(out)
    for c in range(512, 1024, WCOLS):
        out.append(Piece(0, c, WCOLS, KD, "tok", "w_kv"))
    col = 0
    for name, width, kind in (("u", SSM_W, "feat"), ("q", A2, "feat"), ("k", A2, "feat"), ("v", A2, "tok"),
                              ("xq", 512, "feat")):
        start[name] = len(out)
        for c in range(col, col + width, WCOLS):
            out.append(Piece(0, c, WCOLS, KD, kind, "w_in2"))
        col += width
    start["gates"] = len(out)
    for p in range(DM // WCOLS):
        c = p * WCOLS
        for name in GATES:
            if name == "glu_a":
                out.append(Piece(0, c, WCOLS, 4, "feat", "w_glu"))
            elif name == "glu_b":
                out.append(Piece(0, DM + c, WCOLS, 4, "feat", "w_glu"))
            elif name == "attn_up":
                out.append(Piece(0, c, WCOLS, 2, "feat", "w_attn_up"))
            elif name == "xattn_up":
                out.append(Piece(0, c, WCOLS, 4, "feat", "w_xattn_up"))
            else:
                out.append(Piece(0, col + int(name[-1]) * DM + c, WCOLS, KD, "feat", "w_in2"))
    start["w_out2"] = len(out)
    for c in range(0, DM, WCOLS):
        out.append(Piece(0, c, WCOLS, KD, "feat", "w_out2"))
    ffn("ffn2")
    tok_tiles = [MEMT if b.kind == "tok" and b.src == "w_kv" else TOKT for b in out]
    return number(out, tok_tiles), start


def build(nc, ins, outs):
    A = ins
    plan1 = layer_pieces()
    plan2, AT2 = third_pieces()
    with ExitStack() as ctx:
        def at(name, shape, dt, kb):
            return nc.alloc_sbuf_tensor_at(name, shape, dt, offset=BASE + int(kb * 1024))

        def sem(name):
            s = ctx.enter_context(nc.semaphore(name))
            return s

        w_raw = at("w_raw", [P, 2, WSIZE], F32, 0)
        w_hi = at("w_hi", [P, 2, WSIZE], F32R, 16)
        w_lo = at("w_lo", [P, 2, WSIZE], F32R, 32)
        x_sb = at("x_sb", [P, KD, SEQ], F32, 48)
        h_hi = at("h_hi", [P, KD, SEQ], F32R, 64)
        h_lo = at("h_lo", [P, KD, SEQ], F32R, 80)
        FZ = 96
        OZ = FZ + 88
        out_sb = at("out_sb", [P, KD, SEQ], F32, OZ)
        CZ = OZ + 16
        ident = at("ident_sb", [P, P], F32, CZ)
        ones = at("ones_sb", [P, P], F32, CZ + 0.5)
        head_ones = at("head_ones_sb", [P, P], F32, CZ + 1)
        swap = at("swap_sb", [P, P], F32, CZ + 1.5)
        rs = at("rs", [P, SEQ], F32, CZ + 2)
        n1 = len(plan1)
        layer_weights = A["w"][0:DEPTH * n1].rearrange("(l n) p c -> l n p c", l=DEPTH)
        next_gains = A["first_gains"][1:]
        next_weights = A["w"][n1:n1 + DEPTH * n1].rearrange("(l n) p c -> l n p c", l=DEPTH)
        par = at("par_sb", [P, 128], F32, CZ + 4)
        tiny = at("tiny", [P, 64], F32, CZ + 4.5)
        inverse = tiny[:, 32:32 + TOKT]
        eps_c = at("eps_c", [P, 1], F32, CZ + 4.75)
        quarter = at("quarter", [P, 1], F32, CZ + 4.8125)
        first_gain = at("first_gain", [P, KD], F32, CZ + 4.875)
        par2 = at("par2_sb", [P, 96], F32, CZ + 5)

        qk = at("qk", [P, 6, SEQ], F32, FZ)
        av = at("av", [P, TOKT, ATT_W], F32, FZ + 12)
        rv = at("rv", [P, TOKT, RET_W], F32, FZ + 18)
        rg = at("rg", [P, 3, SEQ], F32, FZ + 24)
        rqk = at("rqk", [P, 6, SEQ], F32, FZ + 30)
        ca = at("ca", [P, 2, SEQ + PAD], F32, FZ + 42)
        cg = at("cg", [P, 2, SEQ], F32, FZ + 46.25)
        bias_t = at("bias_t", [P, ATT_HEADS, SEQ], F32, FZ + 50.5)
        decay_t = at("decay_t", [P, RET_HEADS, SEQ], F32, FZ + 62.5)
        cos_t = at("cos_t", [P, SEQ], F32, FZ + 74.5)
        sin_t = at("sin_t", [P, SEQ], F32, FZ + 76.5)
        probs = at("probs", [P, 4, SEQ], F32, FZ + 78.5)
        rot_a = at("rot_a", [P, 2, SEQ], F32, FZ + 78.5)
        conv_sq = at("conv_sq", [P, 2, SEQ], F32, FZ + 46.25)
        ret_sq = at("ret_sq", [P, 3, SEQ], F32, FZ + 12)
        sc_off = [0, 512, 896, 1152]
        ret_sc = at("ret_sc", [P, 2, 1280], F32, FZ)
        ret_rs = at("ret_rs", [P, 3, SEQ], F32, FZ + 50.5)
        probs_t = at("probs_t", [P, 2, SEQ], F32, 84)
        conv_rs = at("conv_rs", [P, SEQ], F32, FZ + 82.5)

        def sq_tile(m):
            return conv_sq[:, m - 3, :] if m < 5 else ret_sq[:, m - 5, :]

        def ln_rs(j):
            return ret_rs[:, j - 1, :] if j else conv_rs[:]

        f_hi = at("f_hi", [P, 16, SEQ], F32R, FZ)
        f_lo = at("f_lo", [P, 16, SEQ], F32R, FZ + 32)
        sq_f = at("sq_f", [P, KD, SEQ], F32, FZ + 64)
        tt = at("tt", [P, 4, SEQ], F32, FZ + 80)
        part = at("part", [P, KD, SEQ], F32, 64)

        bank = [ctx.enter_context(nc.psum_tensor(f"gemm{i}", [P, SEQ], F32)) for i in range(4)]
        s_ps = [ctx.enter_context(nc.psum_tensor(f"score{i}", [P, SEQ], F32)) for i in range(2)]
        t_ps = ctx.enter_context(nc.psum_tensor("turned", [P, SEQ], F32))
        o_ps = ctx.enter_context(nc.psum_tensor("mixed", [P, SEQ], F32))

        score_bank = [s_ps[0], s_ps[1], bank[0], bank[1]]
        turn_bank = [t_ps, bank[2]]

        bias_rep = nc.dram_tensor("bias_rep", [ATT_HEADS, P, BIAS_ROW], F32, kind="Internal").ap()

        def skewed(rep, width, cols):
            flat = rep.rearrange("h p n -> h (p n)")[:, P - 1:P - 1 + P * (width - 1)]
            return flat.rearrange("h (p n) -> p h n", n=width - 1)[:, :, 0:cols]

        consts_in, x_in, table_in, rows_out = sem("consts_in"), sem("x_in"), sem("table_in"), sem("rows_out")

        eps_set, picked, picked_out, eps_made = sem("eps_set"), sem("picked"), sem("picked_out"), sem("eps_made")
        t5_rep = nc.dram_tensor("t5_rep", [PATTERNS, SLOTS, P, ROW], F32, kind="Internal").ap()
        table = at("table_sb", [BUCKETS + 1, PATTERNS * SLOTS], F32, FZ)
        one_hot = at("one_hot_sb", [BUCKETS + 1, PATTERNS, ROW], F32, FZ + 1)
        row_sb = at("row_sb", [SLOTS, PATTERNS, ROW], F32, FZ + 6)
        names = ["w_in0", "w_in1", "w_rounded", "w_rest", "units", "g_free", "gain_in", "par_in", "bias_rep_s", "tab_in", "squares",
                 "norm_sum", "norm_root", "norm_turned", "norm_inv", "norm_spread", "normed", "norm_hi", "h_ready", "x_done", "dve_own",
                 "centred", "maxed", "glu", "taps", "ln_mean", "ln_sq_s", "ln_var", "ln_root", "ret_inv", "ret_scaled", "ret_gated", "ln_done", "rot_ps", "rot_cos", "rot_done",
                 "score_ps", "biased", "exped", "inverted", "scaled", "turned_ps", "turned", "mixed_ps", "att_out",
                 "ret_ps", "ret_sc_s", "ret_mix", "ret_out", "y_hi", "f_sq", "f_hi_s", "f_ready", "part_done", "act_own"]
        S = {n: sem(n) for n in names}
        w_in_s = [S["w_in0"], S["w_in1"]]

        def view(buf, b):
            return buf[:, b.slot, 0:b.kt * b.w].rearrange("p (k c) -> p k c", k=b.kt)

        def load_block(sp, src, b, t=ONCE):
            if b.n >= 2:
                sp.wait_ge(S["w_rounded"], t.n(b.n - 1))
                sp.wait_ge(S["w_rest"], t.n(b.n - 1))
            size = b.kt * b.w
            sp.dma_start(w_raw[:, b.slot, 0:size], src[t.n(b.n), :, 0:size]).then_inc(w_in_s[b.slot], 16)

        def round_block(act, plan, n, t=ONCE, whole=False):
            if isinstance(t.n(n), int) and t.n(n) >= len(plan):
                return
            b = plan[n]
            act.wait_ge(w_in_s[b.slot], t.loads(n))
            if n >= 2:
                act.wait_ge(S["units"], t.u(plan[n - 2].u1))
            size = WSIZE if whole else b.kt * b.w
            act.activation(w_hi[:, b.slot, 0:size], w_raw[:, b.slot, 0:size], ACT.Copy).then_inc(S["w_rounded"], 1)

        def rest_block(dve, plan, n, t=ONCE, whole=False):
            if isinstance(t.n(n), int) and t.n(n) >= len(plan):
                return
            b = plan[n]
            dve.wait_ge(S["w_rounded"], t.n(n + 1))
            size = WSIZE if whole else b.kt * b.w
            dve.tensor_tensor(w_lo[:, b.slot, 0:size], w_raw[:, b.slot, 0:size],
                              w_hi[:, b.slot, 0:size].bitcast(F32), ALU.subtract).then_inc(S["w_rest"], 1)

        def product(pe, b, hi, lo, t=ONCE, ready=None, k0=None, width=SEQ, tokens=None, between=None):
            tokens = tokens or (lambda m: lambda a: a[:, m * P:(m + 1) * P])
            pe.wait_ge(S["w_rest"], t.n(b.n + 1))
            k0 = b.k0 if k0 is None else k0
            wh, wl = view(w_hi, b), view(w_lo, b)
            for m in range(b.tiles):
                if b.first and b.free:
                    pe.wait_ge(S["g_free"], t.t(b.free))
                for k in range(b.kt):
                    if ready is not None and m == 0:
                        pe.wait_ge(S["h_ready"], ready + k + 1)
                    if b.kind == "feat":
                        c = slice(m * P, (m + 1) * P)
                        dst = bank[b.bank + m][:, 0:width]
                        trio = ((wh[:, k, c], hi[:, k0 + k, :]), (wh[:, k, c], lo[:, k0 + k, :]),
                                (wl[:, k, c], hi[:, k0 + k, :]))
                    else:
                        pick = tokens(m)
                        dst = bank[b.bank + m // 2][:, (m % 2) * 256:(m % 2) * 256 + b.w]
                        h, r = pick(hi[:, k, :]), pick(lo[:, k, :])
                        trio = ((h, wh[:, k, :]), (h, wl[:, k, :]), (r, wh[:, k, :]))
                    for j, (lhs, rhs) in enumerate(trio):
                        mm = pe.matmul(dst, lhs, rhs, start=b.first and k == 0 and j == 0,
                                       stop=b.last and k == b.kt - 1 and j == 2)
                mm.then_inc(S["units"], 1)
                if between:
                    between(m)

        def tile_of(b, m, width=SEQ):
            if b.kind == "feat":
                return bank[b.bank + m][:, 0:width]
            return bank[b.bank + m // 2][:, (m % 2) * 256:(m % 2) * 256 + b.w]

        def head_start(engine):
            if engine is nc.sync:
                for s in w_in_s:
                    engine.sem_inc(s, 16)
            else:
                engine.sem_inc(S["w_rounded" if engine is nc.scalar else "w_rest"], 2)

        def load_next(sp, q, src, n=0):
            if n:
                sp.wait_ge(S["w_rounded"], n - 1 + q)
                sp.wait_ge(S["w_rest"], n - 1 + q)
            sp.dma_start(w_raw[:, q, :], src).then_inc(w_in_s[q], 16)

        def round_next(act, q, plan=()):
            act.wait_ge(w_in_s[q], (len(plan) // 2 + 1) * 16)
            if plan:
                act.wait_ge(S["units"], plan[len(plan) - 2 + q].u1)
            act.activation(w_hi[:, q, :], w_raw[:, q, :], ACT.Copy).then_inc(S["w_rounded"], 1)

        def rest_next(dve, q, n=0):
            dve.wait_ge(S["w_rounded"], n + q + 1)
            dve.tensor_tensor(w_lo[:, q, :], w_raw[:, q, :], w_hi[:, q, :].bitcast(F32),
                              ALU.subtract).then_inc(S["w_rest"], 1)

        def norm_squares(act, i, src, sq, wait=None, tiles=range(KD)):
            for k in tiles:
                if wait is not None:
                    act.wait_ge(wait[0], wait[1] + k + 1)
                act.activation(sq[:, k, :], src[:, k, :], ACT.Square).then_inc(S["squares"], 1)

        def norm_add(pe, i, sq, k, n=SEQ):
            pe.wait_ge(S["squares"], KD * (i - 1) + k + 1)
            mm = pe.matmul(o_ps[:, 0:n], ones[:], sq[:, k, :], start=k == 0, stop=k == KD - 1)
            if k == KD - 1:
                mm.then_inc(S["norm_sum"], 1)

        def norm_total(pe, i, sq, n=SEQ, done=0):
            for k in range(done, KD):
                norm_add(pe, i, sq, k, n)
            pe.wait_ge(S["norm_root"], i)
            for q in range(n // P):
                mm = pe.matmul(o_ps[:, q:q + 1], rs[0:1, P * q:P * q + P], ones[0:1, 0:1], start=True, stop=True)
            mm.then_inc(S["norm_turned"], 1)
            pe.wait_ge(S["norm_inv"], i)
            for q in range(n // P):
                mm = pe.matmul(t_ps[:, P * q:P * q + P], inverse[:, q:q + 1].broadcast_to([P, P]), ident[:],
                               start=True, stop=True)
            mm.then_inc(S["norm_spread"], 1)

        def norm_rooted(act, i, n=SEQ):
            act.wait_ge(S["norm_sum"], i)
            act.activation(rs[0:1, 0:n], o_ps[0:1, 0:n], ACT.Sqrt, scale=1.0 / DM,
                           bias=eps_c[0:1, 0:1]).then_inc(S["norm_root"], 1)

        def norm_inverse(dve, i, n=SEQ):
            dve.wait_ge(S["norm_turned"], i)
            dve.reciprocal(inverse[:, 0:n // P], o_ps[:, 0:n // P]).then_inc(S["norm_inv"], 1)
            dve.wait_ge(S["norm_spread"], i)

        def norm_scale(dve, i, k, src, dst, gain, n=SEQ):
            dve.scalar_tensor_tensor(out=dst[:, k, :], in0=src[:, k, :], scalar=gain[:, k:k + 1], in1=t_ps[:, 0:n],
                                     op0=ALU.mult, op1=ALU.mult).then_inc(S["normed"], 1)

        def split_hi(act, i, j, src, wait_sem, wait_base, hi=h_hi):
            for k in range(KD):
                act.wait_ge(wait_sem, wait_base + k + 1)
                act.activation(hi[:, k, :], src[:, k, :], ACT.Copy).then_inc(S["norm_hi"], 1)

        def pre_norm_dve(dve, i, j, gain, n=SEQ, src=x_sb, tmp=out_sb, hi=h_hi, lo=h_lo):
            if i:
                norm_inverse(dve, i, n)
            for k in range(KD + 1):
                if k < KD:
                    norm_scale(dve, i, k, src, tmp, gain, n)
                if k:
                    dve.wait_ge(S["norm_hi"], KD * j + k)
                    dve.tensor_tensor(lo[:, k - 1, :], tmp[:, k - 1, :], hi[:, k - 1, :].bitcast(F32),
                                      ALU.subtract).then_inc(S["h_ready"], 1)

        def post_norm_dve(dve, i, gain, base):
            norm_inverse(dve, i)
            for k in range(KD + 1):
                if k < KD:
                    norm_scale(dve, i, k, out_sb, out_sb, gain)
                if k:
                    dve.wait_ge(S["normed"], KD * i + k)
                    dve.tensor_tensor(x_sb[:, k - 1, :], x_sb[:, k - 1, :], out_sb[:, k - 1, :],
                                      ALU.add).then_inc(S["x_done"], 1)

        gains = {n: par[:, 8 * i:8 * i + 8] for i, n in enumerate(("mix_pre", "mix_post", "mlp_pre", "mlp_post"))}
        conv_w = par[:, 32:94].rearrange("p (j t) -> p j t", j=2)
        conv_b, ln_g, ln_b = par[:, 94:96], par[:, 96:98], par[:, 98:100]
        N_IN = 14
        W_OUT = 14
        UP = [18, 34]
        DOWN = [26, 42]
        PAIRS = RET_HEADS // 2
        LN = [(ones, (3, 4), CONV_W)] + [(head_ones, (5 + p,), HD) for p in range(PAIRS)]
        TAP_OPS = 2 * TAPS
        TAP_SLOTS = 9
        ROTARY_AT = 10

        def clear_counts():
            for s in S.values():
                nc.gpsimd.sem_clear(s)
            nc.all_engine_barrier()

        with nc.Block() as block:
            @block.gpsimd
            def _(pool):
                pool.memset(table[:], MASKED).then_inc(eps_set, 1)
                for g in range(PATTERNS):
                    pool.wait_ge(picked_out, g + 1)
                    pool.dma_start(t5_rep[g], row_sb[:, g, :].unsqueeze(1).broadcast_to(
                        [SLOTS, P, ROW])).then_inc(rows_out, 16)

            @block.tensor
            def _(pe):
                pe.wait_ge(table_in, 32)
                for g in range(PATTERNS):
                    pe.matmul(bank[g][0:SLOTS, 0:ROW], table[:, SLOTS * g:SLOTS * g + SLOTS], one_hot[:, g, :],
                              start=True, stop=True).then_inc(picked, 1)
                pe.wait_ge(consts_in, 64)
                norm_total(pe, 1, out_sb)

            @block.sync
            def _(sp):
                sp.dma_start(one_hot[:], A["c_one_hot"]).then_inc(table_in, 16)
                sp.wait_ge(eps_set, 1)
                sp.dma_start(table[0:BUCKETS, :], A["rel_table"]).then_inc(table_in, 16)
                sp.dma_start(x_sb[:], A["x"].rearrange("(k p) t -> p k t", p=P)).then_inc(x_in, 16)
                for dst, src in ((ident, "c_ident"), (ones, "c_ones"), (head_ones, "c_head_ones"), (swap, "c_swap")):
                    sp.dma_start(dst[:], A[src]).then_inc(consts_in, 16)
                for q in range(2):
                    load_next(sp, q, A["w"][q])
                sp.dma_start(first_gain[:], A["first_gains"][0]).then_inc(S["gain_in"], 16)
                sp.wait_ge(S["gain_in"], 16)

            @block.scalar
            def _(act):
                act.wait_ge(x_in, 16)
                norm_squares(act, 1, x_sb, out_sb)
                act.wait_ge(eps_made, 1)
                norm_rooted(act, 1)
                for q in range(2):
                    round_next(act, q)

            @block.vector
            def _(dve):
                dve.memset(eps_c[:], EPS).then_inc(eps_made, 1)
                dve.memset(quarter[:], np.pi / 2)
                for g in range(PATTERNS):
                    dve.wait_ge(picked, g + 1)
                    dve.tensor_copy(row_sb[:, g, :], bank[g][0:SLOTS, 0:ROW]).then_inc(picked_out, 1)
                norm_inverse(dve, 1)
                for q in range(2):
                    rest_next(dve, q)

        clear_counts()

        with nc.Fori(0, DEPTH) as layer:
            with nc.Block() as block:
                @block.sync
                def _(sp):
                    sp.dma_start(par[:, 0:100], A["par1"][layer]).then_inc(S["par_in"], 16)
                    src = layer_weights[layer]
                    head_start(sp)
                    sp.dma_start(bias_rep, A["att_bias_rows"][layer].unsqueeze(1).broadcast_to(
                        [ATT_HEADS, P, BIAS_ROW])).then_inc(S["bias_rep_s"], 16)
                    sp.wait_ge(S["bias_rep_s"], 16)
                    for dst, s in ((cos_t[:], A["c_cos"]), (sin_t[:], A["c_sin"]),
                                   (decay_t[:], A["c_decay"]), (bias_t[:], skewed(bias_rep, BIAS_ROW, SEQ))):
                        sp.dma_start(dst, s).then_inc(S["tab_in"], 16)
                    for b in plan1[2:N_IN]:
                        load_block(sp, src, b)
                    with sp.Fori(0, (len(plan1) - N_IN) // 2) as i:
                        for b in plan1[N_IN:N_IN + 2]:
                            load_block(sp, src, b, Turn(i, dn=2))
                    for q in range(2):
                        load_next(sp, q, next_weights[layer][q], n1)
                    sp.wait_ge(S["normed"], KD)
                    sp.dma_start(first_gain[:], next_gains[layer]).then_inc(S["gain_in"], 16)
                    sp.wait_ge(S["gain_in"], 16)

                @block.tensor
                def _(pe):
                    def layer_norm_mean(j):
                        mat, tiles, _ = LN[j]
                        for q, m in enumerate(tiles):
                            mm = pe.matmul(t_ps[:], mat[:], out_sb[:, m, :], start=q == 0, stop=q == len(tiles) - 1)
                        mm.then_inc(S["ln_mean"], 1)

                    def layer_norm_var(j):
                        mat, tiles, _ = LN[j]
                        pe.wait_ge(S["ln_sq_s"], sum(len(LN[q][1]) for q in range(j + 1)))
                        for q, m in enumerate(tiles):
                            mm = pe.matmul(t_ps[:], mat[:], sq_tile(m), start=q == 0, stop=q == len(tiles) - 1)
                        mm.then_inc(S["ln_var"], 1)

                    def swapped(j):
                        if j >= 2:
                            pe.wait_ge(S["rot_done"], j - 1)
                        pe.matmul(s_ps[j % 2][:], swap[:], rqk[:, j, :], start=True, stop=True).then_inc(S["rot_ps"], 1)

                    for b in plan1[:N_IN]:
                        product(pe, b, h_hi, h_lo, ready=0 if b.n == 0 else None)
                        if b.n == ROTARY_AT:
                            pe.wait_ge(S["g_free"], plan1[9].t0 + 2)
                            pe.wait_ge(S["taps"], TAP_OPS)
                            layer_norm_mean(0)
                        if b.n == ROTARY_AT + 1:
                            layer_norm_var(0)
                        if ROTARY_AT <= b.n < ROTARY_AT + 3:
                            for j in range(2):
                                swapped(2 * (b.n - ROTARY_AT) + j)

                    pe.wait_ge(S["rot_done"], 6)
                    pe.wait_ge(S["ln_root"], 1)
                    steps = [(h, q) for h in range(ATT_HEADS) for q in range(TOKT)]

                    def scores(s):
                        h, q = steps[s]
                        r = slice(HD * (h % 2), HD * (h % 2) + HD)
                        if s >= 4:
                            pe.wait_ge(S["biased"], s - 3)
                        pe.matmul(score_bank[s % 4][:, 0:P * (q + 1)], qk[r, h // 2, P * q:P * q + P],
                                  qk[r, 3 + h // 2, 0:P * (q + 1)], start=True, stop=True).then_inc(S["score_ps"], 1)

                    def turn(s):
                        h, q = steps[s]
                        pe.wait_ge(S["scaled"], s + 1)
                        if s >= 2:
                            pe.wait_ge(S["turned"], s - 1)
                        for j in range(q + 1):
                            mm = pe.transpose(turn_bank[s % 2][:, P * j:P * j + P], probs[:, s % 4, P * j:P * j + P],
                                              ident[:])
                        mm.then_inc(S["turned_ps"], 1)

                    def mix(s):
                        h, q = steps[s]
                        pe.wait_ge(S["turned"], s + 1)
                        if q == 0 and h % 2 == 0 and h:
                            pe.wait_ge(S["att_out"], h // 2)
                        r = slice(HD * (h % 2), HD * (h % 2) + HD)
                        for j in range(q + 1):
                            mm = pe.matmul(o_ps[r, P * q:P * q + P], av[:, j, HD * h:HD * h + HD],
                                           probs_t[:, s % 2, P * j:P * j + P], start=j == 0, stop=j == q)
                        mm.then_inc(S["mixed_ps"], 1)

                    n = len(steps)
                    pe.wait_ge(S["g_free"], plan1[N_IN].t0)
                    for s in range(n + 3):
                        if s < n:
                            scores(s)
                        if 2 <= s <= n + 1:
                            turn(s - 2)
                        if s >= 3:
                            mix(s - 3)

                    rsteps = [(h, j) for h in range(RET_HEADS) for j in range(TOKT)]

                    def ret_scores(s):
                        h, j = rsteps[s]
                        r = slice(HD * (h % 2), HD * (h % 2) + HD)
                        if s < 2:
                            pe.wait_ge(S["biased"], n - 3 + s)
                        else:
                            pe.wait_ge(S["ret_sc_s"], s - 1)
                        pe.matmul(s_ps[s % 2][:, 0:SEQ - P * j], rqk[r, 3 + h // 2, P * j:P * j + P],
                                  rqk[r, h // 2, P * j:SEQ], start=True, stop=True).then_inc(S["ret_ps"], 1)

                    def ret_mixed(s):
                        h, j = rsteps[s]
                        pe.wait_ge(S["ret_sc_s"], s + 1)
                        if j == 0 and h % 2 == 0:
                            if h:
                                pe.wait_ge(S["ret_out"], h // 2)
                            else:
                                pe.wait_ge(S["att_out"], ATT_HEADS // 2)
                        r = slice(HD * (h % 2), HD * (h % 2) + HD)
                        pe.matmul(o_ps[r, P * j:SEQ], rv[:, j, HD * h:HD * h + HD],
                                  ret_sc[:, h % 2, sc_off[j]:sc_off[j] + SEQ - P * j],
                                  start=j == 0, stop=j == TOKT - 1).then_inc(S["ret_mix"], 1)

                    for s in range(len(rsteps) + 1):
                        if s < len(rsteps):
                            ret_scores(s)
                        if s:
                            ret_mixed(s - 1)
                        p, at_step = divmod(s - 1, 2 * TOKT)
                        if p and at_step == TOKT // 2:
                            pe.wait_ge(S["ret_out"], p)
                            layer_norm_mean(p)
                        if p and at_step == TOKT + TOKT // 2 and p < PAIRS:
                            layer_norm_var(p)
                    pe.wait_ge(S["ret_out"], PAIRS)
                    pe.wait_ge(S["ln_root"], PAIRS)
                    layer_norm_mean(PAIRS)
                    layer_norm_var(PAIRS)

                    for b in plan1[W_OUT:W_OUT + 4]:
                        product(pe, b, h_hi, h_lo, ready=KD if b.n == W_OUT else None)
                        for k in range(2 * (b.n - W_OUT) - 2, 2 * (b.n - W_OUT)):
                            if k >= 0:
                                norm_add(pe, 1, sq_f, k)
                    norm_total(pe, 1, sq_f, done=KD - 2)
                    norm_total(pe, 2, out_sb)
                    for half in range(2):
                        first = plan1[UP[half]]
                        for b in plan1[first.n:first.n + 2]:
                            product(pe, b, h_hi, h_lo, ready=2 * KD if b.n == UP[0] else None)
                        with pe.Fori(0, 3) as i:
                            for b in plan1[first.n + 2:first.n + 4]:
                                product(pe, b, h_hi, h_lo, Turn(i, dn=2, du=4, dt=4))
                        pe.wait_ge(S["f_ready"], 16 * (half + 1))
                        if half == 0:
                            with pe.Fori(0, 2) as i:
                                for b in plan1[DOWN[0]:DOWN[0] + 4]:
                                    product(pe, b, f_hi, f_lo, Turn(i, dn=4, du=8, dt=4))
                    for i in range(2):
                        for b in plan1[DOWN[1]:DOWN[1] + 4]:
                            product(pe, b, f_hi, f_lo, Turn(i, dn=4, du=8, dt=4))
                            k = 4 * i + (b.n - DOWN[1]) // 2 * 2 - 2
                            if b.last and k >= 0:
                                for q in range(2):
                                    norm_add(pe, 3, sq_f, k + q)
                    norm_total(pe, 3, sq_f, done=KD - 2)
                    norm_total(pe, 4, sq_f)

                @block.gpsimd
                def _(pool):
                    for j in range(1, PAIRS):
                        tile = out_sb[:, 4 + j, :]
                        pool.wait_ge(S["ret_inv"], j)
                        pool.tensor_tensor(tile, tile, ln_rs(j), ALU.mult).then_inc(S["ret_scaled"], 1)
                        pool.wait_ge(S["ret_scaled"], j)
                        pool.tensor_tensor(tile, tile, rg[:, j - 1, :], ALU.mult).then_inc(S["ret_gated"], 1)
                        pool.wait_ge(S["ret_gated"], j)

                @block.scalar
                def _(act):
                    head_start(act)
                    split_hi(act, 0, 0, out_sb, S["normed"], 0)

                    def evacuate(b, dst, func=ACT.Copy):
                        for m in range(b.tiles):
                            act.wait_ge(S["units"], b.u0 + (m + 1 if b.kind == "feat" else m // 2 * 2 + 2))
                            act.activation(dst(m), tile_of(b, m), func).then_inc(S["g_free"], 1)

                    act.wait_ge(rows_out, 16 * PATTERNS)
                    def layer_norm_sq(j):
                        _, tiles, width = LN[j]
                        before = sum(len(LN[q][1]) for q in range(j))
                        for q, m in enumerate(tiles):
                            act.wait_ge(S["centred"], before + q + 1)
                            act.activation(sq_tile(m), out_sb[:, m, :], ACT.Square).then_inc(S["ln_sq_s"], 1)

                    def layer_norm_root(j):
                        act.wait_ge(S["ln_var"], j + 1)
                        act.activation(ln_rs(j), t_ps[:], ACT.Sqrt, scale=1.0 / LN[j][2],
                                       bias=eps_c[:, 0:1]).then_inc(S["ln_root"], 1)

                    for b in plan1[:N_IN]:
                        if b.n == 0:
                            evacuate(b, lambda m: ca[:, m, PAD:PAD + SEQ])
                        elif b.n == 1:
                            evacuate(b, lambda m: cg[:, m, :], ACT.Sigmoid)
                        elif b.n < 5:
                            evacuate(b, lambda m: qk[:, 2 * (b.n - 2) + m, :])
                        elif b.n < 7:
                            evacuate(b, lambda m: av[:, m, 256 * (b.n - 5):256 * (b.n - 5) + b.w])
                        elif b.n < 10:
                            evacuate(b, lambda m: rqk[:, 2 * (b.n - 7) + m, :])
                        elif b.n < 12:
                            evacuate(b, lambda m: rv[:, m, 256 * (b.n - 10):256 * (b.n - 10) + b.w])
                        else:
                            evacuate(b, lambda m: rg[:, 2 * (b.n - 12) + m, :], ACT.Silu)
                        round_block(act, plan1, b.n + 2)
                        if b.n == ROTARY_AT:
                            layer_norm_sq(0)
                        if b.n == ROTARY_AT + 1:
                            layer_norm_root(0)

                    for q in range(2):
                        act.wait_ge(S["ln_done"], q + 1)
                        act.activation(out_sb[:, 3 + q, :], out_sb[:, 3 + q, :], ACT.Silu).then_inc(S["act_own"], 1)

                    steps = [(h, q) for h in range(ATT_HEADS) for q in range(TOKT)]
                    n = len(steps)
                    for s in range(n + 3):
                        if s < n:
                            q = steps[s][1]
                            act.wait_ge(S["maxed"], s + 1)
                            act.activation(probs[:, s % 4, 0:P * (q + 1)], probs[:, s % 4, 0:P * (q + 1)], ACT.Exp,
                                           bias=tiny[:, s % 4:s % 4 + 1],
                                           accum_out=tiny[:, 4 + s % 4:5 + s % 4]).then_inc(S["exped"], 1)
                        if 2 <= s <= n + 1:
                            p = s - 2
                            q = steps[p][1]
                            act.wait_ge(S["turned_ps"], p + 1)
                            if p >= 2:
                                act.wait_ge(S["mixed_ps"], p - 1)
                            act.activation(probs_t[:, p % 2, 0:P * (q + 1)], turn_bank[p % 2][:, 0:P * (q + 1)],
                                           ACT.Copy).then_inc(S["turned"], 1)
                        if s >= 3 and (s - 2) % (2 * TOKT) == 0:
                            pair = (s - 2) // (2 * TOKT)
                            act.wait_ge(S["mixed_ps"], 2 * TOKT * pair)
                            act.activation(out_sb[:, pair - 1, :], o_ps[:], ACT.Copy).then_inc(S["att_out"], 1)
                    def split_mixed(k):
                        act.activation(h_hi[:, k, :], out_sb[:, k, :], ACT.Copy).then_inc(S["norm_hi"], 1)

                    act.wait_ge(S["act_own"], 2)
                    act.wait_ge(S["att_out"], 3)
                    for k in range(5):
                        split_mixed(k)
                    for p in range(PAIRS):
                        act.wait_ge(S["ret_mix"], 2 * TOKT * (p + 1))
                        act.activation(out_sb[:, 5 + p, :], o_ps[:], ACT.Copy).then_inc(S["ret_out"], 1)
                        layer_norm_sq(1 + p)
                        layer_norm_root(1 + p)
                        if p:
                            act.wait_ge(S["ret_gated"], p)
                            split_mixed(4 + p)
                    act.wait_ge(S["ln_done"], 3)
                    split_mixed(7)
                    for b in plan1[W_OUT:W_OUT + 4]:
                        k = 2 * (b.n - W_OUT)
                        evacuate(b, lambda m: out_sb[:, k + m, :])
                        norm_squares(act, 1, out_sb, sq_f, wait=(S["g_free"], plan1[W_OUT].t0), tiles=(k, k + 1))
                        round_block(act, plan1, b.n + 2)
                    norm_rooted(act, 1)
                    norm_squares(act, 2, x_sb, out_sb, wait=(S["x_done"], 0))
                    norm_rooted(act, 2)
                    split_hi(act, 2, 2, out_sb, S["normed"], 2 * KD)
                    for half in range(2):
                        first = plan1[UP[half]]
                        with act.Fori(0, 4) as i:
                            t = Turn(i, dn=2, du=4, dt=4)
                            for b in plan1[first.n:first.n + 2]:
                                j = b.n - first.n
                                for m in range(2):
                                    act.wait_ge(S["units"], t.u(b.u0 + m + 1))
                                    act.activation(tt[:, 2 * j + m, :], tile_of(b, m), ACT.Relu).then_inc(S["g_free"], 1)
                                for m in range(2):
                                    act.wait_ge(S["f_sq"], 16 * half + i * 4 + (2 * j + m + 1))
                                    act.activation(f_hi[:, i * 4 + (2 * j + m), :], tt[:, 2 * j + m, :],
                                                   ACT.Copy).then_inc(S["f_hi_s"], 1)
                                round_block(act, plan1, b.n + 2, t)

                        def down(t, dst):
                            for b in plan1[DOWN[half]:DOWN[half] + 4]:
                                if b.last:
                                    for m in range(2):
                                        act.wait_ge(S["units"], t.u(b.u0 + m + 1))
                                        act.activation(dst[:, t.i * 4 + (b.n - DOWN[half]) // 2 * 2 + m, :],
                                                       tile_of(b, m), ACT.Copy).then_inc(S["g_free"], 1)
                                round_block(act, plan1, b.n + 2, t)
                                if half and not b.last:
                                    k = t.i * 4 + (b.n - DOWN[half]) // 2 * 2 - 2
                                    if k >= 0:
                                        norm_squares(act, 3, out_sb, sq_f, wait=(S["part_done"], 0), tiles=(k, k + 1))

                        if half == 0:
                            with act.Fori(0, 2) as i:
                                down(Turn(i, dn=4, du=8, dt=4), out_sb)
                        else:
                            for i in range(2):
                                down(Turn(i, dn=4, du=8, dt=4), part)
                    norm_squares(act, 3, out_sb, sq_f, wait=(S["part_done"], 0), tiles=(KD - 2, KD - 1))
                    norm_rooted(act, 3)
                    round_next(act, 0, plan1)
                    norm_squares(act, 4, x_sb, sq_f, wait=(S["x_done"], KD))
                    norm_rooted(act, 4)
                    round_next(act, 1, plan1)

                @block.vector
                def _(dve):
                    own = [0]

                    def step(instruction):
                        own[0] += 1
                        instruction.then_inc(S["dve_own"], 1)
                        dve.wait_ge(S["dve_own"], own[0])

                    head_start(dve)
                    pre_norm_dve(dve, 0, 0, first_gain)
                    dve.wait_ge(S["par_in"], 16)

                    def tap(t):
                        q, j = t % 2, t // 2
                        acc = out_sb[:, 3 + q, :]
                        if j == 0:
                            ins = dve.tensor_scalar(acc, ca[:, q, 0:SEQ], conv_w[:, q, 0:1], conv_b[:, q:q + 1],
                                                    ALU.mult, ALU.add)
                        else:
                            dve.wait_ge(S["taps"], t - 1)
                            ins = dve.scalar_tensor_tensor(out=acc, in0=ca[:, q, j:j + SEQ],
                                                           scalar=conv_w[:, q, j:j + 1], in1=acc,
                                                           op0=ALU.mult, op1=ALU.add)
                        ins.then_inc(S["taps"], 1)

                    def rotary(j):
                        dve.wait_ge(S["rot_ps"], j + 1)
                        if j:
                            dve.wait_ge(S["rot_done"], j)
                        dve.tensor_tensor(rot_a[:, 0, :], rqk[:, j, :], cos_t[:], ALU.mult).then_inc(S["rot_cos"], 1)
                        step(dve.tensor_tensor(rot_a[:, 1, :], s_ps[j % 2][:], sin_t[:], ALU.mult))
                        dve.wait_ge(S["rot_cos"], j + 1)
                        dve.tensor_tensor(rqk[:, j, :], rot_a[:, 0, :], rot_a[:, 1, :],
                                          ALU.add).then_inc(S["rot_done"], 1)

                    def centre(j):
                        _, tiles, width = LN[j]
                        dve.wait_ge(S["ln_mean"], j + 1)
                        for m in tiles:
                            dve.scalar_tensor_tensor(out=out_sb[:, m, :], in0=t_ps[:], scalar=-1.0 / width,
                                                     in1=out_sb[:, m, :], op0=ALU.mult,
                                                     op1=ALU.add).then_inc(S["centred"], 1)

                    def layer_norm(j):
                        _, tiles, width = LN[j]
                        dve.wait_ge(S["ln_root"], j + 1)
                        step(dve.reciprocal(ln_rs(j), ln_rs(j)))
                        for q, m in enumerate(tiles):
                            step(dve.tensor_tensor(out_sb[:, m, :], out_sb[:, m, :], ln_rs(j), ALU.mult))
                            if j == 0:
                                ins = dve.tensor_scalar(out_sb[:, m, :], out_sb[:, m, :], ln_g[:, q:q + 1],
                                                        ln_b[:, q:q + 1], ALU.mult, ALU.add)
                            else:
                                ins = dve.tensor_tensor(out_sb[:, m, :], out_sb[:, m, :], rg[:, j - 1, :], ALU.mult)
                            ins.then_inc(S["ln_done"], 1)

                    per = -(-TAP_OPS // TAP_SLOTS)
                    for b in plan1[:N_IN]:
                        rest_block(dve, plan1, b.n + 2)
                        at_slot = b.n - (ROTARY_AT - TAP_SLOTS)
                        if at_slot == 0:
                            dve.wait_ge(S["g_free"], plan1[1].t0 + 2)
                            for j in range(2):
                                step(dve.memset(ca[:, j, 0:PAD], 0.0))
                            for q in range(2):
                                step(dve.tensor_tensor(ca[:, q, PAD:PAD + SEQ], ca[:, q, PAD:PAD + SEQ], cg[:, q, :],
                                                       ALU.mult))
                        if at_slot >= 0:
                            for t in range(at_slot * per, min(TAP_OPS, (at_slot + 1) * per)):
                                tap(t)
                        if b.n == ROTARY_AT:
                            centre(0)
                            dve.wait_ge(S["tab_in"], 64)
                        if ROTARY_AT <= b.n < ROTARY_AT + 3:
                            for j in range(2):
                                rotary(2 * (b.n - ROTARY_AT) + j)
                        if b.n == ROTARY_AT + 2:
                            layer_norm(0)

                    step(dve.memset(bias_t[0:CHUNK, :, SEQ - CHUNK:SEQ], MASKED))
                    steps = [(h, q) for h in range(ATT_HEADS) for q in range(TOKT)]
                    n = len(steps)
                    for s in range(n + 1):
                        p = s - 1
                        if s < n:
                            h, q = steps[s]
                            size = P * (q + 1)
                            row = probs[:, s % 4, 0:size]
                            dve.wait_ge(S["score_ps"], s + 1)
                            if s >= 4:
                                dve.wait_ge(S["turned_ps"], s - 3)
                            dve.scalar_tensor_tensor(out=row, in0=score_bank[s % 4][:, 0:size], scalar=HD ** -0.5,
                                                     in1=bias_t[:, h, SEQ - size:SEQ], op0=ALU.mult,
                                                     op1=ALU.add).then_inc(S["biased"], 1)
                        if s:
                            dve.wait_ge(S["exped"], s)
                            dve.reciprocal(tiny[:, 8 + p % 4:9 + p % 4], tiny[:, 4 + p % 4:5 + p % 4]).then_inc(
                                S["inverted"], 1)
                        if s < n:
                            dve.wait_ge(S["biased"], s + 1)
                            dve.tensor_reduce(tiny[:, s % 4:s % 4 + 1], row, AX_X, ALU.max,
                                              negate=True).then_inc(S["maxed"], 1)
                        if s:
                            size = P * (steps[p][1] + 1)
                            dve.wait_ge(S["inverted"], s)
                            dve.tensor_scalar(probs[:, p % 4, 0:size], probs[:, p % 4, 0:size],
                                              tiny[:, 8 + p % 4:9 + p % 4], None, ALU.mult).then_inc(S["scaled"], 1)

                    def rest_mixed(k):
                        dve.wait_ge(S["norm_hi"], KD + k + 1)
                        dve.tensor_tensor(h_lo[:, k, :], out_sb[:, k, :], h_hi[:, k, :].bitcast(F32),
                                          ALU.subtract).then_inc(S["h_ready"], 1)

                    for h in range(RET_HEADS):
                        if h >= 2:
                            dve.wait_ge(S["ret_mix"], TOKT * (h - 1))
                        for j in range(TOKT):
                            size = SEQ - P * j
                            dve.wait_ge(S["ret_ps"], TOKT * h + j + 1)
                            dve.scalar_tensor_tensor(out=ret_sc[:, h % 2, sc_off[j]:sc_off[j] + size],
                                                     in0=s_ps[j % 2][:, 0:size], scalar=HD ** -0.5,
                                                     in1=decay_t[:, h, 0:size], op0=ALU.mult,
                                                     op1=ALU.mult).then_inc(S["ret_sc_s"], 1)
                        if h >= 2 and h % 2 == 0:
                            centre(h // 2)
                        if h >= 2 and h % 2 == 1:
                            j = h // 2
                            dve.wait_ge(S["ln_root"], j + 1)
                            dve.reciprocal(ln_rs(j), ln_rs(j)).then_inc(S["ret_inv"], 1)
                    for k in range(5):
                        rest_mixed(k)
                    centre(PAIRS)
                    rest_mixed(5)
                    rest_mixed(6)
                    layer_norm(PAIRS)
                    rest_mixed(7)
                    for b in plan1[W_OUT:W_OUT + 4]:
                        rest_block(dve, plan1, b.n + 2)
                    post_norm_dve(dve, 1, gains["mix_post"], 0)
                    pre_norm_dve(dve, 2, 2, gains["mlp_pre"])
                    for half in range(2):
                        first = plan1[UP[half]]
                        with dve.Fori(0, 4) as i:
                            t = Turn(i, dn=2, du=4, dt=4)
                            for b in plan1[first.n:first.n + 2]:
                                j = b.n - first.n
                                for m in range(2):
                                    dve.wait_ge(S["g_free"], t.t(b.t0 + m + 1))
                                    dve.tensor_tensor(tt[:, 2 * j + m, :], tt[:, 2 * j + m, :], tt[:, 2 * j + m, :],
                                                      ALU.mult).then_inc(S["f_sq"], 1)
                                for m in range(2):
                                    at_tile = i * 4 + (2 * j + m)
                                    dve.wait_ge(S["f_hi_s"], 16 * half + i * 4 + (2 * j + m + 1))
                                    dve.tensor_tensor(f_lo[:, at_tile, :], tt[:, 2 * j + m, :],
                                                      f_hi[:, at_tile, :].bitcast(F32),
                                                      ALU.subtract).then_inc(S["f_ready"], 1)
                                rest_block(dve, plan1, b.n + 2, t)

                        if half == 0:
                            with dve.Fori(0, 2) as i:
                                for b in plan1[DOWN[0]:DOWN[0] + 4]:
                                    rest_block(dve, plan1, b.n + 2, Turn(i, dn=4, du=8, dt=4))
                        else:
                            for i in range(2):
                                t = Turn(i, dn=4, du=8, dt=4)
                                for b in plan1[DOWN[1]:DOWN[1] + 4]:
                                    rest_block(dve, plan1, b.n + 2, t)
                                    if b.last:
                                        for m in range(2):
                                            k = i * 4 + (b.n - DOWN[1]) // 2 * 2 + m
                                            dve.wait_ge(S["g_free"], t.t(b.t0 + m + 1))
                                            dve.tensor_tensor(out_sb[:, k, :], out_sb[:, k, :], part[:, k, :],
                                                              ALU.add).then_inc(S["part_done"], 1)
                    post_norm_dve(dve, 3, gains["mlp_post"], KD)
                    rest_next(dve, 0, n1)
                    norm_inverse(dve, 4)
                    rest_next(dve, 1, n1)

            clear_counts()

        g_hi = at("g_hi", [P, F2T, SEQ], F32R, FZ)
        g_lo = at("g_lo", [P, F2T, SEQ], F32R, FZ + 44)
        swi = at("swi", [P, 8, SEQ], F32, OZ)
        mk = at("mk", [P, XH, MEM], F32, FZ)
        mv = at("mv", [P, MEMT, SSM_W], F32, FZ + 4)
        u_sb = at("u_sb", [P, 4, SEQ], F32, FZ + 8)
        xq = at("xq", [P, XH, SEQ], F32, FZ + 16)
        q2 = at("q2", [P, 6, SEQ], F32, FZ + 24)
        k2 = at("k2", [P, 6, SEQ], F32, FZ + 36)
        v2 = at("v2", [P, TOKT, A2], F32, FZ + 48)
        mem_sb = at("mem_sb", [P, KD, MEM], F32, FZ + 60)
        mem_t = at("mem_t", [P, KD, MEM], F32, FZ + 68)
        m_hi = at("m_hi", [P, KD, MEM], F32R, 64)
        m_lo = at("m_lo", [P, KD, MEM], F32R, 80)
        bc = at("bc", [P, 4, STILES * SSM_G], F32, FZ + 60)
        bbar = at("bbar", [P, 4, STILES * SSM_G], F32, FZ + 64)
        b_mat = at("b_mat", [P, 4, 2, P], F32, FZ + 68)
        c_mat = at("c_mat", [P, 4, 2, P], F32, FZ + 72)
        b_turned = at("b_turned", [P, 2, 2 * P], F32, FZ + 76)
        time_t = at("time_t", [P, SEQ], F32, FZ + 78)
        trig = at("trig", [P, 2, 2, SEQ], F32, FZ + 80)
        phase = at("phase", [P, 2, SEQ], F32, FZ + 88)
        z_sc = at("z_sc", [P, 2, 2, SEQ], F32, FZ + 92)
        tmp2 = at("tmp2", [P, 2, SEQ], F32, FZ + 100)
        x_kept = nc.dram_tensor("x_kept", [P, KD, SEQ], F32, kind="Internal").ap()
        state = at("state", [P, 2, 2, SEQ], F32, 48)
        z_sin = at("z_sin", [P, 2, 2, SEQ], F32, 56)
        sp_ = at("state_par", [P, 24, STILES], F32, CZ + 5.5)
        t5a = at("t5a", [P, SLOTS, MEM], F32, FZ + 60)
        t5b = at("t5b", [P, 2, SLOTS, P], F32, FZ + 64)
        row2 = at("row2", [P, 3, MEM], F32, FZ + 68)
        row2_t = at("row2_t", [P, 2, MEM], F32, FZ + 71)
        peak = at("peak", [P, 80], F32, FZ + 73)
        score2 = [s_ps[0], s_ps[1], bank[3]]
        turn2_bank = [t_ps, o_ps]
        pv = at("pv", [P, 2, PATTERNS, SEQ], F32, 48)
        mb = at("mb", [P, 2, PATTERNS, SEQ], F32, FZ + 74)
        low = at("low", [P, SEQ], F32, FZ + 86)
        rden = at("rden", [P, SEQ], F32, FZ + 88)
        ya = at("ya", [P, 2, SEQ], F32, FZ + 90)
        yx = at("yx", [P, XH, SEQ], F32, FZ + 94)
        ys_hi = at("ys_hi", [P, 4, SEQ], F32R, FZ + 24)
        ys_lo = at("ys_lo", [P, 4, SEQ], F32R, FZ + 32)
        yx_hi = at("yx_hi", [P, 4, SEQ], F32R, FZ + 40)
        yx_lo = at("yx_lo", [P, 4, SEQ], F32R, FZ + 48)
        ya_hi = at("ya_hi", [P, 2, SEQ], F32R, FZ + 56)
        ya_lo = at("ya_lo", [P, 2, SEQ], F32R, FZ + 60)
        mg_hi = at("mg_hi", [P, KD, SEQ], F32R, FZ + 64)
        mg_lo = at("mg_lo", [P, KD, SEQ], F32R, FZ + 80)
        gate_a = at("gate_a", [P, 12, SEQ], F32, FZ)
        mix_sq = at("mix_sq", [P, KD, SEQ], F32, FZ)
        gate_b = at("gate_b", [P, 2, SEQ], F32, FZ + 96)

        def gate_tile(j, m):
            return gate_a[:, 2 * j + m, :] if j < 6 else gate_b[:, m, :]

        gains2 = {n: par2[:, 8 * i:8 * i + 8] for i, n in enumerate(("ffn1", "mem", "mix", "ffn2", "final"))}
        a_re, a_im, log_dt = (par2[:, 40 + 16 * i:56 + 16 * i] for i in range(3))
        ssm_d = par2[:, 88:92]
        names2 = ["par2_in", "mem_in", "bc_in", "time_in", "mat_zero", "mats", "turns_a", "turns_s", "fract", "fract_low", "phased",
                  "trig_s", "rotated", "summed", "scanned", "z_sin_s", "z_cos_s", "real_s", "x_kept_s", "x_back", "coef_a",
                  "coef_t", "bbar_s", "turned_b", "bt_s", "bu_ps", "bu_read", "state_s", "y_ps", "y_read", "y_s", "gelu_s",
                  "t5_in", "s2_ps", "s2_bias", "s2_max", "s2_exp", "s2_prob", "s2_turn_ps", "s2_turn", "s2_mix", "s2_out",
                  "mb_ps", "low_s", "weigh", "lowest", "pool_own", "pv_sum", "ya_s", "yx_s", "split2", "rest2", "prod2", "merged", "mg_hi_s", "mg_s",
                  "x2_done", "g2", "g2_hi", "g2_s", "final_s", "stored"]
        S.update({n: sem(n) for n in names2})
        n_up, n_down = F2T, F2T - 2

        first_q = AT2["q"]
        n_proj = AT2["gates"] - first_q
        slot_at = {}
        for s in range(STILES):
            slot_at[divmod(s * 2 * n_proj // STILES, 2)] = s

        def slot_of(b, m):
            half, left = divmod(m + 1, b.tiles // 2)
            return slot_at.get((b.n - first_q, half - 1)) if left == 0 else None

        def residues(g, i):
            if g == 0:
                return lambda a: a[:, i * P:(i + 1) * P]
            return lambda a: a.rearrange("p (m r) -> p r m", r=4)[:, i, :]

        steps2 = [(h, g, i) for h in range(SLOTS) for g in range(PATTERNS) for i in range(TOKT)]
        N2 = len(steps2)
        xsteps = [(h, i) for h in range(XH) for i in range(TOKT)]
        NX = len(xsteps)
        SUM_LATER = 3 * TOKT - 1
        YS_SPLIT = 6

        def keys_of(s):
            h, g, i = steps2[s]
            return (P * (i - 1), 2 * P) if g == 0 and i else (P * i, P)

        def bias_of(s):
            h, g, i = steps2[s]
            if g == 0:
                return t5a[:, h, :] if i else t5a[:, h, P:2 * P]
            return t5b[:, g - 1, h, :]

        with nc.Block() as block:
            @block.sync
            def _(sp):
                src = A["w"][DEPTH * n1:]
                sp.dma_start(par2[:, 0:92], A["par2"]).then_inc(S["par2_in"], 16)

                def load_loop(start, turns, body):
                    with sp.Fori(0, turns) as i:
                        for b in plan2[start:start + body]:
                            load_block(sp, src, b, Turn(i, dn=body))

                head_start(sp)
                load_loop(2, 10, 2)
                load_loop(AT2["ffn1_down"], 4, 4)
                load_block(sp, src, plan2[AT2["mk"]])
                load_block(sp, src, plan2[AT2["mk"] + 1])
                sp.wait_ge(S["units"], plan2[AT2["mk"] - 1].u1)
                sp.dma_start(mem_sb[:], A["mem"].rearrange("(k p) t -> p k t", p=P)).then_inc(S["mem_in"], 16)
                for b in plan2[AT2["mv"]:AT2["u"]]:
                    load_block(sp, src, b)
                sp.wait_ge(S["h_ready"], 2 * KD)
                sp.dma_start(bc[:], A["ssm_bc"]).then_inc(S["bc_in"], 16)
                sp.dma_start(time_t[:], A["c_time"]).then_inc(S["time_in"], 16)
                for b in plan2[AT2["u"]:AT2["u"] + 2]:
                    load_block(sp, src, b)
                sp.wait_ge(S["x2_done"], KD)
                sp.dma_start(x_kept, x_sb[:]).then_inc(S["x_kept_s"], 16)
                for b in plan2[AT2["q"]:AT2["gates"]]:
                    load_block(sp, src, b)
                load_block(sp, src, plan2[AT2["gates"]])
                load_block(sp, src, plan2[AT2["gates"] + 1])
                sp.wait_ge(S["y_s"], 4)
                sp.wait_ge(rows_out, 16 * PATTERNS)
                sp.dma_start(t5a[:], skewed(t5_rep[0], ROW, MEM)).then_inc(S["t5_in"], 16)
                for g in (1, 2):
                    sp.dma_start(t5b[:, g - 1], skewed(t5_rep[g], ROW, P)).then_inc(S["t5_in"], 16)
                sp.wait_ge(S["x_kept_s"], 16)
                sp.wait_ge(S["ya_s"], SLOTS)
                sp.dma_start(x_sb[:], x_kept).then_inc(S["x_back"], 16)
                load_loop_start = AT2["gates"] + 2
                for b in plan2[load_loop_start:AT2["ffn2_up"]]:
                    load_block(sp, src, b)
                load_loop(AT2["ffn2_up"], 11, 2)
                load_loop(AT2["ffn2_down"], 4, 4)
                for k in range(0, KD, 2):
                    sp.wait_ge(S["final_s"], k + 2)
                    sp.dma_start(outs[0].rearrange("(k p) t -> p k t", p=P)[:, k:k + 2],
                                 out_sb[:, k:k + 2, :]).then_inc(S["stored"], 16)
                sp.wait_ge(S["stored"], KD // 2 * 16)

            @block.gpsimd
            def _(pool):
                pool.wait_ge(S["h_ready"], 2 * KD)
                pool.memset(b_mat[:], 0.0).then_inc(S["mat_zero"], 1)
                pool.memset(c_mat[:], 0.0).then_inc(S["mat_zero"], 1)
                pool.wait_ge(S["mat_zero"], 2)
                pool.wait_ge(S["bbar_s"], 3)
                def mats(s):
                    b = s % 4
                    if s >= 4:
                        pool.wait_ge(S["turned_b"], s - 3)
                        pool.wait_ge(S["y_ps"], s - 3)
                    for q in range(2):
                        r = slice(SSM_N * q, SSM_N * q + SSM_N)
                        c = slice(32 * b + 16 * q, 32 * b + 16 * q + 16)
                        f = slice(SSM_G * s, SSM_G * s + SSM_G)
                        for j in range(2):
                            pool.tensor_copy(b_mat[r, b, j, c], bbar[r, j, f]).then_inc(S["mats"], 1)
                            pool.tensor_copy(c_mat[r, b, j, c], (bc[r, 2, f], bbar[r, 3, f])[j]).then_inc(S["mats"], 1)

                def whole_turns(s):
                    if s >= 2:
                        pool.wait_ge(S["fract"], s - 1)
                    to = phase[:, s % 2, :]
                    pool.tensor_scalar(to, time_t[:], sp_[:, 9, s:s + 1], MAGIC, ALU.mult,
                                       ALU.add).then_inc(S["turns_a"], 1)
                    pool.wait_ge(S["turns_a"], s + 1)
                    pool.tensor_scalar(to, to, MAGIC, None, ALU.subtract).then_inc(S["turns_s"], 1)

                def sines(s):
                    pool.wait_ge(S["scanned"], 2 * s + 2)
                    if s >= 2:
                        pool.wait_ge(S["state_s"], s - 1)
                    for w in range(2):
                        pool.tensor_tensor(z_sin[:, s % 2, w, :], z_sc[:, s % 2, 1 - w, :], trig[:, s % 2, 1, :],
                                           ALU.mult).then_inc(S["z_sin_s"], 1)

                pool.wait_ge(S["time_in"], 16)
                for s in range(2):
                    whole_turns(s)
                    pool.wait_ge(S["turns_s"], s + 1)
                    mats(s)
                    pool.wait_ge(S["mats"], 8 * (s + 1))
                pool.wait_ge(S["x_kept_s"], 16)
                pool.wait_ge(S["normed"], 3 * KD)
                for s in range(STILES):
                    if s + 2 < STILES:
                        mats(s + 2)
                        pool.wait_ge(S["mats"], 8 * (s + 3))
                    sines(s)
                    if s + 2 < STILES:
                        whole_turns(s + 2)
                        pool.wait_ge(S["z_sin_s"], 2 * s + 2)
                        pool.wait_ge(S["turns_s"], s + 3)
                pool.wait_ge(S["z_sin_s"], 2 * STILES)

                own = [0]

                def step(instruction):
                    own[0] += 1
                    instruction.then_inc(S["pool_own"], 1)
                    pool.wait_ge(S["pool_own"], own[0])

                for h in range(SLOTS):
                    to, m = pv[:, h % 2], mb[:, h % 2]
                    pool.wait_ge(S["lowest"], h + 1)
                    for g in range(PATTERNS):
                        pool.tensor_tensor(m[:, g, :], low[:], m[:, g, :], ALU.subtract).then_inc(S["low_s"], 1)
                        pool.wait_ge(S["low_s"], PATTERNS * h + g + 1)
                    for g in range(PATTERNS):
                        pool.wait_ge(S["weigh"], PATTERNS * h + g + 1)
                        step(pool.tensor_tensor(to[:, g, :], to[:, g, :], m[:, g, :], ALU.mult))
                        if g:
                            step(pool.tensor_tensor(to[:, 0, :], to[:, 0, :], to[:, g, :], ALU.add))
                    pool.sem_inc(S["pv_sum"], 1)

            @block.tensor
            def _(pe):
                def ffn(name, g_base, ready):
                    up, down = AT2[name + "_up"], AT2[name + "_down"]
                    for b in plan2[up:up + 2]:
                        product(pe, b, h_hi, h_lo, ready=ready if b.n == up else None)
                    with pe.Fori(0, 10) as i:
                        for b in plan2[up + 2:up + 4]:
                            product(pe, b, h_hi, h_lo, Turn(i, dn=2, du=4, dt=4))
                    pe.wait_ge(S["g2_s"], g_base + F2T + 2)
                    if name == "ffn1":
                        with pe.Fori(0, 2) as i:
                            for b in plan2[down:down + 8]:
                                product(pe, b, g_hi, g_lo, Turn(i, dn=8, du=16, dt=4))
                    else:
                        for i in range(2):
                            for b in plan2[down:down + 8]:
                                product(pe, b, g_hi, g_lo, Turn(i, dn=8, du=16, dt=4))
                                k = 4 * i + (b.n - down) // 4 * 2 - 2
                                if b.last and k >= 0:
                                    for q in range(2):
                                        norm_add(pe, 4, out_sb, k + q)

                ffn("ffn1", 0, 0)
                norm_total(pe, 1, mem_t, MEM)
                for b in plan2[AT2["mk"]:AT2["u"]]:
                    product(pe, b, m_hi, m_lo, ready=KD if b.n == AT2["mk"] else None, width=MEM)
                norm_total(pe, 2, out_sb)
                for b in plan2[AT2["u"]:AT2["q"]]:
                    product(pe, b, h_hi, h_lo, ready=2 * KD if b.n == AT2["u"] else None)

                def turn_b(s):
                    pe.wait_ge(S["mats"], 8 * (s + 1))
                    if s:
                        pe.wait_ge(S["bt_s"], s)
                    for j in range(2):
                        mm = pe.transpose(t_ps[:, P * j:P * j + P], b_mat[:, s % 4, j, :], ident[:])
                    mm.then_inc(S["turned_b"], 1)

                def scan_in(s):
                    pe.wait_ge(S["bt_s"], s + 1)
                    if s:
                        pe.wait_ge(S["bu_read"], s)
                    for j in range(2):
                        mm = pe.matmul(s_ps[j][:], b_turned[:, s % 2, P * j:P * j + P], u_sb[:, s // 4, :],
                                       start=True, stop=True)
                    mm.then_inc(S["bu_ps"], 1)

                def scan_out(s):
                    pe.wait_ge(S["real_s"], s + 1)
                    pe.wait_ge(S["state_s"], s + 1)
                    if s % 4 == 0:
                        pe.wait_ge(S["y_read"], s // 4) if s else pe.wait_ge(S["norm_inv"], 2)
                    for j in range(2):
                        mm = pe.matmul(o_ps[:], c_mat[:, s % 4, j, :], state[:, s % 2, j, :],
                                       start=s % 4 == 0 and j == 0, stop=s % 4 == 3 and j == 1)
                    mm.then_inc(S["y_ps"], 1)

                turn_b(0)
                pe.wait_ge(S["g_free"], plan2[AT2["q"]].t0)
                for b in plan2[AT2["q"]:AT2["gates"]]:
                    def between(m):
                        s = slot_of(b, m)
                        if s is not None:
                            scan_in(s)
                            if s >= 2:
                                scan_out(s - 2)
                            if s + 1 < STILES:
                                turn_b(s + 1)

                    g = b.n - AT2["v"]
                    product(pe, b, h_hi, h_lo, tokens=(lambda m: residues(g, m)) if b.kind == "tok" else None,
                            between=between)
                for s in (STILES - 2, STILES - 1):
                    scan_out(s)

                pe.wait_ge(S["g_free"], plan2[AT2["gates"]].t0)
                pe.wait_ge(S["bu_read"], STILES)

                def scores2(s):
                    h, g, i = steps2[s]
                    t, r = 2 * g + h // 2, slice(HD * (h % 2), HD * (h % 2) + HD)
                    k0, size = keys_of(s)
                    if s >= 3:
                        pe.wait_ge(S["s2_bias"], s - 2)
                    pe.matmul(score2[s % 3][:, 0:size], q2[r, t, P * i:P * i + P], k2[r, t, k0:k0 + size],
                              start=True, stop=True).then_inc(S["s2_ps"], 1)

                def turn2(s):
                    size = keys_of(s)[1]
                    pe.wait_ge(S["s2_exp"], s + 1)
                    if s >= 2:
                        pe.wait_ge(S["s2_turn"], s - 1)
                    for j in range(size // P):
                        mm = pe.transpose(turn2_bank[s % 2][:, P * j:P * j + P], row2[:, s % 3, P * j:P * j + P],
                                          ident[:])
                    mm.then_inc(S["s2_turn_ps"], 1)

                def mix2(s):
                    h, g, i = steps2[s]
                    k0, size = keys_of(s)
                    hg = s // TOKT
                    pe.wait_ge(S["s2_turn"], s + 1)
                    if i == 0 and hg >= 2:
                        pe.wait_ge(S["s2_out"], 2 * (hg - 1))
                    c = slice(P * i, P * i + P)
                    v_cols = slice(2 * P * g + HD * h, 2 * P * g + HD * h + HD)
                    for j in range(size // P):
                        last = j == size // P - 1
                        kt = k0 // P + j
                        pe.matmul(bank[hg % 2][0:HD, c], v2[:, kt, v_cols], row2_t[:, s % 2, P * j:P * j + P],
                                  start=j == 0, stop=last)
                        pe.matmul(bank[hg % 2][HD:P, c], ones[:, 0:HD], row2_t[:, s % 2, P * j:P * j + P],
                                  start=j == 0, stop=last)
                    if i == 0 and hg:
                        pe.wait_ge(S["s2_out"], 2 * hg)
                    pe.matmul(bank[2][:, c], peak[:, s:s + 1].broadcast_to([P, P]), ident[:],
                              start=True, stop=True).then_inc(S["s2_mix"], 1)

                pe.wait_ge(S["y_read"], 4)
                for s in range(N2 + 3):
                    if s < N2:
                        scores2(s)
                    if 2 <= s <= N2 + 1:
                        turn2(s - 2)
                    if s >= 3:
                        mix2(s - 3)

                def scores_x(s):
                    h, i = xsteps[s]
                    n = N2 + s
                    pe.wait_ge(S["s2_bias"], n - 2)
                    pe.matmul(score2[n % 3][:, 0:MEM], xq[:, h, P * i:P * i + P], mk[:, h, :],
                              start=True, stop=True).then_inc(S["s2_ps"], 1)

                def turn_x(s):
                    n = N2 + s
                    pe.wait_ge(S["s2_prob"], s + 1)
                    pe.wait_ge(S["s2_turn"], n - 1)
                    for j in range(MEMT):
                        mm = pe.transpose(turn2_bank[n % 2][:, P * j:P * j + P], row2[:, n % 3, P * j:P * j + P],
                                          ident[:])
                    mm.then_inc(S["s2_turn_ps"], 1)

                def mix_x(s):
                    h, i = xsteps[s]
                    n = N2 + s
                    pe.wait_ge(S["s2_turn"], n + 1)
                    if i == 0:
                        if h < 2:
                            pe.wait_ge(S["s2_out"], 2 * SLOTS * PATTERNS)
                        else:
                            pe.wait_ge(S["yx_s"], h - 1)
                    for j in range(MEMT):
                        mm = pe.matmul(bank[h % 2][:, P * i:P * i + P], mv[:, j, P * h:P * h + P],
                                       row2_t[:, n % 2, P * j:P * j + P], start=j == 0, stop=j == MEMT - 1)
                    mm.then_inc(S["s2_mix"], 1)

                for s in range(NX + 3):
                    if s < NX:
                        scores_x(s)
                    if 2 <= s <= NX + 1:
                        turn_x(s - 2)
                    if s >= 3:
                        mix_x(s - 3)

                pe.wait_ge(S["rest2"], 4)
                pe.wait_ge(S["s2_exp"], N2 + NX)
                pe.wait_ge(S["yx_s"], XH)
                sources = {"glu_b": (ys_hi, ys_lo), "glu_a": (ys_hi, ys_lo), "attn_up": (ya_hi, ya_lo),
                           "xattn_up": (yx_hi, yx_lo)}
                for b in plan2[AT2["gates"]:AT2["w_out2"]]:
                    if b.n == AT2["gates"] + GATES.index("attn_up"):
                        pe.wait_ge(S["rest2"], 10)
                    hi, lo = sources.get(GATES[(b.n - AT2["gates"]) % 7], (h_hi, h_lo))
                    product(pe, b, hi, lo)
                pe.wait_ge(S["mg_s"], KD)
                for b in plan2[AT2["w_out2"]:AT2["ffn2_up"]]:
                    product(pe, b, mg_hi, mg_lo)
                    for k in range(2 * (b.n - AT2["w_out2"]) - 2, 2 * (b.n - AT2["w_out2"])):
                        if k >= 0:
                            norm_add(pe, 3, mix_sq, k)
                norm_total(pe, 3, mix_sq, done=KD - 2)
                ffn("ffn2", F2T + 2, 3 * KD)
                norm_total(pe, 4, out_sb, done=KD - 2)

            @block.scalar
            def _(act):
                def evacuate(b, dst, func=ACT.Copy, scale=1.0, width=SEQ, m0=0):
                    for m in range(b.tiles):
                        act.wait_ge(S["units"], b.u0 + (m + 1 if b.kind == "feat" else m // 2 * 2 + 2))
                        act.activation(dst(m), tile_of(b, m, width), func, scale=scale).then_inc(S["g_free"], 1)

                def ffn(name, g_base):
                    up, down = AT2[name + "_up"], AT2[name + "_down"]
                    s_base = 0 if name == "ffn1" else F2T + 2
                    with act.Fori(0, 11) as i:
                        t = Turn(i, dn=2, du=4, dt=4)
                        for b in plan2[up:up + 2]:
                            j = b.n - up
                            if j == 0:
                                act.wait_ge(S["g2_s"], s_base + 2 + i * 2)
                            for m in range(2):
                                act.wait_ge(S["units"], t.u(b.u0 + m + 1))
                                act.activation(swi[:, 2 * j + m, :], tile_of(b, m),
                                               (ACT.Silu, ACT.Copy)[j]).then_inc(S["g_free"], 1)
                            if j:
                                for m in range(2):
                                    act.wait_ge(S["g2"], g_base + i * 2 + (m + 1))
                                    act.activation(g_hi[:, i * 2 + m, :], swi[:, m, :],
                                                   ACT.Copy).then_inc(S["g2_hi"], 1)
                            round_block(act, plan2, b.n + 2, t)

                    def down_pair(i):
                        for q in range(2):
                            for b in plan2[down + 4 * q:down + 4 * q + 4]:
                                t = Turn(i, dn=8, du=16, dt=4)
                                if b.last:
                                    for m in range(2):
                                        act.wait_ge(S["units"], t.u(b.u0 + m + 1))
                                        act.activation(part[:, i * 4 + (2 * q + m), :], tile_of(b, m), ACT.Copy,
                                                       scale=0.5).then_inc(S["g_free"], 1)
                                round_block(act, plan2, b.n + 2, t, whole=b.n + 2 >= down + 8)
                                if name == "ffn2" and b.n == down + 4 * q + 1:
                                    k = 4 * i + 2 * q - 2
                                    if k >= 0:
                                        norm_squares(act, 4, x_sb, out_sb, wait=(S["x2_done"], 2 * KD), tiles=(k, k + 1))

                    if name == "ffn1":
                        with act.Fori(0, 2) as i:
                            down_pair(i)
                    else:
                        for i in range(2):
                            down_pair(i)

                head_start(act)
                split_hi(act, 0, 0, out_sb, S["normed"], 0)
                ffn("ffn1", 0)
                act.wait_ge(S["mem_in"], 16)
                norm_squares(act, 1, mem_sb, mem_t)
                norm_rooted(act, 1, MEM)
                split_hi(act, 1, 1, mem_t, S["normed"], KD, hi=m_hi)
                for b in plan2[AT2["mk"]:AT2["u"]]:
                    if b.kind == "feat":
                        evacuate(b, lambda m: mk[:, 2 * (b.n - AT2["mk"]) + m, :], width=MEM)
                    else:
                        evacuate(b, lambda m: mv[:, m, 256 * (b.n - AT2["mv"]):256 * (b.n - AT2["mv"]) + 256])
                    round_block(act, plan2, b.n + 2)
                norm_squares(act, 2, x_sb, out_sb, wait=(S["x2_done"], 0))
                norm_rooted(act, 2)
                act.wait_ge(S["units"], plan2[AT2["u"] - 1].u1)
                split_hi(act, 2, 2, out_sb, S["normed"], 2 * KD)

                act.wait_ge(S["par2_in"], 16)
                act.activation(sp_[:, 0, :], log_dt, ACT.Exp).then_inc(S["coef_a"], 1)
                act.wait_ge(S["coef_t"], 1)
                act.activation(sp_[:, 2, :], sp_[:, 1, :], ACT.Exp).then_inc(S["coef_a"], 1)
                act.wait_ge(S["coef_t"], 2)
                act.activation(sp_[:, 5, :], sp_[:, 4, :], ACT.Abs).then_inc(S["coef_a"], 1)
                act.wait_ge(S["coef_a"], 3)
                act.activation(sp_[:, 6, :], sp_[:, 4, :], ACT.Sin).then_inc(S["coef_a"], 1)
                act.activation(sp_[:, 7, :], sp_[:, 5, :], ACT.Sin, scale=-1.0,
                               bias=quarter[:, 0:1]).then_inc(S["coef_a"], 1)
                for b in plan2[AT2["u"]:AT2["q"]]:
                    evacuate(b, lambda m: u_sb[:, 2 * (b.n - AT2["u"]) + m, :])
                    round_block(act, plan2, b.n + 2)

                def waves(s):
                    act.wait_ge(S["phased"], s + 1)
                    if s >= 2:
                        act.wait_ge(S["z_cos_s"], 2 * s - 2)
                    cos, sin = trig[:, s % 2, 0, :], trig[:, s % 2, 1, :]
                    act.activation(cos, sin, ACT.Abs).then_inc(S["trig_s"], 1)
                    act.wait_ge(S["trig_s"], 3 * s + 1)
                    act.activation(sin, sin, ACT.Sin, scale=BELOW_2PI).then_inc(S["trig_s"], 1)
                    act.activation(cos, cos, ACT.Sin, scale=-BELOW_2PI, bias=quarter[:, 0:1]).then_inc(S["trig_s"], 1)

                def copy_b(s):
                    act.wait_ge(S["turned_b"], s + 1)
                    if s >= 2:
                        act.wait_ge(S["bu_ps"], s - 1)
                    act.activation(b_turned[:, s % 2, :], t_ps[:, 0:2 * P], ACT.Copy).then_inc(S["bt_s"], 1)

                copy_b(0)
                waves(0)
                due = None
                for b in plan2[AT2["q"]:AT2["gates"]]:
                    for m in range(b.tiles):
                        if due is not None and (m + 1) % (b.tiles // 2) == 0:
                            waves(due)
                            due = None
                        act.wait_ge(S["units"], b.u0 + (m + 1 if b.kind == "feat" else m // 2 * 2 + 2))
                        src = tile_of(b, m)
                        if b.n < AT2["v"]:
                            to, t = (q2, 2 * (b.n - AT2["q"]) + m) if b.n < AT2["k"] else (k2, 2 * (b.n - AT2["k"]) + m)
                            r = (1, 4, 4)[t // 2]
                            dst = to[:, t, :].rearrange("p (r m) -> p m r", r=r) if r > 1 else to[:, t, :]
                            src = src.rearrange("p (m r) -> p m r", r=r) if r > 1 else src
                        elif b.n < AT2["xq"]:
                            dst = v2[:, m, 256 * (b.n - AT2["v"]):256 * (b.n - AT2["v"]) + 256]
                        else:
                            dst = xq[:, 2 * (b.n - AT2["xq"]) + m, :]
                        act.activation(dst, src, ACT.Copy).then_inc(S["g_free"], 1)
                        s = slot_of(b, m)
                        if s is not None and s + 1 < STILES:
                            copy_b(s + 1)
                            due = s + 1
                    round_block(act, plan2, b.n + 2)
                for a in range(4):
                    act.wait_ge(S["y_s"], a + 1)
                    act.activation(u_sb[:, a, :], u_sb[:, a, :], ACT.Gelu_apprx_tanh).then_inc(S["gelu_s"], 1)

                def copy_turned(n, size):
                    act.wait_ge(S["s2_turn_ps"], n + 1)
                    if n >= 2:
                        act.wait_ge(S["s2_mix"], n - 1)
                    act.activation(row2_t[:, n % 2, 0:size], turn2_bank[n % 2][:, 0:size], ACT.Copy).then_inc(S["s2_turn"], 1)

                def copy_mixed(hg):
                    g = hg % PATTERNS
                    act.wait_ge(S["s2_mix"], TOKT * (hg + 1))
                    if hg >= 2 * PATTERNS:
                        act.wait_ge(S["ya_s"], hg // PATTERNS - 1)
                    r = (1, 4, 4)[g]
                    for dst, src in ((pv, bank[hg % 2]), (mb, bank[2])):
                        d, s_ = dst[:, hg // PATTERNS % 2, g, :], src[:]
                        if r > 1:
                            d, s_ = d.rearrange("p (m r) -> p m r", r=r), s_.rearrange("p (r m) -> p m r", r=r)
                        act.activation(d, s_, ACT.Copy).then_inc(S["s2_out"], 1)

                def weights_of(h):
                    for g in range(PATTERNS):
                        act.wait_ge(S["low_s"], PATTERNS * h + g + 1)
                        m = mb[:, h % 2, g, :]
                        act.activation(m, m, ACT.Exp).then_inc(S["weigh"], 1)

                for s in range(N2 + 3):
                    if s < N2:
                        size = keys_of(s)[1]
                        act.wait_ge(S["s2_max"], s + 1)
                        act.activation(row2[:, s % 3, 0:size], row2[:, s % 3, 0:size], ACT.Exp,
                                       bias=peak[:, s:s + 1]).then_inc(S["s2_exp"], 1)
                    if 2 <= s <= N2 + 1:
                        copy_turned(s - 2, keys_of(s - 2)[1])
                    if s >= 3 and (s - 2) % TOKT == 0:
                        hg = (s - 2) // TOKT - 1
                        if hg and hg % PATTERNS == 0:
                            weights_of(hg // PATTERNS - 1)
                        copy_mixed(hg)
                for s in range(NX + 3):
                    if s < NX:
                        n = N2 + s
                        act.wait_ge(S["s2_max"], n + 1)
                        act.activation(row2[:, n % 3, :], score2[n % 3][:, 0:MEM], ACT.Exp, scale=P ** -0.5,
                                       bias=peak[:, N2 + s:N2 + s + 1],
                                       accum_out=peak[:, 64 + s % 2:65 + s % 2]).then_inc(S["s2_exp"], 1)
                    if s == TOKT:
                        weights_of(SLOTS - 1)
                    if 2 <= s <= NX + 1:
                        copy_turned(N2 + s - 2, MEM)
                    if s >= 3 and (s - 2) % TOKT == 0:
                        h = (s - 2) // TOKT - 1
                        act.wait_ge(S["s2_mix"], N2 + TOKT * (h + 1))
                        act.activation(yx[:, h, :], bank[h % 2][:], ACT.Copy).then_inc(S["yx_s"], 1)
                    if YS_SPLIT <= s < YS_SPLIT + 4:
                        act.wait_ge(S["s2_mix"], N2)
                        act.wait_ge(S["gelu_s"], 4)
                        act.activation(ys_hi[:, s - YS_SPLIT, :], u_sb[:, s - YS_SPLIT, :],
                                       ACT.Copy).then_inc(S["split2"], 1)

                act.wait_ge(S["ya_s"], SLOTS)
                act.wait_ge(S["yx_s"], XH)
                for src, dst, tiles in ((yx, yx_hi, 4), (ya, ya_hi, 2)):
                    for k in range(tiles):
                        act.activation(dst[:, k, :], src[:, k, :], ACT.Copy).then_inc(S["split2"], 1)
                act.wait_ge(S["rest2"], 10)
                for b in plan2[AT2["gates"]:AT2["w_out2"]]:
                    p, j = divmod(b.n - AT2["gates"], 7)
                    func = ACT.Sigmoid if GATES[j] in ("glu_b", "gate0", "gate1", "gate2") else ACT.Copy
                    evacuate(b, lambda m: gate_tile(j, m), func)
                    if j == 6:
                        for m in range(2):
                            act.wait_ge(S["merged"], 2 * p + m + 1)
                            act.activation(mg_hi[:, 2 * p + m, :], gate_tile(1, m), ACT.Copy).then_inc(S["mg_hi_s"], 1)
                    round_block(act, plan2, b.n + 2)
                for b in plan2[AT2["w_out2"]:AT2["ffn2_up"]]:
                    k = 2 * (b.n - AT2["w_out2"])
                    if k:
                        norm_squares(act, 3, x_sb, mix_sq, wait=(S["x2_done"], KD), tiles=(k - 2, k - 1))
                    evacuate(b, lambda m: part[:, k + m, :])
                    round_block(act, plan2, b.n + 2)
                norm_squares(act, 3, x_sb, mix_sq, wait=(S["x2_done"], KD), tiles=(KD - 2, KD - 1))
                norm_rooted(act, 3)
                split_hi(act, 3, 3, out_sb, S["normed"], 3 * KD)
                ffn("ffn2", F2T)
                norm_squares(act, 4, x_sb, out_sb, wait=(S["x2_done"], 2 * KD), tiles=(KD - 2, KD - 1))
                norm_rooted(act, 4)

            @block.vector
            def _(dve):
                own = [0]

                def step(instruction):
                    own[0] += 1
                    instruction.then_inc(S["dve_own"], 1)
                    dve.wait_ge(S["dve_own"], own[0])

                def add_part(k):
                    dve.tensor_tensor(x_sb[:, k, :], x_sb[:, k, :], part[:, k, :], ALU.add).then_inc(S["x2_done"], 1)

                def ffn(name, g_base):
                    up, down = AT2[name + "_up"], AT2[name + "_down"]
                    dve.sem_inc(S["g2_s"], 2)
                    with dve.Fori(0, 11) as i:
                        t = Turn(i, dn=2, du=4, dt=4)
                        for b in plan2[up:up + 2]:
                            if b.n > up:
                                for m in range(2):
                                    dve.wait_ge(S["g_free"], t.t(b.t0 + m + 1))
                                    dve.tensor_tensor(swi[:, m, :], swi[:, m, :], swi[:, 2 + m, :],
                                                      ALU.mult).then_inc(S["g2"], 1)
                                for m in range(2):
                                    dve.wait_ge(S["g2_hi"], g_base + i * 2 + (m + 1))
                                    dve.tensor_tensor(g_lo[:, i * 2 + m, :], swi[:, m, :],
                                                      g_hi[:, i * 2 + m, :].bitcast(F32),
                                                      ALU.subtract).then_inc(S["g2_s"], 1)
                            rest_block(dve, plan2, b.n + 2, t)

                    def down_pair(i):
                        for q in range(2):
                            for b in plan2[down + 4 * q:down + 4 * q + 4]:
                                t = Turn(i, dn=8, du=16, dt=4)
                                rest_block(dve, plan2, b.n + 2, t, whole=b.n + 2 >= down + 8)
                                if b.last:
                                    for m in range(2):
                                        k = i * 4 + (2 * q + m)
                                        dve.wait_ge(S["g_free"], t.t(b.t0 + m + 1))
                                        add_part(k)

                    if name == "ffn1":
                        with dve.Fori(0, 2) as i:
                            down_pair(i)
                    else:
                        for i in range(2):
                            down_pair(i)

                head_start(dve)
                pre_norm_dve(dve, 0, 0, first_gain)
                dve.wait_ge(S["par2_in"], 16)
                ffn("ffn1", 0)
                pre_norm_dve(dve, 1, 1, gains2["mem"], MEM, mem_sb, mem_t, m_hi, m_lo)
                for b in plan2[AT2["mk"]:AT2["u"]]:
                    rest_block(dve, plan2, b.n + 2)
                pre_norm_dve(dve, 2, 2, gains2["mix"])

                row = lambda i: sp_[:, i, :]
                dve.wait_ge(S["coef_a"], 1)
                step(dve.tensor_tensor(row(3), a_im, row(0), ALU.mult))
                dve.tensor_tensor(row(1), a_re, row(0), ALU.mult).then_inc(S["coef_t"], 1)
                step(dve.tensor_scalar(row(8), row(3), 1.0 / TWO_PI, MAGIC, ALU.mult, ALU.add))
                step(dve.tensor_scalar(row(8), row(8), MAGIC, None, ALU.subtract))
                for c in (PI2_A, PI2_B, PI2_C):
                    step(dve.scalar_tensor_tensor(out=row(3), in0=row(8), scalar=-c, in1=row(3), op0=ALU.mult,
                                                  op1=ALU.add))
                dve.tensor_scalar(row(4), row(3), BELOW_PI, -BELOW_PI, ALU.min, ALU.max).then_inc(S["coef_t"], 1)
                step(dve.tensor_scalar(row(9), row(3), 1.0 / TWO_PI, None, ALU.mult))
                step(dve.tensor_scalar(row(10), row(9), MAGIC / 2 ** 14, None, ALU.add))
                step(dve.tensor_scalar(row(10), row(10), MAGIC / 2 ** 14, None, ALU.subtract))
                step(dve.tensor_tensor(row(11), row(9), row(10), ALU.subtract))
                dve.wait_ge(S["coef_a"], 5)
                step(dve.tensor_tensor(row(12), row(2), row(7), ALU.mult))
                step(dve.tensor_scalar(row(12), row(12), 1.0, None, ALU.subtract))
                step(dve.tensor_tensor(row(13), row(2), row(6), ALU.mult))
                step(dve.tensor_tensor(row(14), a_re, a_re, ALU.mult))
                step(dve.tensor_tensor(row(15), a_im, a_im, ALU.mult))
                step(dve.tensor_tensor(row(14), row(14), row(15), ALU.add))
                step(dve.reciprocal(row(14), row(14)))
                step(dve.tensor_tensor(row(16), row(12), a_re, ALU.mult))
                step(dve.tensor_tensor(row(17), row(13), a_im, ALU.mult))
                step(dve.tensor_tensor(row(16), row(16), row(17), ALU.add))
                step(dve.tensor_tensor(row(18), row(13), a_re, ALU.mult))
                step(dve.tensor_tensor(row(19), row(12), a_im, ALU.mult))
                step(dve.tensor_tensor(row(18), row(18), row(19), ALU.subtract))
                step(dve.tensor_tensor(row(16), row(16), row(14), ALU.mult))
                step(dve.tensor_tensor(row(18), row(18), row(14), ALU.mult))
                dve.wait_ge(S["bc_in"], 16)
                by_state = lambda a: a.rearrange("p (s h) -> p s h", h=SSM_G)
                wide = lambda i: sp_[:, i, :].unsqueeze(2).broadcast_to([P, STILES, SSM_G])
                b_re, b_im = by_state(bc[:, 0, :]), by_state(bc[:, 1, :])
                for out_i, x1, x2, op in ((0, b_re, b_im, ALU.subtract), (1, b_im, b_re, ALU.add)):
                    step(dve.tensor_tensor(by_state(bbar[:, out_i, :]), wide(16), x1, ALU.mult))
                    step(dve.tensor_tensor(by_state(bbar[:, 2, :]), wide(18), x2, ALU.mult))
                    dve.tensor_tensor(bbar[:, out_i, :], bbar[:, out_i, :], bbar[:, 2, :], op).then_inc(S["bbar_s"], 1)
                    dve.wait_ge(S["bbar_s"], out_i + 1)
                dve.tensor_scalar(bbar[:, 3, :], bc[:, 3, :], -1.0, None, ALU.mult).then_inc(S["bbar_s"], 1)
                for b in plan2[AT2["u"]:AT2["q"]]:
                    rest_block(dve, plan2, b.n + 2)

                def phase_step(s, part):
                    if s == STILES:
                        return
                    to = trig[:, s % 2, 1, :]
                    if part == 0:
                        dve.wait_ge(S["turns_s"], s + 1)
                        if s >= 2:
                            dve.wait_ge(S["z_sin_s"], 2 * s - 2)
                        dve.scalar_tensor_tensor(out=to, in0=time_t[:], scalar=sp_[:, 10, s:s + 1],
                                                 in1=phase[:, s % 2, :], op0=ALU.mult,
                                                 op1=ALU.subtract).then_inc(S["fract"], 1)
                    elif part == 1:
                        dve.wait_ge(S["fract"], s + 1)
                        dve.scalar_tensor_tensor(out=to, in0=time_t[:], scalar=sp_[:, 11, s:s + 1], in1=to,
                                                 op0=ALU.mult, op1=ALU.add).then_inc(S["fract_low"], 1)
                    else:
                        dve.wait_ge(S["fract_low"], s + 1)
                        dve.tensor_scalar(to, to, 0.5, -0.5, ALU.min, ALU.max).then_inc(S["phased"], 1)

                def state_sum(s):
                    for w, op, signal in ((0, ALU.subtract, "real_s"), (1, ALU.add, "state_s")):
                        dve.wait_ge(S["z_sin_s"], 2 * s + w + 1)
                        dve.wait_ge(S["z_cos_s"], 2 * s + w + 1)
                        dve.tensor_tensor(state[:, s % 2, w, :], state[:, s % 2, w, :], z_sin[:, s % 2, w, :],
                                          op).then_inc(S[signal], 1)

                def scan(s, rest=None):
                    if s >= 6 and s % 4 == 2:
                        skip(s // 4 - 1)
                    dve.wait_ge(S["trig_s"], 3 * s + 3)
                    dve.wait_ge(S["bu_ps"], s + 1)
                    if s >= 2:
                        dve.wait_ge(S["z_sin_s"], 2 * s - 2)
                        dve.wait_ge(S["z_cos_s"], 2 * s - 2)
                    if s:
                        dve.wait_ge(S["summed"], 2 * s)
                    cos, sin = trig[:, s % 2, 0, :], trig[:, s % 2, 1, :]
                    br, bi = s_ps[0][:], s_ps[1][:]
                    z = [z_sc[:, s % 2, w, :] for w in range(2)]
                    dve.tensor_tensor(z[0], br, cos, ALU.mult).then_inc(S["rotated"], 1)
                    dve.tensor_tensor(z[1], bi, cos, ALU.mult).then_inc(S["rotated"], 1)
                    dve.tensor_tensor(tmp2[:, 0, :], bi, sin, ALU.mult).then_inc(S["rotated"], 1)
                    dve.tensor_tensor(tmp2[:, 1, :], br, sin, ALU.mult).then_inc(S["bu_read"], 1)
                    if s:
                        state_sum(s - 1)
                    phase_step(s + 1, 0)
                    dve.wait_ge(S["rotated"], 3 * s + 3)
                    dve.wait_ge(S["bu_read"], s + 1)
                    dve.tensor_tensor(z[0], z[0], tmp2[:, 0, :], ALU.add).then_inc(S["summed"], 1)
                    dve.tensor_tensor(z[1], z[1], tmp2[:, 1, :], ALU.subtract).then_inc(S["summed"], 1)
                    phase_step(s + 1, 1)
                    decay = sp_[:, 2, s:s + 1].broadcast_to([P, SEQ])
                    for w in range(2):
                        dve.wait_ge(S["summed"], 2 * s + w + 1)
                        dve.tensor_tensor_scan(z[w], decay, z[w], 0.0, ALU.mult, ALU.add).then_inc(S["scanned"], 1)
                        if w == 0:
                            phase_step(s + 1, 2)
                    if rest is not None:
                        rest_block(dve, plan2, rest)
                    if s == 0:
                        dve.wait_ge(S["x_kept_s"], 16)
                    if s >= 2:
                        dve.wait_ge(S["y_ps"], s - 1)
                    for w in range(2):
                        dve.wait_ge(S["scanned"], 2 * s + w + 1)
                        dve.tensor_tensor(state[:, s % 2, w, :], z[w], cos, ALU.mult).then_inc(S["z_cos_s"], 1)

                def skip(a):
                    dve.wait_ge(S["y_ps"], 4 * a + 4)
                    dve.scalar_tensor_tensor(out=u_sb[:, a, :], in0=u_sb[:, a, :], scalar=ssm_d[:, a:a + 1], in1=o_ps[:],
                                             op0=ALU.mult, op1=ALU.add).then_inc(S["y_read"], 1)
                    dve.wait_ge(S["y_read"], a + 1)
                    dve.sem_inc(S["y_s"], 1)

                dve.wait_ge(S["time_in"], 16)
                for part_ in range(3):
                    phase_step(0, part_)
                for b in plan2[AT2["q"]:AT2["gates"]]:
                    for m in range(b.tiles):
                        s, last_tile = slot_of(b, m), m == b.tiles - 1
                        if s is not None:
                            scan(s, rest=b.n + 2 if last_tile else None)
                        elif last_tile:
                            rest_block(dve, plan2, b.n + 2)
                state_sum(STILES - 1)
                skip(3)

                dve.wait_ge(S["t5_in"], 48)

                def lowest(h):
                    dve.wait_ge(S["s2_out"], 2 * PATTERNS * (h + 1))
                    if h:
                        dve.wait_ge(S["low_s"], PATTERNS * h)
                    step(dve.tensor_tensor(low[:], mb[:, h % 2, 0, :], mb[:, h % 2, 1, :], ALU.min))
                    dve.tensor_tensor(low[:], low[:], mb[:, h % 2, 2, :], ALU.min).then_inc(S["lowest"], 1)

                def combined(h):
                    dve.wait_ge(S["pv_sum"], h + 1)
                    step(dve.reciprocal(rden[0:HD, :], pv[HD:P, h % 2, 0, :]))
                    r = slice(HD * (h % 2), HD * (h % 2) + HD)
                    dve.tensor_tensor(ya[r, h // 2, :], pv[0:HD, h % 2, 0, :], rden[0:HD, :],
                                      ALU.mult).then_inc(S["ya_s"], 1)
                    dve.wait_ge(S["ya_s"], h + 1)

                for s in range(N2 + 1):
                    if s < N2:
                        size = keys_of(s)[1]
                        row_ = row2[:, s % 3, 0:size]
                        dve.wait_ge(S["s2_ps"], s + 1)
                        if s >= 3:
                            dve.wait_ge(S["s2_turn_ps"], s - 2)
                        dve.scalar_tensor_tensor(out=row_, in0=score2[s % 3][:, 0:size], scalar=HD ** -0.5,
                                                 in1=bias_of(s), op0=ALU.mult, op1=ALU.add).then_inc(S["s2_bias"], 1)
                        dve.wait_ge(S["s2_bias"], s + 1)
                        dve.tensor_reduce(peak[:, s:s + 1], row_, AX_X, ALU.max, negate=True).then_inc(S["s2_max"], 1)
                    h, at_step = divmod(s - 4, TOKT * PATTERNS)
                    if h >= 0 and at_step == TOKT * PATTERNS - 1:
                        lowest(h)
                    h, at_step = divmod(s - SUM_LATER, TOKT * PATTERNS)
                    if h >= 0 and at_step == TOKT * PATTERNS - 1:
                        combined(h)

                def x_scaled(s):
                    n = N2 + s
                    dve.wait_ge(S["s2_exp"], n + 1)
                    step(dve.reciprocal(peak[:, 66 + s % 2:67 + s % 2], peak[:, 64 + s % 2:65 + s % 2]))
                    dve.tensor_scalar(row2[:, n % 3, :], row2[:, n % 3, :], peak[:, 66 + s % 2:67 + s % 2], None,
                                      ALU.mult).then_inc(S["s2_prob"], 1)

                for s in range(NX + 1):
                    n = N2 + s
                    if s == 3:
                        lowest(SLOTS - 1)
                    if s == SUM_LATER:
                        combined(SLOTS - 1)
                    if s < NX:
                        dve.wait_ge(S["s2_ps"], n + 1)
                        dve.wait_ge(S["s2_turn_ps"], n - 2)
                        step(dve.tensor_reduce(peak[:, n:n + 1], score2[n % 3][:, 0:MEM], AX_X, ALU.max, negate=True))
                        dve.tensor_scalar(peak[:, n:n + 1], peak[:, n:n + 1], P ** -0.5, None,
                                          ALU.mult).then_inc(S["s2_max"], 1)
                    if s:
                        x_scaled(s - 1)
                        dve.sem_inc(S["s2_bias"], 1)
                    k = s - YS_SPLIT - 3
                    if 0 <= k < 4:
                        dve.wait_ge(S["split2"], k + 1)
                        dve.tensor_tensor(ys_lo[:, k, :], u_sb[:, k, :], ys_hi[:, k, :].bitcast(F32),
                                          ALU.subtract).then_inc(S["rest2"], 1)

                k = 4
                for src, hi, lo, tiles in ((yx, yx_hi, yx_lo, 4), (ya, ya_hi, ya_lo, 2)):
                    for t in range(tiles):
                        k += 1
                        dve.wait_ge(S["split2"], k)
                        dve.tensor_tensor(lo[:, t, :], src[:, t, :], hi[:, t, :].bitcast(F32),
                                          ALU.subtract).then_inc(S["rest2"], 1)
                for b in plan2[AT2["gates"]:AT2["w_out2"]]:
                    p, j = divmod(b.n - AT2["gates"], 7)
                    dve.wait_ge(S["g_free"], b.t0 + 2)
                    for m in range(2):
                        total = gate_tile(1, m)
                        if j in (1, 2):
                            step(dve.tensor_tensor(total, total, gate_tile(0 if j == 1 else 2, m), ALU.mult))
                        elif j in (4, 6):
                            step(dve.tensor_tensor(gate_tile(j, m), gate_tile(j, m), gate_tile(j - 1, m), ALU.mult))
                            ins = dve.tensor_tensor(total, total, gate_tile(j, m), ALU.add)
                            if j == 6:
                                ins.then_inc(S["merged"], 1)
                            else:
                                step(ins)
                    if j == 6:
                        for m in range(2):
                            k = 2 * p + m
                            dve.wait_ge(S["mg_hi_s"], k + 1)
                            dve.tensor_tensor(mg_lo[:, k, :], gate_tile(1, m), mg_hi[:, k, :].bitcast(F32),
                                              ALU.subtract).then_inc(S["mg_s"], 1)
                    rest_block(dve, plan2, b.n + 2)
                dve.wait_ge(S["x_back"], 16)
                for b in plan2[AT2["w_out2"]:AT2["ffn2_up"]]:
                    rest_block(dve, plan2, b.n + 2)
                    for m in range(2):
                        dve.wait_ge(S["g_free"], b.t0 + m + 1)
                        add_part(2 * (b.n - AT2["w_out2"]) + m)
                pre_norm_dve(dve, 3, 3, gains2["ffn2"])
                ffn("ffn2", F2T)
                norm_inverse(dve, 4)
                for k in range(KD):
                    dve.scalar_tensor_tensor(out=out_sb[:, k, :], in0=x_sb[:, k, :], scalar=gains2["final"][:, k:k + 1],
                                             in1=t_ps[:], op0=ALU.mult, op1=ALU.mult).then_inc(S["final_s"], 1)


def packed(plan, *mats):
    mats = dict(mats)
    out = np.zeros((len(plan), P, WSIZE), np.float32)
    for b in plan:
        a = mats[b.src][b.rows:b.rows + b.kt * P, b.cols:b.cols + b.w]
        out[b.n, :, 0:b.kt * b.w] = a.reshape(b.kt, P, b.w).transpose(1, 0, 2).reshape(P, b.kt * b.w)
    return out


def columns(v):
    return v.reshape(-1, P).T


def t5_bucket(dist):
    exact = BUCKETS // 2
    safe = np.maximum(np.asarray(dist, np.int32), 1).astype(np.float32)
    large = exact + (np.log(safe / exact) / np.log(MAX_DIST / exact) * (BUCKETS - exact)).astype(np.int32)
    return np.where(dist < exact, dist, np.minimum(large, BUCKETS - 1))


def states(v):
    v = v.reshape(STILES, P, *v.shape[2:])
    return np.moveaxis(v, 0, 1)


def constants():
    half = HD // 2
    inv = (1.0 / (10000.0 ** np.linspace(0.0, 1.0, half, dtype=np.float32))).astype(np.float32)
    ang = (inv[:, None] * np.arange(SEQ, dtype=np.float32)[None, :]).astype(np.float32)
    cos = np.tile(np.cos(ang), (4, 1)).astype(np.float32)
    sin = np.tile(np.sin(ang), (4, 1)).astype(np.float32)
    p = np.arange(P)
    swap = np.zeros((P, P), np.float32)
    for m in range(P):
        if m % HD < half:
            swap[m + half, m] = -1.0
        else:
            swap[m - half, m] = 1.0
    log_g = np.log1p(-(2.0 ** (-5.0 - np.arange(RET_HEADS))))
    d = np.arange(SEQ)[None, :] - p[:, None]
    decay = np.where(d >= 0, np.exp(np.maximum(d, 0)[None] * log_g[:, None, None]), 0.0)
    one_hot = np.zeros((BUCKETS + 1, PATTERNS, ROW), np.float32)
    for g in range(PATTERNS):
        zero = 255 if g == 0 else 127
        every = (1, 1, 4)[g]
        for n in range(ROW):
            steps = zero - n
            b = BUCKETS
            if 0 <= steps <= P and steps % every == 0:
                b = int(t5_bucket(steps * (1, 4, 4)[g]))
            one_hot[b, g, n] = 1.0
    return {
        "c_one_hot": one_hot,
        "c_time": np.tile(np.arange(SEQ, dtype=np.float32), (P, 1)),
        "c_ident": np.eye(P, dtype=np.float32),
        "c_ones": np.ones((P, P), np.float32),
        "c_head_ones": (p[:, None] // HD == p[None, :] // HD).astype(np.float32),
        "c_swap": swap,
        "c_cos": cos,
        "c_sin": sin,
        "c_decay": np.ascontiguousarray(decay.transpose(1, 0, 2)).astype(np.float32),
    }


def laid_out(a):
    plan = layer_pieces()
    out = constants()
    out["x"] = np.ascontiguousarray(a["x"][0].T)
    layers = [packed(plan, ("w_in", a["w_in"][l]), ("w_out", a["w_out"][l]), ("w_up", a["w_up"][l]),
                     ("w_down", a["w_down"][l])) for l in range(DEPTH)]
    par = []
    for l in range(DEPTH):
        cw = a["conv_w"][l].T.reshape(2, P, TAPS).transpose(1, 0, 2).reshape(P, 2 * TAPS)
        par.append(np.concatenate(
            [columns(a[n][l]) for n in ("norm_mix_pre", "norm_mix_post", "norm_mlp_pre", "norm_mlp_post")]
            + [cw] + [columns(a[n][l]) for n in ("conv_b", "conv_ln_g", "conv_ln_b")], axis=1))
    out["par1"] = np.stack(par)
    at = np.clip(SEQ - 1 - np.arange(SEQ + P - 1), -REL_CLIP, REL_CLIP) + REL_CLIP
    out["att_bias_rows"] = a["attn_rel_bias"][:, :, at]
    out["rel_table"] = a["rel_table_2"]
    plan2, _ = third_pieces()
    third = packed(plan2, ("ffn1_in", a["ffn1_w_in_2"][0]), ("ffn1_down", a["ffn1_w_down_2"][0]),
                       ("w_kv", a["xattn_w_kv_2"][0]), ("w_in2", a["w_in_2"][0]), ("w_glu", a["ssm_w_glu_2"][0]),
                       ("w_attn_up", a["attn_w_up_2"][0]), ("w_xattn_up", a["xattn_w_up_2"][0]),
                       ("w_out2", a["w_out_2"][0]), ("ffn2_in", a["ffn2_w_in_2"][0]),
                       ("ffn2_down", a["ffn2_w_down_2"][0]))
    out["w"] = np.concatenate(layers + [third])
    out["first_gains"] = np.stack([columns(v) for v in (*a["norm_mix_pre"], a["ffn1_norm_2"][0])])
    log_dt = np.broadcast_to(a["ssm_log_dt_2"][0][:, None], (SSM_W // SSM_G, SSM_N))
    out["par2"] = np.concatenate(
        [columns(v) for v in (a["ffn1_norm_2"][0], a["mem_norm_2"][0], a["mix_norm_2"][0], a["ffn2_norm_2"][0],
                              a["final_norm_2"])]
        + [states(a["ssm_a_re_2"][0]), states(a["ssm_a_im_2"][0]), states(log_dt),
           columns(a["ssm_d_2"][0].reshape(-1))], axis=1)
    out["ssm_bc"] = np.stack([states(a["ssm_b_re_2"][0]), states(a["ssm_b_im_2"][0]),
                              states(a["ssm_c_re_2"][0].transpose(0, 2, 1)),
                              states(a["ssm_c_im_2"][0].transpose(0, 2, 1))], axis=1)
    out["mem"] = a["mem_2"][0].T
    return out


def kernel(**inputs):
    import concourse.bacc as _bacc
    from concourse.bass_utils import run_bass_kernel_spmd as _run

    arrays = {n: np.ascontiguousarray(v) for n, v in laid_out({n: np.asarray(v) for n, v in inputs.items()}).items()}
    nc = _bacc.Bacc("TRN2", target_bir_lowering=False, num_devices=1)
    ins = {n: nc.dram_tensor(f"in_{n}", v.shape, F32, kind="ExternalInput").ap() for n, v in arrays.items()}
    out = nc.dram_tensor("out_t", [DM, SEQ], F32, kind="ExternalOutput").ap()
    build(nc, ins, [out])
    r = _run(nc, [{f"in_{n}": v for n, v in arrays.items()}], core_ids=[0])
    return np.ascontiguousarray(r.results[0]["out_t"].T)[None]
```
